# Optimizing a Trainium2 kernel written in Bass

```python
import math, functools
import jax, jax.numpy as jnp
from jax import lax
import numpy as np
import math

D_MODEL = 1024
BATCH = 1
SEQ = 256
DEPTH = 2

MEM_TOKENS = 256
HEAD_DIM = 64
ROPE_THETA = 500000.0
PARTIAL_ROT = HEAD_DIM // 4
Q_BLOCK = 128
RMS_EPS = 1e-6
LN_EPS = 1e-5
DSA_HEADS = 8
DSA_TOPK = 256
IDX_HEADS = 4
IDX_DIM = 64
MLA_HEADS = 8
MLA_Q_RANK = 384
MLA_KV_RANK = 256
MLA_NOPE = 64
MLA_ROPE = 32
MLA_V = 64
DIFF_HEADS = 4
DIFF_DIM = 64
SGU_CHUNK = 128
SGU_GROUPS = 8
SGU_WIDTH = 512
MEM_HEADS = 4
MEM_DIM = 128
N_BRANCH = 5
BRANCH_WIDTH = 512

SPLIT_SIZES = (
    DSA_HEADS * HEAD_DIM, HEAD_DIM, HEAD_DIM,
    IDX_HEADS * IDX_DIM, IDX_DIM, IDX_HEADS,
    MLA_Q_RANK, MLA_KV_RANK, MLA_ROPE,
    2 * DIFF_HEADS * DIFF_DIM, 2 * DIFF_HEADS * DIFF_DIM, DIFF_HEADS * 2 * DIFF_DIM,
    SGU_WIDTH, SGU_WIDTH,
    MEM_HEADS * MEM_DIM,
    N_BRANCH * BRANCH_WIDTH,
    N_BRANCH * D_MODEL,
)
IN_WIDTH = sum(SPLIT_SIZES)


def rms_norm(x, g, eps=RMS_EPS):
    xf = x.astype(jnp.float32)
    y = xf * lax.rsqrt(jnp.mean(xf * xf, axis=-1, keepdims=True) + eps)
    return (y * g.astype(jnp.float32)).astype(x.dtype)

def layer_norm(x, g, b, eps=LN_EPS):
    xf = x.astype(jnp.float32)
    mu = jnp.mean(xf, axis=-1, keepdims=True)
    xc = xf - mu
    y = xc * lax.rsqrt(jnp.mean(xc * xc, axis=-1, keepdims=True) + eps)
    return (y * g.astype(jnp.float32) + b.astype(jnp.float32)).astype(x.dtype)

def rope_tables(positions, rot_dim):
    inv_freq = ROPE_THETA ** (-jnp.arange(0, rot_dim, 2, dtype=jnp.float32) / rot_dim)
    ang = positions.astype(jnp.float32)[..., None] * inv_freq
    return jnp.cos(ang), jnp.sin(ang)

def apply_rope(x, cos, sin):
    half = cos.shape[-1]
    c = cos[:, :, None, :].astype(x.dtype)
    s = sin[:, :, None, :].astype(x.dtype)
    x1 = x[..., :half]
    x2 = x[..., half:2 * half]
    return jnp.concatenate([x1 * c - x2 * s, x2 * c + x1 * s, x[..., 2 * half:]], axis=-1)

def _to_blocks(t, nb):
    return t.reshape((t.shape[0], nb, Q_BLOCK) + t.shape[2:]).swapaxes(0, 1)

def _from_blocks(t):
    nb, b, q = t.shape[:3]
    return t.swapaxes(0, 1).reshape((b, nb * q) + t.shape[3:])

def causal_attention(q, k, v, scale, mix=None):
    S = q.shape[1]
    nb = S // Q_BLOCK
    key_pos = jnp.arange(S)

    def body(args):
        qb, i = args
        q_pos = i * Q_BLOCK + jnp.arange(Q_BLOCK)
        s = jnp.einsum('bqhd,bkhd->bhqk', qb, k).astype(jnp.float32) * scale
        s = jnp.where(key_pos[None, :] <= q_pos[:, None], s, -jnp.inf)
        p = jax.nn.softmax(s, axis=-1)
        if mix is not None:
            p = mix(p)
        return jnp.einsum('bhqk,bkhd->bqhd', p.astype(v.dtype), v)

    return _from_blocks(lax.map(body, (_to_blocks(q, nb), jnp.arange(nb))))

def dsa_attention(q, k, v, qi, ki, wi):
    B, S, H, dh = q.shape
    k_sel = min(DSA_TOPK, S // 4)
    nb = S // Q_BLOCK
    key_pos = jnp.arange(S)
    gather = jax.vmap(lambda t, j: t[j])

    def body(args):
        qb, qib, wib, i = args
        q_pos = i * Q_BLOCK + jnp.arange(Q_BLOCK)
        dots = jnp.einsum('bqhd,bkd->bqhk', qib, ki).astype(jnp.float32)
        score = jnp.einsum('bqh,bqhk->bqk', wib.astype(jnp.float32), jax.nn.relu(dots))
        score = jnp.where(key_pos[None, None, :] <= q_pos[None, :, None], score, -jnp.inf)
        _, idx = lax.top_k(score, k_sel)
        valid = idx <= q_pos[None, :, None]
        k_g = gather(k, idx)
        v_g = gather(v, idx)
        s = jnp.einsum('bqhd,bqkd->bqhk', qb, k_g).astype(jnp.float32) * dh ** -0.5
        s = jnp.where(valid[:, :, None, :], s, -jnp.inf)
        p = jax.nn.softmax(s, axis=-1)
        return jnp.einsum('bqhk,bqkd->bqhd', p.astype(v.dtype), v_g)

    out = lax.map(body, (_to_blocks(q, nb), _to_blocks(qi, nb), _to_blocks(wi, nb), jnp.arange(nb)))
    return _from_blocks(out)

def dsa_branch(a_q, a_k, a_v, i_q, i_k, i_w, cos, sin):
    B, S, _ = a_q.shape
    q = apply_rope(a_q.reshape(B, S, DSA_HEADS, HEAD_DIM), cos, sin)
    k = apply_rope(a_k[:, :, None, :], cos, sin)[:, :, 0]
    qi = apply_rope(i_q.reshape(B, S, IDX_HEADS, IDX_DIM), cos, sin)
    ki = apply_rope(i_k[:, :, None, :], cos, sin)[:, :, 0]
    wi = i_w * (IDX_HEADS * IDX_DIM) ** -0.5
    return dsa_attention(q, k, a_v, qi, ki, wi).reshape(B, S, DSA_HEADS * HEAD_DIM)

def mla_branch(cq, ckv, kr, q_norm_g, kv_norm_g, w_uq, w_ukv, cos, sin):
    B, S, _ = cq.shape
    q = (rms_norm(cq, q_norm_g) @ w_uq).reshape(B, S, MLA_HEADS, MLA_NOPE + MLA_ROPE)
    q = jnp.concatenate([q[..., :MLA_NOPE], apply_rope(q[..., MLA_NOPE:], cos, sin)], axis=-1)
    kv = (rms_norm(ckv, kv_norm_g) @ w_ukv).reshape(B, S, MLA_HEADS, MLA_NOPE + MLA_V)
    k_rope = apply_rope(kr[:, :, None, :], cos, sin)
    k = jnp.concatenate([kv[..., :MLA_NOPE], jnp.broadcast_to(k_rope, (B, S, MLA_HEADS, MLA_ROPE))], axis=-1)
    o = causal_attention(q, k, kv[..., MLA_NOPE:], (MLA_NOPE + MLA_ROPE) ** -0.5)
    return o.reshape(B, S, MLA_HEADS * MLA_V)

def diff_branch(cq, ck, cv, lam_params, sub_norm_g, layer, cos, sin):
    B, S, _ = cq.shape
    lam_init = 0.8 - 0.6 * math.exp(-0.3 * layer)
    lp = lam_params.astype(jnp.float32)
    lam = jnp.exp(jnp.sum(lp[0] * lp[1])) - jnp.exp(jnp.sum(lp[2] * lp[3])) + lam_init
    q = apply_rope(cq.reshape(B, S, 2 * DIFF_HEADS, DIFF_DIM), cos, sin)
    k = apply_rope(ck.reshape(B, S, 2 * DIFF_HEADS, DIFF_DIM), cos, sin)
    v = cv.reshape(B, S, DIFF_HEADS, 2 * DIFF_DIM)

    def diff_mix(p):
        b, h2, nq, nk = p.shape
        pr = p.reshape(b, h2 // 2, 2, nq, nk)
        return pr[:, :, 0] - lam * pr[:, :, 1]

    o = causal_attention(q, k, v, DIFF_DIM ** -0.5, diff_mix)
    o = rms_norm(o, sub_norm_g) * (1.0 - lam_init)
    return o.reshape(B, S, DIFF_HEADS * 2 * DIFF_DIM)

def sgu_branch(u, v, ln_g, ln_b, w_s, b_s):
    B, S, _ = u.shape
    nc = S // SGU_CHUNK
    vc = layer_norm(v, ln_g, ln_b).reshape(B, nc, SGU_CHUNK, SGU_GROUPS, SGU_WIDTH // SGU_GROUPS)
    w_causal = w_s * jnp.tril(jnp.ones((SGU_CHUNK, SGU_CHUNK), w_s.dtype))
    z = jnp.einsum('gij,bcjgd->bcigd', w_causal, vc) + b_s.T[None, None, :, :, None]
    return u * z.reshape(B, S, SGU_WIDTH)

def memory_branch(eq, mem_n, w_kv):
    B, S, _ = eq.shape
    M = mem_n.shape[1]
    kv = (mem_n @ w_kv).reshape(B, M, 2, MEM_HEADS, MEM_DIM)
    q = eq.reshape(B, S, MEM_HEADS, MEM_DIM)
    s = jnp.einsum('bshd,bmhd->bhsm', q, kv[:, :, 0]).astype(jnp.float32) * MEM_DIM ** -0.5
    p = jax.nn.softmax(s, axis=-1)
    o = jnp.einsum('bhsm,bmhd->bshd', p.astype(kv.dtype), kv[:, :, 1])
    return o.reshape(B, S, MEM_HEADS * MEM_DIM)

def first_inputs(seed: int = 0) -> dict:
    key = jax.random.key(seed)
    ks = jax.random.split(key, 24)
    f32 = jnp.float32

    def nrm(k, shape, scale):
        return jax.random.normal(k, shape, f32) * scale

    def gain(k, shape):
        return 1.0 + 0.02 * jax.random.normal(k, shape, f32)

    offs = jax.random.randint(ks[2], (BATCH, 1), 0, 4096)
    positions = (offs + jnp.arange(SEQ)[None, :]).astype(jnp.int32)
    return {
        'x': nrm(ks[0], (BATCH, SEQ, D_MODEL), 1.0),
        'mem': nrm(ks[1], (BATCH, MEM_TOKENS, D_MODEL), 1.0),
        'positions': positions,
        'norm_g': gain(ks[3], (DEPTH, D_MODEL)),
        'w_in': nrm(ks[4], (DEPTH, D_MODEL, IN_WIDTH), D_MODEL ** -0.5),
        'mla_q_norm_g': gain(ks[5], (DEPTH, MLA_Q_RANK)),
        'mla_kv_norm_g': gain(ks[6], (DEPTH, MLA_KV_RANK)),
        'mla_w_uq': nrm(ks[7], (DEPTH, MLA_Q_RANK, MLA_HEADS * (MLA_NOPE + MLA_ROPE)), MLA_Q_RANK ** -0.5),
        'mla_w_ukv': nrm(ks[8], (DEPTH, MLA_KV_RANK, MLA_HEADS * (MLA_NOPE + MLA_V)), MLA_KV_RANK ** -0.5),
        'diff_lambda': nrm(ks[9], (DEPTH, 4, DIFF_DIM), 0.1),
        'diff_norm_g': gain(ks[10], (DEPTH, 2 * DIFF_DIM)),
        'sgu_ln_g': gain(ks[11], (DEPTH, SGU_WIDTH)),
        'sgu_ln_b': nrm(ks[12], (DEPTH, SGU_WIDTH), 0.02),
        'sgu_w': nrm(ks[13], (DEPTH, SGU_GROUPS, SGU_CHUNK, SGU_CHUNK), SGU_CHUNK ** -0.5),
        'sgu_b': gain(ks[14], (DEPTH, SGU_GROUPS, SGU_CHUNK)),
        'mem_norm_g': gain(ks[15], (D_MODEL,)),
        'mem_w_kv': nrm(ks[16], (DEPTH, D_MODEL, 2 * MEM_HEADS * MEM_DIM), D_MODEL ** -0.5),
        'w_branch': nrm(ks[17], (DEPTH, N_BRANCH, BRANCH_WIDTH, D_MODEL), BRANCH_WIDTH ** -0.5),
        'w_out': nrm(ks[18], (DEPTH, D_MODEL, D_MODEL), D_MODEL ** -0.5),
        'final_norm_g': gain(ks[19], (D_MODEL,)),
    }

def first_block(x, mem, positions, norm_g, w_in, mla_q_norm_g, mla_kv_norm_g, mla_w_uq, mla_w_ukv,
              diff_lambda, diff_norm_g, sgu_ln_g, sgu_ln_b, sgu_w, sgu_b, mem_norm_g, mem_w_kv,
              w_branch, w_out, final_norm_g):
    B, S, _ = x.shape
    offsets = np.cumsum(SPLIT_SIZES)[:-1].tolist()
    cos_p, sin_p = rope_tables(positions, PARTIAL_ROT)
    cos_m, sin_m = rope_tables(positions, MLA_ROPE)
    mem_n = rms_norm(mem, mem_norm_g)
    h = x
    for l in range(DEPTH):
        xn = rms_norm(h, norm_g[l])
        (a_q, a_k, a_v, i_q, i_k, i_w, b_cq, b_ckv, b_kr, c_q, c_k, c_v,
         d_u, d_v, e_q, gates, merge) = jnp.split(xn @ w_in[l], offsets, axis=-1)
        branches = (
            dsa_branch(a_q, a_k, a_v, i_q, i_k, i_w, cos_p, sin_p),
            mla_branch(b_cq, b_ckv, b_kr, mla_q_norm_g[l], mla_kv_norm_g[l], mla_w_uq[l], mla_w_ukv[l], cos_m, sin_m),
            diff_branch(c_q, c_k, c_v, diff_lambda[l], diff_norm_g[l], l, cos_p, sin_p),
            sgu_branch(d_u, d_v, sgu_ln_g[l], sgu_ln_b[l], sgu_w[l], sgu_b[l]),
            memory_branch(e_q, mem_n, mem_w_kv[l]),
        )
        gates = gates.reshape(B, S, N_BRANCH, BRANCH_WIDTH)
        merge = merge.reshape(B, S, N_BRANCH, D_MODEL)
        mixed = functools.reduce(jnp.add, [
            jax.nn.sigmoid(merge[:, :, n]) * ((o * jax.nn.silu(gates[:, :, n])) @ w_branch[l, n])
            for n, o in enumerate(branches)])
        h = h + mixed @ w_out[l]
    return rms_norm(h, final_norm_g)


DEPTH_2 = 1

D_MIX = D_MODEL
GLA_HEADS = 4
GLA_DV = (D_MIX // 2) // GLA_HEADS
GLA_DK = GLA_DV // 2
GLA_GATE_RANK = 16
GLA_TAU = 16.0
GLA_CHUNK = 64
MOBA_HEADS = 8
MOBA_HD = (D_MIX - GLA_HEADS * GLA_DV) // MOBA_HEADS
MOBA_BLOCK = 256
MOBA_TOPK = 3
MOBA_QCHUNK = 8
REL_BUCKETS = 32
REL_MAX_DIST = 128
D_FF = 4 * D_MODEL
N_ADA = 6
EPS = 1e-6

GLA_QK_W = GLA_HEADS * GLA_DK
GLA_V_W = GLA_HEADS * GLA_DV
MOBA_W = MOBA_HEADS * MOBA_HD
IN_WIDTHS = (GLA_QK_W, GLA_QK_W, GLA_V_W, GLA_V_W, GLA_GATE_RANK, MOBA_W, MOBA_W, MOBA_W)
D_IN = sum(IN_WIDTHS)
IN_SPLITS = [int(v) for v in np.cumsum(IN_WIDTHS)[:-1]]


def rmsnorm(x, g):
    xf = x.astype(jnp.float32)
    y = xf * lax.rsqrt(jnp.mean(xf * xf, axis=-1, keepdims=True) + EPS)
    return y.astype(x.dtype) * g

def modulate(h, shift, scale):
    return h * (1.0 + scale[:, None, :]) + shift[:, None, :]

def gla_mixer(q, k, v, log_a):
    B, S, H, dk = q.shape
    dv = v.shape[-1]
    C = GLA_CHUNK
    N = S // C
    f32 = jnp.float32

    def chunks(t):
        return t.astype(f32).reshape(B, N, C, H, t.shape[-1]).transpose(0, 3, 1, 2, 4)

    q = chunks(q) * (dk ** -0.5)
    k = chunks(k)
    v = chunks(v)
    g = chunks(log_a)
    b = jnp.cumsum(g, axis=3)
    b_last = b[:, :, :, -1:, :]
    b_ref = b[:, :, :, C // 2 - 1:C // 2, :]
    att = jnp.einsum('bhnid,bhnjd->bhnij', q * jnp.exp(b - b_ref), k * jnp.exp(b_ref - b))
    causal = jnp.tril(jnp.ones((C, C), dtype=bool))
    att = jnp.where(causal, att, 0.0)
    o_intra = jnp.einsum('bhnij,bhnjv->bhniv', att, v)
    kv = jnp.einsum('bhncd,bhncv->bhndv', k * jnp.exp(b_last - b), v)
    decay = jnp.exp(b_last[:, :, :, 0, :])

    def step(s_prev, inp):
        kv_n, dec_n = inp
        return dec_n[..., None] * s_prev + kv_n, s_prev

    s0 = jnp.zeros((B, H, dk, dv), f32)
    _, s_before = lax.scan(step, s0, (kv.transpose(2, 0, 1, 3, 4), decay.transpose(2, 0, 1, 3)))
    s_before = s_before.transpose(1, 2, 0, 3, 4)
    o_inter = jnp.einsum('bhncd,bhndv->bhncv', q * jnp.exp(b), s_before)
    o = o_intra + o_inter
    return o.transpose(0, 2, 3, 1, 4).reshape(B, S, H, dv)

def t5_bucket(rel):
    n = jnp.maximum(rel, 0)
    max_exact = REL_BUCKETS // 2
    ratio = jnp.maximum(n, 1).astype(jnp.float32) / max_exact
    large = max_exact + (jnp.log(ratio) / math.log(REL_MAX_DIST / max_exact)
                         * (REL_BUCKETS - max_exact)).astype(jnp.int32)
    large = jnp.minimum(large, REL_BUCKETS - 1)
    return jnp.where(n < max_exact, n, large)

def moba_mixer(q, k, v, rel_bias):
    B, S, H, hd = q.shape
    BLK = MOBA_BLOCK
    QC = MOBA_QCHUNK
    NB = -(-S // BLK)
    Sp = NB * BLK
    topk = min(MOBA_TOPK, NB)
    f32 = jnp.float32
    qh = q.transpose(0, 2, 1, 3) * (hd ** -0.5)
    pad = ((0, 0), (0, 0), (0, Sp - S), (0, 0))
    kb = jnp.pad(k.transpose(0, 2, 1, 3), pad).reshape(B, H, NB, BLK, hd)
    vb = jnp.pad(v.transpose(0, 2, 1, 3), pad).reshape(B, H, NB, BLK, hd)
    k_mean = jnp.mean(kb.astype(f32), axis=3)
    bias_flat = rel_bias.T.reshape(-1)
    head_off = (jnp.arange(H, dtype=jnp.int32) * REL_BUCKETS)[None, :, None, None]
    blk_pos = jnp.arange(BLK, dtype=jnp.int32)
    blk_ids = jnp.arange(NB, dtype=jnp.int32)
    nq = S // QC
    q_chunks = qh.reshape(B, H, nq, QC, hd).transpose(2, 0, 1, 3, 4)
    gather_blocks = jax.vmap(jax.vmap(lambda kk, ii: kk[ii]))

    def one_chunk(args):
        ci, q_c = args
        t = ci * QC + jnp.arange(QC, dtype=jnp.int32)
        own = (ci * QC) // BLK
        gate = jnp.einsum('bhqd,bhnd->bhqn', q_c.astype(f32), k_mean)
        gate = jnp.where(blk_ids < own, gate, -jnp.inf)
        gval, gidx = lax.top_k(gate, topk)
        valid = jnp.isfinite(gval)
        k_sel = gather_blocks(kb, gidx)
        v_sel = gather_blocks(vb, gidx)
        s_sel = jnp.einsum('bhqd,bhqkld->bhqkl', q_c, k_sel).astype(f32)
        pos_sel = gidx[..., None] * BLK + blk_pos
        rel_sel = t[None, None, :, None, None] - pos_sel
        s_sel = s_sel + bias_flat[head_off[..., None] + t5_bucket(rel_sel)]
        s_sel = jnp.where(valid[..., None], s_sel, -jnp.inf)
        k_own = lax.dynamic_slice_in_dim(kb, own, 1, axis=2)[:, :, 0]
        v_own = lax.dynamic_slice_in_dim(vb, own, 1, axis=2)[:, :, 0]
        s_own = jnp.einsum('bhqd,bhld->bhql', q_c, k_own).astype(f32)
        rel_own = t[:, None] - (own * BLK + blk_pos)[None, :]
        s_own = s_own + bias_flat[head_off + t5_bucket(rel_own)[None, None]]
        s_own = jnp.where(rel_own[None, None] >= 0, s_own, -jnp.inf)
        logits = jnp.concatenate([s_sel.reshape(B, H, QC, topk * BLK), s_own], axis=-1)
        p = jax.nn.softmax(logits, axis=-1)
        p_sel = p[..., :topk * BLK].reshape(B, H, QC, topk, BLK).astype(v.dtype)
        p_own = p[..., topk * BLK:].astype(v.dtype)
        return (jnp.einsum('bhqkl,bhqkld->bhqd', p_sel, v_sel)
                + jnp.einsum('bhql,bhld->bhqd', p_own, v_own))

    out = lax.map(one_chunk, (jnp.arange(nq, dtype=jnp.int32), q_chunks))
    return out.transpose(1, 0, 3, 2, 4).reshape(B, S, H, hd)

def second_inputs(seed: int = 0) -> dict:
    key = jax.random.key(seed)
    ks = jax.random.split(key, 16)
    f32 = jnp.float32
    nrm = lambda k, shape, s: (jax.random.normal(k, shape, f32) * s)
    gain = lambda k, shape: 1.0 + 0.05 * jax.random.normal(k, shape, f32)
    return {
        "x": nrm(ks[0], (BATCH, SEQ, D_MODEL), 1.0),
        "c": nrm(ks[1], (BATCH, D_MODEL), 1.0),
        "w_ada": nrm(ks[2], (DEPTH_2, D_MODEL, N_ADA * D_MODEL), D_MODEL ** -0.5),
        "b_ada": nrm(ks[3], (DEPTH_2, N_ADA * D_MODEL), 0.02),
        "g_mix": gain(ks[4], (DEPTH_2, D_MODEL)),
        "w_in": nrm(ks[5], (DEPTH_2, D_MODEL, D_IN), D_MODEL ** -0.5),
        "w_gla_gate": nrm(ks[6], (DEPTH_2, GLA_GATE_RANK, GLA_QK_W), GLA_GATE_RANK ** -0.5),
        "b_gla_gate": nrm(ks[7], (DEPTH_2, GLA_QK_W), 0.1),
        "g_gla_out": gain(ks[8], (DEPTH_2, GLA_V_W)),
        "rel_bias": nrm(ks[9], (REL_BUCKETS, MOBA_HEADS), 0.5),
        "w_out": nrm(ks[10], (DEPTH_2, D_MIX, D_MODEL), D_MIX ** -0.5),
        "g_mlp": gain(ks[11], (DEPTH_2, D_MODEL)),
        "w_ff1": nrm(ks[12], (DEPTH_2, D_MODEL, D_FF), D_MODEL ** -0.5),
        "w_ff2": nrm(ks[13], (DEPTH_2, D_FF, D_MODEL), D_FF ** -0.5),
        "g_final": gain(ks[14], (D_MODEL,)),
    }

def second_block(x, c, w_ada, b_ada, g_mix, w_in, w_gla_gate, b_gla_gate, g_gla_out, rel_bias,
              w_out, g_mlp, w_ff1, w_ff2, g_final):
    B, S, _ = x.shape
    c_act = jax.nn.silu(c)
    for l in range(DEPTH_2):
        ada = c_act @ w_ada[l] + b_ada[l]
        shift_a, scale_a, gate_a, shift_m, scale_m, gate_m = jnp.split(ada, N_ADA, axis=-1)
        h = modulate(rmsnorm(x, g_mix[l]), shift_a, scale_a)
        proj = h @ w_in[l]
        gq, gk, gv, gr, gg, mq, mk, mv = jnp.split(proj, IN_SPLITS, axis=-1)
        log_a = jax.nn.log_sigmoid((gg @ w_gla_gate[l] + b_gla_gate[l]).astype(jnp.float32)) / GLA_TAU
        o_gla = gla_mixer(gq.reshape(B, S, GLA_HEADS, GLA_DK), gk.reshape(B, S, GLA_HEADS, GLA_DK),
                          gv.reshape(B, S, GLA_HEADS, GLA_DV), log_a.reshape(B, S, GLA_HEADS, GLA_DK))
        o_gla = rmsnorm(o_gla.astype(x.dtype), g_gla_out[l].reshape(GLA_HEADS, GLA_DV))
        o_gla = o_gla.reshape(B, S, GLA_V_W) * jax.nn.silu(gr)
        o_moba = moba_mixer(mq.reshape(B, S, MOBA_HEADS, MOBA_HD), mk.reshape(B, S, MOBA_HEADS, MOBA_HD),
                            mv.reshape(B, S, MOBA_HEADS, MOBA_HD), rel_bias).reshape(B, S, MOBA_W)
        y = jnp.concatenate([o_gla, o_moba], axis=-1) @ w_out[l]
        x = x + gate_a[:, None, :] * y
        h = modulate(rmsnorm(x, g_mlp[l]), shift_m, scale_m)
        x = x + gate_m[:, None, :] * (jnp.square(jax.nn.relu(h @ w_ff1[l])) @ w_ff2[l])
    return rmsnorm(x, g_final)


def setup_inputs(seed=0):
    out = dict(first_inputs(seed))
    for name, value in second_inputs(seed + 1).items():
        if name != "x":
            out[name + "_2"] = value
    return out


def reference(
    x, mem, positions, norm_g, w_in, mla_q_norm_g, mla_kv_norm_g, mla_w_uq, mla_w_ukv,
    diff_lambda, diff_norm_g, sgu_ln_g, sgu_ln_b, sgu_w, sgu_b, mem_norm_g, mem_w_kv, w_branch,
    w_out, final_norm_g, c_2, w_ada_2, b_ada_2, g_mix_2, w_in_2, w_gla_gate_2, b_gla_gate_2,
    g_gla_out_2, rel_bias_2, w_out_2, g_mlp_2, w_ff1_2, w_ff2_2, g_final_2,
):
    x = first_block(
        x, mem, positions, norm_g, w_in, mla_q_norm_g, mla_kv_norm_g, mla_w_uq, mla_w_ukv,
        diff_lambda, diff_norm_g, sgu_ln_g, sgu_ln_b, sgu_w, sgu_b, mem_norm_g, mem_w_kv,
        w_branch, w_out, final_norm_g,
    )
    return second_block(
        x, c_2, w_ada_2, b_ada_2, g_mix_2, w_in_2, w_gla_gate_2, b_gla_gate_2, g_gla_out_2,
        rel_bias_2, w_out_2, g_mlp_2, w_ff1_2, w_ff2_2, g_final_2,
    )


_drawn_inputs = setup_inputs


def setup_inputs(seed=0):
    import zlib

    import numpy as np

    out = dict(_drawn_inputs(seed))
    spreads = {}
    factors = {'mla_q_norm_g': 8.0,
     'mla_kv_norm_g': 3.812,
     'diff_norm_g': 6.499,
     'sgu_ln_g': 7.255,
     'sgu_ln_b': 7.552,
     'sgu_b': 5.286,
     'mem_norm_g': 8.0,
     'b_gla_gate_2': 3.174,
     'g_gla_out_2': 3.339}
    for name, (base, spread) in spreads.items():
        noise = np.random.default_rng([zlib.crc32(name.encode()), seed]).standard_normal(out[name].shape)
        drawn = base * np.exp(spread * noise) if base else spread * noise
        out[name] = __import__('jax').numpy.asarray(drawn.astype(out[name].dtype))
    for name, factor in factors.items():
        out[name] = (out[name] * factor).astype(out[name].dtype)
    return out
```

```python
from contextlib import ExitStack

import numpy as np

import concourse.bass as bass
from concourse import mybir

F32 = mybir.dt.float32
F32R = mybir.dt.float32r
BF16 = mybir.dt.bfloat16
I32 = mybir.dt.int32
ALU = mybir.AluOpType
ACT = mybir.ActivationFunctionType
AX_X = mybir.AxisListType.X

P = 128
TILES = 2
TOK = P * TILES
BANK = 512
RAW_SLOTS = 4
SPLIT_SLOTS = 4
LEAD = 3
SLAB = 1024
AUX = 4
PEXP = 2

NAMES = ("aq", "ak", "av", "iq", "ik", "iw", "cq", "ckv", "kr", "dq", "dk", "dv", "su", "sv", "eq", "gates", "merge")
WIDTHS = (512, 64, 64, 256, 64, 4, 384, 256, 32, 512, 512, 512, 512, 512, 512, 2560, 5120)
COL = dict(zip(NAMES, np.concatenate([[0], np.cumsum(WIDTHS)[:-1]]).tolist()))
PROJ = COL["gates"]
BRANCHES = {"a": 0, "b": 1, "c": 2, "d": 3, "e": 4}
DSA_HEADS, IDX_HEADS, IDX_DIM, MLA_HEADS, NOPE, ROT = 8, 4, 64, 8, 64, 32
TOPK = TOK // 4
MAGIC = float(0x5F3759DF)
MASKED = -1.0e30
PI_BELOW = 3.1415925
TWO_PI_PARTS = (6.28125, float(np.float16(2 * np.pi - 6.28125)),
                float(2 * np.pi - 6.28125 - float(np.float16(2 * np.pi - 6.28125))))
FREQ = [float(f) for n in (16, 32) for f in np.power(np.float32(500000.0), -np.arange(0, n, 2, dtype=np.float32) / np.float32(n))]
TAKEN = -3.0e38
ADA_PARTS = 12


class Record:
    pass


class Steps:

    def __init__(self, eng, sem):
        self.eng, self.sem, self.n = eng, sem, 0

    def did(self, ins):
        self.n += 1
        return ins.then_inc(self.sem, 1)

    def settle(self):
        if self.n:
            self.eng.wait_ge(self.sem, self.n)


def rsqrt(v, st, y, x, t, scale, eps):
    st.settle()
    st.did(v.tensor_scalar(x, x, scale, eps, ALU.mult, ALU.add))
    st.settle()
    st.did(v.tensor_scalar(y.bitcast(I32), x.bitcast(I32), -0.5, MAGIC, ALU.mult, ALU.add))
    for _ in range(3):
        st.settle()
        st.did(v.scalar_tensor_tensor(t, y, -0.5, y, ALU.mult, ALU.mult))
        st.settle()
        st.did(v.tensor_tensor(t, t, x, ALU.mult))
        st.settle()
        st.did(v.scalar_tensor_tensor(y, t, 1.5, y, ALU.add, ALU.mult))


def unit(name, lhs, kc, src, n, pair=None, opens=True, closes=True):
    x = Record()
    x.name, x.lhs, x.kc, x.src, x.n, x.pair, x.opens, x.closes = name, lhs, kc, src, n, pair, opens, closes
    return x


def step(name, kind, after=(), before=None, narrow=False, j=0, kc=0, src=None, dst=None, gain=None, gain_ready=None, shift=None,
         scale=1.0, w=P, rows=P, b="", t=0, g=0, r=0, i=0, n=0, heads=()):
    s = Record()
    s.name, s.kind, s.after, s.before, s.narrow, s.j, s.kc, s.src, s.dst = name, kind, after, before, narrow, j, kc, src, dst
    s.gain, s.gain_ready, s.shift, s.scale, s.w, s.rows, s.b, s.t, s.g = gain, gain_ready, shift, scale, w, rows, b, t, g
    s.r, s.i, s.n, s.heads = r, i, n, heads
    return s


HAS_BANK = {"split", "turn", "score", "probs", "value", "sgu_w", "sgu_z", "dots",
            "shifted", "turn_gg", "gla_z", "gla_sum", "gla_decay", "inner", "state", "gla_o",
            "ada_sum", "ada_rows"}


class Plan:

    def __init__(self, units, steps, rate=1):
        self.units, self.slabs, self.order = units, [], []
        begin, placed, at, load, closed = {}, {"start": 0}, {}, {}, {}
        pairs = 0
        for x in units:
            if x.pair is None:
                x.pair, pairs = pairs % 2, pairs + 1
            x.turn = closed.get(x.pair, 0)
            closed[x.pair] = x.turn + x.closes
            begin[x.name] = len(self.slabs)
            per = max(1, SLAB // x.n)
            for k0 in range(0, x.kc, per):
                kn = min(per, x.kc - k0)
                slab = Record()
                slab.i, slab.unit, slab.k0, slab.kn = len(self.slabs), x, k0, kn
                slab.first, slab.last = k0 == 0, k0 + kn == x.kc
                self.slabs.append(slab)
            placed[x.name] = len(self.slabs)
        for s in steps:
            lo = max([placed[a] + gap for a, gap in s.after], default=0)
            end = begin[s.before] if s.before else len(self.slabs)
            n = lo
            if s.kind in HAS_BANK and s.kind != "ada_sum" and s.before is None:
                while load.get(n, 0) >= rate and n < len(self.slabs):
                    n += 1
                load[n] = load.get(n, 0) + 1
            assert n <= end, (s.name, lo, end)
            placed[s.name] = n
            at.setdefault(n, []).append(s)
        for n in range(len(self.slabs) + 1):
            if n:
                self.order.append(("slab", self.slabs[n - 1]))
                if self.slabs[n - 1].last:
                    self.order.append(("evac", self.slabs[n - 1].unit))
            self.order += [(s.kind, s) for s in at.get(n, [])]
        self.bank, self.seq, count, uses = {}, {}, {}, [0] * AUX
        narrow = 0
        for kind, s in self.order:
            if kind in ("slab", "evac"):
                continue
            if kind in HAS_BANK:
                if s.narrow:
                    b, narrow = 2 + narrow % 2, narrow + 1
                else:
                    b = len(self.bank) % AUX
                use = Record()
                use.n, use.bank, use.turn = len(self.bank), b, uses[b]
                self.bank[s.name] = use
                uses[b] += 1
            self.seq[s.name] = count.get(kind, 0)
            count[kind] = count.get(kind, 0) + 1
        self.unit = {x.name: x for x in units}
        self.last_slab = {s.unit.name: s.i for s in self.slabs if s.last}


def load_slab(m, sp, plan, s):
    if s.i >= RAW_SLOTS:
        sp.wait_ge(m.lo_ready, s.i - RAW_SLOTS + 1)
    n = s.unit.n
    sp.dma_start(m.raw[:, s.i % RAW_SLOTS, 0:s.kn * n].rearrange("p (k n) -> p k n", n=n), s.unit.src(s.k0, s.kn))\
      .then_inc(m.arrived[s.i % RAW_SLOTS], 16)


def split_high(m, act, s):
    w = s.kn * s.unit.n
    act.wait_ge(m.arrived[s.i % RAW_SLOTS], 16 * (s.i // RAW_SLOTS + 1))
    if s.i >= SPLIT_SLOTS:
        act.wait_ge(m.slab_used, s.i - SPLIT_SLOTS + 1)
    act.activation(m.wh[:, s.i % SPLIT_SLOTS, 0:w], m.raw[:, s.i % RAW_SLOTS, 0:w], ACT.Copy).then_inc(m.hi_ready, 1)


def split_low(m, dve, s):
    w = s.kn * s.unit.n
    dve.wait_ge(m.hi_ready, s.i + 1)
    dve.tensor_tensor(m.wl[:, s.i % SPLIT_SLOTS, 0:w], m.raw[:, s.i % RAW_SLOTS, 0:w],
                      m.wh[:, s.i % SPLIT_SLOTS, 0:w].bitcast(F32), ALU.subtract).then_inc(m.lo_ready, 1)


def multiply(m, pe, plan, s, ready):
    x = s.unit
    if s.first:
        if x.opens and x.turn:
            pe.wait_ge(m.dense_done[x.pair], x.turn)
        for r in ready:
            pe.wait_ge(*r)
    pe.wait_ge(m.lo_ready, s.i + 1)
    hi, lo = m.lhs[x.lhs]
    for t in range(TILES):
        out = m.pairs[x.pair][:, t, 0:x.n]
        for k in range(s.kn):
            tok = slice(t * P, t * P + P)
            wh = m.wh[:, s.i % SPLIT_SLOTS, k * x.n:(k + 1) * x.n]
            wl = m.wl[:, s.i % SPLIT_SLOTS, k * x.n:(k + 1) * x.n]
            pe.matmul(out, hi[:, s.k0 + k, tok], wh, start=x.opens and s.first and k == 0, stop=False)
            pe.matmul(out, hi[:, s.k0 + k, tok], wl, start=False, stop=False)
            last = pe.matmul(out, lo[:, s.k0 + k, tok], wh, start=False, stop=x.closes and s.last and k == s.kn - 1)
    last.then_inc(m.slab_used, 1)


def take_bank(m, pe, k):
    if k.turn:
        pe.wait_ge(m.aux_done[k.bank], k.turn)


def aux_is_done(m, plan, name):
    k = plan.bank[name]
    return m.aux_done[k.bank], k.turn + 1


def unit_is_done(m, plan, name):
    x = plan.unit[name]
    return m.dense_done[x.pair], x.turn + 1


def turn_blocks(m, pe, k, blocks, ready):
    take_bank(m, pe, k)
    for r in ready:
        pe.wait_ge(*r)
    for i, src in enumerate(blocks):
        last = pe.transpose(m.aux[0:src.shape[-1], k.bank, i * P:(i + 1) * P], src, m.ident[:, :])
    last.then_inc(m.aux_ready, 1)


def split_cols(s, m):
    return 2 * s.j, min(2, s.kc - 2 * s.j)


def split_blocks(s, m):
    k0, kn = split_cols(s, m)
    return [s.src(t)[:, (k0 + i) * P:(k0 + i + 1) * P] for i in range(kn) for t in range(TILES)]


def split_hi(m, act, plan, s):
    k, (k0, kn) = plan.bank[s.name], split_cols(s, m)
    hi = m.lhs[s.dst][0]
    act.wait_ge(m.aux_ready, k.n + 1)
    if s.gain is None:
        last = act.activation(hi[:, k0:k0 + kn, :], m.aux[:, k.bank, 0:kn * TOK].rearrange("p (k n) -> p k n", n=TOK), ACT.Copy)
    else:
        if s.gain_ready:
            act.wait_ge(*s.gain_ready)
        for i in range(kn):
            last = act.activation(hi[:, k0 + i, :], m.aux[:, k.bank, i * TOK:(i + 1) * TOK], ACT.Copy,
                                  scale=s.gain[:, k0 + i:k0 + i + 1])
    last.then_inc(m.turned_hi, 1)


def split_lo(m, dve, plan, s):
    k, (k0, kn) = plan.bank[s.name], split_cols(s, m)
    hi, lo = m.lhs[s.dst]
    dve.wait_ge(m.turned_hi, plan.seq[s.name] + 1)
    if s.gain is None:
        last = dve.tensor_tensor(lo[:, k0:k0 + kn, :], m.aux[:, k.bank, 0:kn * TOK].rearrange("p (k n) -> p k n", n=TOK),
                                 hi[:, k0:k0 + kn, :].bitcast(F32), ALU.subtract)
    else:
        for i in range(kn):
            last = dve.scalar_tensor_tensor(lo[:, k0 + i, :], m.aux[:, k.bank, i * TOK:(i + 1) * TOK],
                                            s.gain[:, k0 + i:k0 + i + 1], hi[:, k0 + i, :].bitcast(F32),
                                            ALU.mult, ALU.subtract)
    last.then_inc(m.aux_done[k.bank], 1)


def mean_square(dve, st, stats, out, src, width):
    n = -(-width // BANK)
    w = width // n
    for t in range(TILES):
        for c in range(n):
            st.did(dve.bn_stats(stats[:, t, c, :], src(t)[:, c * w:(c + 1) * w]))
    st.settle()
    for t in range(TILES):
        st.did(dve.bn_aggr(stats[:, t, 2, 0:2], stats[:, t, 0:n, :]))
    st.settle()
    mean = stats[:, :, 2, 0]
    st.did(dve.tensor_tensor(out, mean, mean, ALU.mult))
    st.settle()
    st.did(dve.tensor_tensor(out, out, stats[:, :, 2, 1], ALU.add))


def norm_stats(m, dve, st, col, after=None):
    st.settle()
    for c in range(2):
        st.did(dve.bn_stats(m.stats[:, 0, c, :], m.h[:, 0, c * BANK:(c + 1) * BANK]))
    st.settle()
    st.did(dve.bn_aggr(m.stats[:, 0, 2, 0:2], m.stats[:, 0, 0:2, :]))
    st.settle()
    mean = m.stats[:, 0, 2, 0:1]
    st.did(dve.scalar_tensor_tensor(m.ms[:, col:col + 1], mean, mean, m.stats[:, 0, 2, 1:2], ALU.mult, ALU.add))
    dve.wait_ge(*after)
    rsqrt(dve, st, m.rs[:, col:col + 2], m.ms[:, col:col + 2], m.nt[:, col:col + 2], 1.0, 1e-6)
    st.settle()


def square_tile(m, act, col):
    act.activation(m.mixed[:, 1, :], m.h[:, 1, :], ACT.Square, scale=1.0 / 32, accum_out=m.ms[:, col + 1:col + 2])\
       .then_inc(m.squared, 1)


def setup_block(nc, m, x, mem, positions, mem_norm_g, c, rel_bias, buckets):
    def mem_src(t):
        return m.mixed[:, t, :]

    steps = [step(f"mem{j}", "split", j=j, kc=8, src=mem_src, dst="mem", gain=m.gain, gain_ready=(m.small_in, 48)) for j in range(4)]
    plan = Plan([], steps)
    with nc.Block() as block:
        @block.sync
        def _(sp):
            sp.dma_start(m.mixed[:, :, :], mem[0].rearrange("(t p) d -> p t d", p=P)).then_inc(m.mem_in, 16)
            sp.dma_start(m.h[:, :, :], x[0].rearrange("(t p) d -> p t d", p=P)).then_inc(m.small_in, 16)
            sp.dma_start(m.gain[:, :], mem_norm_g.rearrange("(k p) -> p k", p=P)).then_inc(m.small_in, 16)
            sp.dma_start(m.pos_i[:, :], positions.rearrange("o (t p) -> p (o t)", p=P)).then_inc(m.small_in, 16)
            sp.dma_start(m.c_col, c[0].rearrange("(k p) -> p k", p=P)).then_inc(m.small_in2, 16)
            sp.dma_start(m.buckets, buckets).then_inc(m.small_in4, 16)
            sp.dma_start(m.rel_bias[0:REL_BUCKETS, :], rel_bias).then_inc(m.small_in4, 16)
            sp.wait_ge(m.bias_rows_ready, 1)
            sp.dma_start(m.bias_rows, m.bias_out).then_inc(m.bias_in, 16)
            sp.wait_ge(m.small_in, 48)
            sp.wait_ge(m.bias_in, 16)

        @block.gpsimd
        def _(pool):
            st = Steps(pool, m.pool_step)
            st.did(pool.memset(m.ident[:, :], 0.0))
            st.did(pool.memset(m.neg_ident[:, :], 0.0))
            st.did(pool.memset(m.later[:, :], 0.0))
            st.did(pool.memset(m.later_neg[:, :], 0.0))
            st.did(pool.memset(m.upto[:, :], 1.0))
            for i, f in enumerate(FREQ):
                pool.memset(m.freq[:, i:i + 1], f).then_inc(m.freqs, 1)
            st.settle()
            pool.affine_select(out=m.ident[:, :], in_=m.ident[:, :], compare_op=ALU.not_equal, fill=1.0, base=0,
                               pattern=[[-1, P]], channel_multiplier=1).then_inc(m.consts, 1)
            st.did(pool.affine_select(out=m.neg_ident[:, :], in_=m.neg_ident[:, :], compare_op=ALU.not_equal, fill=MASKED, base=0,
                               pattern=[[-1, P]], channel_multiplier=1))
            st.did(pool.affine_select(out=m.later[:, P:TOK], in_=m.later[:, P:TOK], compare_op=ALU.is_ge, fill=1.0, base=0,
                               pattern=[[-1, P]], channel_multiplier=1))
            st.did(pool.affine_select(out=m.later_neg[:, :], in_=m.later_neg[:, :], compare_op=ALU.is_ge, fill=MASKED, base=0,
                               pattern=[[-1, P]], channel_multiplier=1))
            st.did(pool.affine_select(out=m.upto[:, :], in_=m.upto[:, :], compare_op=ALU.is_ge, fill=0.0, base=0,
                               pattern=[[1, P]], channel_multiplier=-1))

        @block.vector
        def _(dve):
            st = Steps(dve, m.dve_step)
            for l, v in enumerate(m.lam_inits):
                st.did(dve.memset(m.lam_init[:, l:l + 1], v))
                st.did(dve.memset(m.one_less_lam[:, l:l + 1], 1.0 - v))
            dve.wait_ge(m.mem_in, 16)
            mean_square(dve, st, m.stats, m.ms[:, 0:2], mem_src, 1024)
            rsqrt(dve, st, m.rs[:, 0:2], m.ms[:, 0:2], m.nt[:, 0:2], 1.0, 1e-6)
            st.settle()
            for t in range(TILES):
                last = dve.tensor_scalar(m.mixed[:, t, :], m.mixed[:, t, :], m.rs[:, t:t + 1], None, ALU.mult)
            last.then_inc(m.normed, 1)
            dve.memset(m.rel_bias[REL_BUCKETS:REL_BUCKETS + 1, :], 1.0).then_inc(m.ones_ready, 1)
            dve.wait_ge(m.gate_tanh, 1)
            st.did(dve.scalar_tensor_tensor(m.c_tanh, m.c_tanh, 1.0, m.c_col, ALU.add, ALU.mult))
            st.settle()
            st.did(dve.tensor_scalar(m.c_silu[:, :], m.c_tanh, 0.5, None, ALU.mult))
            st.did(dve.memset(m.ones_col[:, :], 1.0))
            for _, s in plan.order:
                split_lo(m, dve, plan, s)
            dve.wait_ge(m.small_in, 48)
            dve.wait_ge(m.freqs, len(FREQ))
            st.did(dve.tensor_copy(m.pos[:, :], m.pos_i[:, :]))
            st.settle()
            for t in range(TILES):
                st.did(dve.tensor_scalar(m.angle[:, t, :], m.freq[:, :], m.pos[:, t:t + 1], None, ALU.mult))
            st.settle()
            a, k = m.angle[:, :, :], m.turns[:, :, :]
            big = 1.5 * 2.0 ** 23
            for out, quarter in ((m.sin_in, 0.0), (m.cos_in, 0.25)):
                st.did(dve.tensor_scalar(k, a, float(1.0 / (2 * np.pi)), quarter, ALU.mult, ALU.add))
                st.settle()
                st.did(dve.tensor_scalar(k, k, big, None, ALU.add))
                st.settle()
                st.did(dve.tensor_scalar(k, k, big, None, ALU.subtract))
                st.settle()
                src = a
                for part in TWO_PI_PARTS:
                    st.did(dve.scalar_tensor_tensor(out[:, :, :], k, -part, src, ALU.mult, ALU.add))
                    st.settle()
                    src = out[:, :, :]
                if quarter:
                    st.did(dve.tensor_scalar(out[:, :, :], out[:, :, :], float(np.pi / 2), None, ALU.add))
                    st.settle()
                for op, turn in ((ALU.is_gt, -1.0), (ALU.is_lt, 1.0)):
                    st.did(dve.tensor_scalar(k, out[:, :, :], -turn * PI_BELOW, turn * float(np.float32(2 * np.pi)), op, ALU.mult))
                    st.settle()
                    st.did(dve.tensor_tensor(out[:, :, :], out[:, :, :], k, ALU.add))
                    st.settle()
                dve.tensor_scalar(out[:, :, :], out[:, :, :], PI_BELOW, -PI_BELOW, ALU.min, ALU.max).then_inc(m.angles, 1)

        @block.scalar
        def _(act):
            act.wait_ge(m.small_in2, 16)
            act.activation(m.c_tanh, m.c_col, ACT.Tanh, scale=0.5).then_inc(m.gate_tanh, 1)
            for _, s in plan.order:
                split_hi(m, act, plan, s)
            st = Steps(act, m.act_step)
            act.wait_ge(m.angles, 2)
            n0, n1 = 8, 16
            for (c, s_, lo, n) in ((m.cos_p, m.sin_p, 0, n0), (m.cos_m, m.sin_m, n0, n1)):
                for half in range(2):
                    act.activation(c[:, :, half * n:half * n + n], m.cos_in[:, :, lo:lo + n], ACT.Sin)
                    act.activation(s_[:, :, half * n:half * n + n], m.sin_in[:, :, lo:lo + n], ACT.Sin,
                                   scale=-1.0 if half == 0 else 1.0)
            act.wait_ge(m.aux_ready, 5)
            act.activation(m.bias_out, m.aux[0:MOBA_HEADS, 0, 0:REL], ACT.Copy).then_inc(m.bias_rows_ready, 1)

        @block.tensor
        def _(pe):
            pe.wait_ge(m.consts, 1)
            for _, s in plan.order:
                turn_blocks(m, pe, plan.bank[s.name], split_blocks(s, m), [(m.normed, 1)])
            pe.wait_ge(*aux_is_done(m, plan, "mem0"))
            pe.wait_ge(m.small_in4, 32)
            pe.wait_ge(m.ones_ready, 1)
            pe.matmul(m.aux[0:MOBA_HEADS, 0, 0:REL], m.rel_bias, m.buckets, start=True, stop=True).then_inc(m.aux_ready, 1)


def layer_units(m, l, w_in, mem_w_kv, mla_w_uq, mla_w_ukv, w_branch, w_out):
    def part(w, col, n):
        return lambda k0, kn: w[k0 * P:(k0 + kn) * P, col:col + n].rearrange("(k p) n -> p k n", p=P)

    def inw(name, col, n):
        return unit(name, "x", 8, part(w_in[l], col, n), n)

    us = [unit("memk", "mem", 8, part(mem_w_kv[l], 0, 512), 512), unit("memv", "mem", 8, part(mem_w_kv[l], 512, 512), 512)]
    us += [inw("u_" + n, COL[n], 512) for n in ("sv", "su", "eq", "dq", "dk", "dv")]
    us += [inw("u_p0", 0, 512), inw("u_p1", 512, 512), inw("u_p2", 1024, 512), inw("u_p3", 1536, 100)]

    def branch(b):
        n = BRANCHES[b]
        out = [inw("gate_" + b, COL["gates"] + 512 * n, 512)]
        for j in range(2):
            out += [inw(f"merge_{b}{j}", COL["merge"] + 1024 * n + 512 * j, 512),
                    unit(f"out_{b}{j}", "og", 4, part(w_branch[l, n], 512 * j, 512), 512)]
        return out

    gate_c, *rest_c = branch("c")
    us += branch("e") + branch("d")
    us += [unit("uq0", "qn", 3, part(mla_w_uq[l], 0, 512), 512), unit("uq1", "qn", 3, part(mla_w_uq[l], 512, 256), 256)]
    us += [gate_c]
    us += [unit(f"ukv{j}", "kvn", 2, part(mla_w_ukv[l], 512 * j, 512), 512) for j in range(2)]
    us += rest_c + branch("a") + branch("b")
    us += [unit(f"res{j}", "mx", 8, part(w_out[l], 512 * j, 512), 512) for j in range(2)]
    return us


def groups(b, t):
    order = {"a": [0, 2, 4, 6, 1, 3, 5, 7], "m": [0, 2, 4, 6, 1, 3, 5, 7], "c": [0, 2, 4, 6, 1, 3, 5, 7], "b": list(range(8)), "e": list(range(4))}[b]
    per = 4 if (t == 0 and b != "e") else 2
    return [order[i:i + per] for i in range(0, len(order), per)]


def attention_steps(b, first, gap, values=()):
    out, prev = [], None
    for t in range(TILES):
        gs = groups(b, t)
        for i, hs in enumerate(gs):
            out.append(step(f"s_{b}{t}{i}", "score", after=first(t), b=b, t=t, heads=hs))
            if i >= 1:
                out.append(step(f"p_{b}{t}{i - 1}", "probs", after=[(f"s_{b}{t}{i - 1}", gap)], b=b, t=t, heads=gs[i - 1]))
        n = len(gs) - 1
        out.append(step(f"p_{b}{t}{n}", "probs", after=[(f"s_{b}{t}{n}", gap)], b=b, t=t, heads=gs[n]))
        for g in range(2 if b == "c" else 1):
            heads = list(range(4 * g, 4 * g + 4)) if b == "c" else sorted(h for hs in gs for h in hs)
            out.append(step(f"v_{b}{t}{g}", "value", after=[(f"p_{b}{t}{n}", 1), *values], b=b, t=t, heads=heads, g=g))
    return out


def layer_steps(m):
    def region(name, n=512):
        return lambda t: m.proj[:, t, COL[name]:COL[name] + n]

    def split(name, kc, src, dst, after, before, gain=None, gain_ready=None):
        return [step(f"{name}{j}", "split", after=after, before=before, j=j, kc=kc, src=src, dst=dst, gain=gain,
                     gain_ready=gain_ready) for j in range(-(-kc // 2))]

    def turn(name, n, src, w, dst, rows, after, scale=1.0):
        return [step(f"{name}{j}", "turn", after=after, j=j, src=src, w=w, dst=dst, rows=rows, scale=scale)
                for j in range(n // 2)]

    A, B = m.qk_a, m.qk_b
    m.q = {"e": A[:, 0:4, :], "a": A[:, 0:4, :], "c": B[:, 0:4, :], "b": B[0:96, 0:8, :]}
    m.k = {"e": A[:, 4:8, :], "a": A[:, 4:6, :], "c": B[:, 4:8, :], "b": B[0:96, 8:16, :]}
    m.iq = A[:, 6:8, :]
    s = [step("norm_x", "norm_x")]
    s += [step(f"sgu_w{j}", "sgu_w", after=[("norm_x", 6 + j)], j=j) for j in range(2)]
    s += split("x", 8, lambda t: m.mixed[:, t, :], "x", [("norm_x", 3)], "u_sv", m.gain, (m.small_in, 16))
    s += turn("memk", 4, lambda t: m.memk[:, t, :], P, m.k["e"], P, [("memk", 1), ("x3", 0)])
    s += [step("sgu_norm", "sgu_norm", after=[("u_sv", 0)])]
    s += [step(f"sgu_z{t}", "sgu_z", after=[("u_su", 1)], t=t) for t in range(TILES)]
    s += turn("eq", 4, region("eq"), P, m.q["e"], P, [("u_eq", 1)], scale=float(P) ** -0.5)
    s += attention_steps("e", lambda t: [("eq1", 1)], 2)
    s += [step("rope_d", "rope", after=[("u_dk", 0)])]
    s += turn("dq", 4, region("dq"), P, m.q["c"], P, [("u_dk", 3)], scale=0.125)
    s += turn("dk", 4, region("dk"), P, m.k["c"], P, [("u_dk", 3)])
    s += attention_steps("c", lambda t: [("dk1", 1), ("u_dv", 1), ("v_e10", 0)], 2)
    s += [step("diff_mix", "diff_mix", after=[("v_c11", 0)])]
    s += [step("rope_a", "rope", after=[("u_p1", 0)])]
    s += turn("aq", 4, region("aq"), P, m.q["a"], P, [("u_p1", 3), ("v_e10", 0)], scale=0.125)
    s += turn("kk", 2, lambda t: m.kk[:, t, :], P, m.k["a"], P, [("u_p1", 3), ("v_e10", 0)])
    s += turn("iq", 2, region("iq", 256), P, m.iq, P, [("u_p1", 3), ("v_e10", 0)])
    s += [step(f"dots{2 * t + i}", "dots", after=[("iq0", 1)], t=t, heads=[i, i + 2]) for t in range(TILES) for i in range(2)]
    s += [step(f"top{t}{i}", "topk", after=[(f"dots{2 * t + 1}", 1)] + ([(f"top0{TOPK // 16 - 1}", 1)] if t else []) +
               ([(f"top{t}{i - 1}", 1)] if i else []), t=t, i=i) for t in range(TILES) for i in range(TOPK // 16)]
    s += [step("low_rank", "low_rank", after=[("u_p3", 0)])]
    s += split("qn", 3, region("cq", 384), "qn", [("low_rank", 2), ("out_d1", 0)], "uq0", m.qgain, (m.small_in2, 32))
    s += split("kvn", 2, region("ckv", 256), "kvn", [("low_rank", 2), ("uq1", 0)], "ukv0", m.kvgain, (m.small_in2, 32))
    s += attention_steps("a", lambda t: [(f"top1{TOPK // 16 - 1}", 1), ("v_c11", 0)], 2)
    s += [step("rope_b", "rope", after=[("ukv1", 0)])]
    s += turn("bq", 8, lambda t: m.proj[:, t, COL["su"]:COL["su"] + 768], 96, m.q["b"], 96, [("ukv1", 3), ("diff_mix", 0)], scale=96.0 ** -0.5)
    s += turn("bk", 8, lambda t: m.kfull[:, t, :], 96, m.k["b"], 96, [("ukv1", 3), ("diff_mix", 0)])
    s += attention_steps("b", lambda t: [("bk3", 1)], 2)
    for b in "edcab":
        s += [step("mix_" + b, "gate", after=[("gate_" + b, 0)], b=b)]
        s += split("og_" + b, 4, lambda t: m.th[:, t, :], "og", [("mix_" + b, 2)] + ([("ukv1", 0)] if b == "c" else []), f"out_{b}0")
    s += split("mx", 8, lambda t: m.mixed[:, t, :], "mx", [("out_b1", 0)], "res0")
    for i in range(8 * m.ada_parts):
        s.append(step(f"ada{i}", "ada", after=[("start", 2 * i + 1)], i=i))
        if i % 8 == 7:
            s.append(step(f"ada_sum{i // 8}", "ada_sum", after=[("start", 2 * i + 3)], i=i // 8))
    return s


class Attention:

    def __init__(self, plan):
        steps = [s for k, s in plan.order if k == "score"]
        self.number = {s.name: i for i, s in enumerate(steps)}
        self.steps = steps
        self.score_of = {(s.b, s.t, s.heads[0]): s for s in steps}
        self.probs_of = {(s.b, s.t, s.heads[0]): s for k, s in plan.order if k == "probs"}

    def width(self, s):
        return TOK if s.b == "e" or s.t == 1 else P


def turn_probs(m, pe, plan, att, s):
    score = att.score_of[s.b, s.t, s.heads[0]]
    e = m.pexp[:, att.number[score.name] % PEXP, :]
    turn_blocks(m, pe, plan.bank[s.name], [e[:, i * P:(i + 1) * P] for i in range(4)], [aux_is_done(m, plan, score.name)])


def maxima(m, dve, plan, att, s):
    k, w, n = plan.bank[s.name], att.width(s), att.number[s.name]
    dve.wait_ge(m.aux_ready, k.n + 1)
    dve.tensor_reduce(m.neg_max[:, 4 * n:4 * n + len(s.heads)], m.aux[:, k.bank, :].rearrange("p (h n) -> p h n", n=w), AX_X,
                      ALU.max, negate=True).then_inc(m.max_ready, 1)


def exponentials(m, act, plan, att, s):
    k, w, n = plan.bank[s.name], att.width(s), att.number[s.name]
    if n >= PEXP:
        old = att.steps[n - PEXP]
        act.wait_ge(m.aux_ready, plan.bank[att.probs_of[old.b, old.t, old.heads[0]].name].n + 1)
    act.wait_ge(m.max_ready, n + 1)
    for i, h in enumerate(s.heads):
        last = act.activation(m.pexp[:, n % PEXP, i * w:(i + 1) * w], m.aux[:, k.bank, i * w:(i + 1) * w], ACT.Exp,
                              bias=m.neg_max[:, 4 * n + i:4 * n + i + 1], accum_out=m.sums[s.b][:, s.t, h:h + 1])
    last.then_inc(m.aux_done[k.bank], 1)


def keep_probs(m, act, plan, s):
    k = plan.bank[s.name]
    act.wait_ge(m.aux_ready, k.n + 1)
    c = 4 // len(s.heads)
    hs = slice(s.heads[0], s.heads[-1] + 1, s.heads[1] - s.heads[0])
    act.activation(m.pt[:, hs, 0:c, :], m.aux[:, k.bank, :].rearrange("p (h c n) -> p h c n", c=c, n=P),
                   ACT.Copy).then_inc(m.aux_done[k.bank], 1)


def inverse_sums(m, dve, st, plan, att, s):
    n = len(s.heads)
    inv = m.inv[:, s.t, 0:n]
    for hs in groups(s.b, s.t):
        dve.wait_ge(*aux_is_done(m, plan, att.score_of[s.b, s.t, hs[0]].name))
    st.settle()
    st.did(dve.reciprocal(inv, m.sums[s.b][:, s.t, s.heads[0]:s.heads[0] + n]))
    st.settle()
    return inv


def layer_block(nc, m, l, weights, small, w_ada):
    (norm_g, mla_q_norm_g, mla_kv_norm_g, diff_lambda, diff_norm_g, sgu_ln_g, sgu_ln_b, sgu_w, sgu_b) = small
    plan = Plan(layer_units(m, l, *weights), layer_steps(m), rate=1)
    ROPES = {"rope_d": 1, "rope_a": 2, "rope_b": 3}
    ropes_done = {r: plan.seq[r] + 1 for r in ROPES}
    att = Attention(plan)
    gates = {s.b: plan.seq[s.name] for k, s in plan.order if k == "gate"}
    merges = [x.name for k, x in plan.order if k == "evac" and x.name.startswith("merge")]
    outs = [x.name for k, x in plan.order if k == "evac" and x.name.startswith("out")]
    DIM = {"a": 64, "b": 64, "c": 128, "e": 128}
    OUT = {"a": "aq", "b": "cq", "c": "dq", "d": "su", "e": "eq"}
    step_of = {s.name: s for k, s in plan.order if k not in ("slab", "evac")}

    def lhs_ready(x):
        name = {"x": "x3", "qn": "qn1", "kvn": "kvn0", "mx": "mx3"}.get(x.lhs)
        if x.lhs == "og":
            name = f"og_{x.name[4]}1"
        if name is None:
            return []
        s = step_of[name]
        return [aux_is_done(m, plan, f"{name[:-1]}{j}") for j in range(s.j + 1)]

    def keys(b, h, w):
        if b == "a":
            return m.k["a"][64 * (h % 2):64 * (h % 2) + 64, 0, 0:w]
        if b == "c":
            return m.k["c"][64 * (h % 2):64 * (h % 2) + 64, h // 2, 0:w]
        return m.k[b][:, h, 0:w]

    def queries(b, h, t):
        if b in "ac":
            return m.q[b][64 * (h % 2):64 * (h % 2) + 64, h // 2, t * P:(t + 1) * P]
        return m.q[b][:, h, t * P:(t + 1) * P]

    def values(b, h, c):
        if b == "a":
            return m.proj[:, c, COL["av"]:COL["av"] + 64]
        if b == "c":
            return m.proj[:, c, COL["dv"] + 128 * (h // 2):COL["dv"] + 128 * (h // 2) + 128]
        if b == "b":
            return m.vb[:, c, 64 * h:64 * h + 64]
        return m.memv[:, c, 128 * h:128 * h + 128]

    with nc.Block() as block:
        @block.sync
        def _(sp):
            parts = w_ada[0].rearrange("k (l n) -> l k n", l=m.depth)[l]
            for s in plan.slabs:
                load_slab(m, sp, plan, s)
                i = (s.i - 6) // 2
                if s.i % 2 == 0 and 0 <= i < 8 * m.ada_parts:
                    if i:
                        sp.wait_ge(m.ada_used, i)
                    sp.dma_start(m.ada_w[:, :], parts[P * (i % 8):P * (i % 8) + P, 512 * (i // 8):512 * (i // 8) + 512])\
                      .then_inc(m.ada_in, 16)

        @block.tensor
        def _(pe):
            pe.wait_ge(m.consts, 1)
            for kind, s in plan.order:
                if kind == "slab":
                    multiply(m, pe, plan, s, lhs_ready(s.unit) if s.first else [])
                elif kind == "ada_sum":
                    k = plan.bank[s.name]
                    take_bank(m, pe, k)
                    pe.wait_ge(m.ada_used, 8 * s.i + 8)
                    for i in range(4):
                        last = pe.matmul(m.aux[:, k.bank, i:i + 1], m.ada_acc[:, i * P:(i + 1) * P], m.ones_col[:, :],
                                         start=True, stop=True)
                    last.then_inc(m.aux_ready, 1)
                elif kind == "split":
                    src_ready = {"x": [(m.normed, 1)], "q": [(m.low_rank, 1)], "k": [(m.low_rank, 1)], "m": [(m.mixed_up, len(outs))],
                                 "o": [(m.gated, gates[s.name[3]] + 1 if s.name[0] == "o" else 0)]}[s.name[0]]
                    turn_blocks(m, pe, plan.bank[s.name], split_blocks(s, m), src_ready)
                elif kind == "turn":
                    ready = {"memk": [unit_is_done(m, plan, "memk")], "eq": [unit_is_done(m, plan, "u_eq")],
                             "dq": [(m.roped, ropes_done["rope_d"])], "dk": [(m.roped, ropes_done["rope_d"])],
                             "aq": [(m.roped, ropes_done["rope_a"])], "kk": [(m.roped, ropes_done["rope_a"])],
                             "iq": [(m.roped, ropes_done["rope_a"])],
                             "bq": [(m.roped, ropes_done["rope_b"])], "bk": [(m.roped, ropes_done["rope_b"])]}[s.name[:-1]]
                    blocks = [s.src(t)[:, (2 * s.j + i) * s.w:(2 * s.j + i + 1) * s.w] for i in range(2) for t in range(TILES)]
                    turn_blocks(m, pe, plan.bank[s.name], blocks, ready)
                elif kind == "sgu_w":
                    turn_blocks(m, pe, plan.bank[s.name], [m.sgu_raw[:, 4 * s.j + i, :] for i in range(4)], [(m.sgu_in, 16)])
                elif kind == "sgu_z":
                    k = plan.bank[s.name]
                    take_bank(m, pe, k)
                    pe.wait_ge(*aux_is_done(m, plan, "sgu_w0"))
                    pe.wait_ge(*aux_is_done(m, plan, "sgu_w1"))
                    pe.wait_ge(m.sgu_normed, 1)
                    for g in range(8):
                        c = COL["sv"] + 64 * g
                        last = pe.matmul(m.aux[:, k.bank, 64 * g:64 * g + 64], m.sgu_t[:, g, :], m.proj[:, s.t, c:c + 64],
                                         start=True, stop=True)
                    last.then_inc(m.aux_ready, 1)
                elif kind == "dots":
                    k, w = plan.bank[s.name], P if s.t == 0 else TOK
                    take_bank(m, pe, k)
                    for need in ("iq0", "kk0"):
                        pe.wait_ge(*aux_is_done(m, plan, need))
                    for i, h in enumerate(s.heads):
                        rows = slice(64 * (h % 2), 64 * (h % 2) + 64)
                        last = pe.matmul(m.aux[:, k.bank, i * w:(i + 1) * w], m.iq[rows, h // 2, s.t * P:(s.t + 1) * P],
                                         m.k["a"][rows, 1, 0:w], start=True, stop=True)
                    last.then_inc(m.aux_ready, 1)
                elif kind == "score":
                    k, w = plan.bank[s.name], att.width(s)
                    take_bank(m, pe, k)
                    for need in {"e": ("memk0", "memk1", "eq0", "eq1"), "c": ("dq0", "dq1", "dk0", "dk1"), "a": ("aq0", "aq1", "kk0"),
                                 "b": tuple(f"b{x}{j}" for x in "qk" for j in range(4))}[s.b]:
                        if s is att.score_of[s.b, 0, 0]:
                            pe.wait_ge(*aux_is_done(m, plan, need))
                    if s.b == "a":
                        pe.wait_ge(m.chosen, s.t + 1)
                    mask = None if s.b == "e" else m.unchosen[:, s.t, 0:w] if s.b == "a" else m.later[:, TOK - w:TOK]
                    for i, h in enumerate(s.heads):
                        out = m.aux[:, k.bank, i * w:(i + 1) * w]
                        last = pe.matmul(out, queries(s.b, h, s.t), keys(s.b, h, w), start=True, stop=mask is None)
                        if mask is not None:
                            last = pe.matmul(out, m.neg_ident[:, :], mask, start=False, stop=True)
                    last.then_inc(m.aux_ready, 1)
                elif kind == "probs":
                    turn_probs(m, pe, plan, att, s)
                elif kind == "value":
                    k = plan.bank[s.name]
                    take_bank(m, pe, k)
                    for hs in groups(s.b, s.t):
                        pe.wait_ge(*aux_is_done(m, plan, att.probs_of[s.b, s.t, hs[0]].name))
                    if s.b == "c":
                        pe.wait_ge(*unit_is_done(m, plan, "u_dv"))
                    if s.b == "e":
                        pe.wait_ge(*unit_is_done(m, plan, "memv"))
                    chunks, d = 2 if s.b == "e" or s.t == 1 else 1, DIM[s.b]
                    for i, h in enumerate(s.heads):
                        for c in range(chunks):
                            last = pe.matmul(m.aux[:, k.bank, i * d:(i + 1) * d], m.pt[:, h, c, :], values(s.b, h, c),
                                             start=c == 0, stop=c == chunks - 1)
                    last.then_inc(m.aux_ready, 1)

        @block.scalar
        def _(act):
            square_tile(m, act, 0)
            act.dma_start(m.gain[:, :], norm_g[l].rearrange("(k p) -> p k", p=P)).then_inc(m.small_in, 16)
            for i in range(LEAD):
                split_high(m, act, plan.slabs[i])
            act.dma_start(m.sgu_raw[:, :, :], sgu_w[l].rearrange("g i j -> i g j")).then_inc(m.sgu_in, 16)
            act.dma_start(m.sgu_g[:, :], sgu_ln_g[l].partition_broadcast(P)).then_inc(m.small_in3, 16)
            act.dma_start(m.sgu_be[:, :], sgu_ln_b[l].partition_broadcast(P)).then_inc(m.small_in3, 16)
            act.dma_start(m.sgu_bias[:, :], sgu_b[l].rearrange("g i -> i g")).then_inc(m.small_in3, 16)
            act.dma_start(m.qgain[:, :], mla_q_norm_g[l].rearrange("(k p) -> p k", p=P)).then_inc(m.small_in2, 16)
            act.dma_start(m.kvgain[:, :], mla_kv_norm_g[l].rearrange("(k p) -> p k", p=P)).then_inc(m.small_in2, 16)
            act.dma_start(m.lam_in[:, :], diff_lambda[l].rearrange("a d -> (a d)").partition_broadcast(P)).then_inc(m.small_in4, 16)
            act.dma_start(m.diff_g[:, :], diff_norm_g[l].partition_broadcast(P)).then_inc(m.small_in4, 16)
            for kind, s in plan.order:
                if kind == "slab":
                    if s.i + LEAD < len(plan.slabs):
                        split_high(m, act, plan.slabs[s.i + LEAD])
                elif kind == "evac":
                    src = m.pairs[s.pair][:, :, 0:s.n]
                    done = m.dense_done[s.pair]
                    if s.name[:3] in ("mem", "u_s", "u_e", "u_d", "u_p", "uq0", "uq1"):
                        act.wait_ge(m.slab_used, plan.last_slab[s.name] + 1)
                        if s.name in ("memk", "memv"):
                            dst = {"memk": m.memk, "memv": m.memv}[s.name][:, :, :]
                        elif s.name[:2] == "uq":
                            c = COL["su"] + 512 * int(s.name[2])
                            dst = m.proj[:, :, c:c + s.n]
                        else:
                            c = 512 * int(s.name[3]) if s.name[:3] == "u_p" else COL[s.name[2:]]
                            dst = m.proj[:, :, c:c + s.n]
                        act.activation(dst, src, ACT.Copy).then_inc(done, 1)
                    elif s.name[:3] == "ukv":
                        act.wait_ge(m.slab_used, plan.last_slab[s.name] + 1)
                        h0 = 4 * int(s.name[3])
                        for t in range(TILES):
                            heads = m.pairs[s.pair][:, t, :].rearrange("p (h d) -> p h d", d=128)
                            kf = m.kfull[:, t, :].rearrange("p (h d) -> p h d", d=96)
                            act.activation(kf[:, h0:h0 + 4, 0:64], heads[:, :, 0:64], ACT.Copy)
                            vv = m.vb[:, t, :].rearrange("p (h d) -> p h d", d=64)
                            last = act.activation(vv[:, h0:h0 + 4, :], heads[:, :, 64:128], ACT.Copy)
                        last.then_inc(done, 1)
                    elif s.name[:5] == "gate_":
                        act.wait_ge(m.slab_used, plan.last_slab[s.name] + 1)
                        act.activation(m.th[:, :, :], src, ACT.Tanh, scale=0.5).then_inc(m.gate_tanh, 1)
                    elif s.name[:5] == "merge":
                        act.wait_ge(m.slab_used, plan.last_slab[s.name] + 1)
                        i = merges.index(s.name)
                        if i:
                            act.wait_ge(m.mixed_up, i)
                        act.activation(m.sg[:, :, :], src, ACT.Tanh, scale=0.5).then_inc(done, 1)
                elif kind == "split":
                    split_hi(m, act, plan, s)
                elif kind == "turn":
                    k = plan.bank[s.name]
                    act.wait_ge(m.aux_ready, k.n + 1)
                    if s.name[:2] == "bk":
                        act.wait_ge(m.diffed, TILES)
                    act.activation(s.dst[:, 2 * s.j:2 * s.j + 2, :],
                                   m.aux[0:s.rows, k.bank, :].rearrange("p (k n) -> p k n", n=TOK), ACT.Copy,
                                   scale=s.scale).then_inc(m.aux_done[k.bank], 1)
                elif kind == "score":
                    exponentials(m, act, plan, att, s)
                elif kind == "probs":
                    keep_probs(m, act, plan, s)
                elif kind == "ada_sum":
                    k = plan.bank[s.name]
                    act.wait_ge(m.aux_ready, k.n + 1)
                    act.activation(m.ada[:, bass.ds(l, 1), 4 * s.i:4 * s.i + 4], m.aux[:, k.bank, 0:4].unsqueeze(1), ACT.Copy)\
                       .then_inc(m.aux_done[k.bank], 1)
                elif kind == "diff_mix":
                    act.wait_ge(m.lam_ready, 2)
                    act.activation(m.lam[:, 2:4], m.lam[:, 0:2], ACT.Exp).then_inc(m.lam_ready, 1)
            for sem_, n in ((m.small_in, 16), (m.sgu_in, 16), (m.small_in2, 32), (m.small_in3, 48), (m.small_in4, 32)):
                act.wait_ge(sem_, n)

        @block.gpsimd
        def _(pool):
            st = Steps(pool, m.pool_step)

            def rotate(x, heads, half, cos, sin, last_inc):
                r = m.rot[:, :, 0:heads * 2 * half].rearrange("p t (h d) -> p t h d", h=heads)
                c = cos.unsqueeze(2).to_broadcast([P, TILES, heads, 2 * half])
                s0 = sin[:, :, 0:half].unsqueeze(2).to_broadcast([P, TILES, heads, half])
                s1 = sin[:, :, half:2 * half].unsqueeze(2).to_broadcast([P, TILES, heads, half])
                st.settle()
                st.did(pool.tensor_tensor(r[:, :, :, 0:half], x[:, :, :, half:2 * half], s0, ALU.mult))
                st.did(pool.tensor_tensor(r[:, :, :, half:2 * half], x[:, :, :, 0:half], s1, ALU.mult))
                st.settle()
                st.did(pool.tensor_tensor(x, x, c, ALU.mult))
                st.settle()
                ins = pool.tensor_tensor(x, x, r, ALU.add)
                if last_inc is None:
                    st.did(ins)
                else:
                    ins.then_inc(last_inc, 1)

            def heads_of(c, n, w, lo, hi):
                return m.proj[:, :, c:c + n * w].rearrange("p t (h d) -> p t h d", d=w)[:, :, :, lo:hi]

            for kind, s in plan.order:
                if kind == "ada":
                    chunk = s.i % 8
                    pool.wait_ge(m.ada_in, 16 * s.i + 16)
                    if chunk == 0:
                        if s.i:
                            pool.wait_ge(m.aux_ready, plan.bank[f"ada_sum{s.i // 8 - 1}"].n + 1)
                        pool.tensor_scalar(m.ada_acc[:, :], m.ada_w[:, :], m.c_silu[:, 0:1], None, ALU.mult).then_inc(m.ada_used, 1)
                    else:
                        st.did(pool.tensor_scalar(m.ada_w[:, :], m.ada_w[:, :], m.c_silu[:, chunk:chunk + 1], None, ALU.mult))
                        st.settle()
                        pool.wait_ge(m.ada_used, s.i)
                        pool.tensor_tensor(m.ada_acc[:, :], m.ada_acc[:, :], m.ada_w[:, :], ALU.add).then_inc(m.ada_used, 1)
                if kind != "rope":
                    continue
                if s.name == "rope_d":
                    pool.wait_ge(m.sgu_out, TILES)
                    pool.wait_ge(*unit_is_done(m, plan, "u_dq"))
                    pool.wait_ge(*unit_is_done(m, plan, "u_dk"))
                    rotate(heads_of(COL["dq"], 16, 64, 0, 16), 16, 8, m.cos_p[:, :, :], m.sin_p[:, :, :], m.roped)
                elif s.name == "rope_a":
                    pool.wait_ge(*unit_is_done(m, plan, "u_p0"))
                    pool.wait_ge(*unit_is_done(m, plan, "u_p1"))
                    rotate(heads_of(COL["aq"], 9, 64, 0, 16), 9, 8, m.cos_p[:, :, :], m.sin_p[:, :, :], None)
                    rotate(heads_of(COL["iq"], 5, 64, 0, 16), 5, 8, m.cos_p[:, :, :], m.sin_p[:, :, :], None)
                    st.did(pool.tensor_scalar(m.wi[:, :, :], m.proj[:, :, COL["iw"]:COL["iw"] + 4],
                                              float(IDX_HEADS * IDX_DIM) ** -0.5, None, ALU.mult))
                    st.settle()
                    for i, c in enumerate((COL["ak"], COL["ik"])):
                        for j in range(2):
                            last = pool.tensor_copy(m.kk[:, :, P * i + 64 * j:P * i + 64 * j + 64], m.proj[:, :, c:c + 64])
                            if i + j < 2:
                                st.did(last)
                    last.then_inc(m.roped, 1)
                elif s.name == "rope_b":
                    for x in ("u_p3", "uq0", "uq1", "ukv1"):
                        pool.wait_ge(*unit_is_done(m, plan, x))
                    rotate(heads_of(COL["su"], 8, 96, 64, 96), 8, 16, m.cos_m[:, :, :], m.sin_m[:, :, :], None)
                    rotate(heads_of(COL["kr"], 1, 32, 0, 32), 1, 16, m.cos_m[:, :, :], m.sin_m[:, :, :], None)
                    st.settle()
                    kf = m.kfull[:, :, :].rearrange("p t (h d) -> p t h d", d=96)[:, :, :, 64:96]
                    kr = m.proj[:, :, COL["kr"]:COL["kr"] + 32].unsqueeze(2).to_broadcast([P, TILES, MLA_HEADS, ROT])
                    pool.tensor_copy(kf, kr).then_inc(m.roped, 1)

        @block.vector
        def _(dve):
            st = Steps(dve, m.dve_step)
            def weigh(s):
                k, w = plan.bank[s.name], P if s.t == 0 else TOK
                sc = m.index_score[:, s.t, 0:w]
                dve.wait_ge(m.aux_ready, k.n + 1)
                dve.wait_ge(m.roped, ropes_done["rope_a"])
                for i, h in enumerate(s.heads):
                    out = sc if h == 0 else m.index_work[:, s.t, 0:w]
                    st.settle()
                    ins = dve.tensor_scalar(out, m.aux[:, k.bank, i * w:(i + 1) * w], 0.0, m.wi[:, s.t, h:h + 1], ALU.max, ALU.mult)
                    if i == len(s.heads) - 1:
                        ins.then_inc(m.aux_done[k.bank], 1)
                        dve.wait_ge(*aux_is_done(m, plan, s.name))
                    else:
                        st.did(ins)
                        st.settle()
                    if h:
                        st.did(dve.tensor_tensor(sc, sc, out, ALU.add))

            def choose(t, part):
                w = P if t == 0 else TOK
                sc, work, best = m.index_score[:, t, 0:w], m.index_work[:, t, 0:w], m.best[:, :]
                st.settle()
                if part == 0:
                    st.did(dve.tensor_tensor(sc[:, w - P:w], sc[:, w - P:w], m.later_neg[:, :], ALU.add))
                src = work if part else sc
                for _ in range(2):
                    st.settle()
                    st.did(dve.max(best, src))
                    st.settle()
                    st.did(dve.match_replace(work, best, src, TAKEN))
                    src = work
                if part < TOPK // 16 - 1:
                    return
                st.settle()
                if t:
                    st.did(dve.tensor_scalar(m.unchosen[:, t, 0:P], work[:, 0:P], 0.5 * TAKEN, None, ALU.is_gt))
                dve.scalar_tensor_tensor(m.unchosen[:, t, w - P:w], work[:, w - P:w], 0.5 * TAKEN, m.later[:, P:TOK],
                                         ALU.is_gt, ALU.max).then_inc(m.chosen, 1)

            for kind, s in plan.order:
                if kind == "slab":
                    if s.i + LEAD < len(plan.slabs):
                        split_low(m, dve, plan.slabs[s.i + LEAD])
                elif kind == "norm_x":
                    split_low(m, dve, plan.slabs[0])
                    norm_stats(m, dve, st, 0, (m.squared, 1))
                    for i in range(1, LEAD):
                        split_low(m, dve, plan.slabs[i])
                    for t in range(TILES):
                        last = dve.tensor_scalar(m.mixed[:, t, :], m.h[:, t, :], m.rs[:, t:t + 1], None, ALU.mult)
                    last.then_inc(m.normed, 1)
                elif kind == "split":
                    split_lo(m, dve, plan, s)
                elif kind == "sgu_w":
                    k = plan.bank[s.name]
                    dve.wait_ge(m.aux_ready, k.n + 1)
                    dve.tensor_tensor(m.sgu_t[:, 4 * s.j:4 * s.j + 4, :], m.aux[:, k.bank, :].rearrange("p (g i) -> p g i", i=P),
                                      m.upto[:, :].unsqueeze(1).to_broadcast([P, 4, P]), ALU.mult).then_inc(m.aux_done[k.bank], 1)
                elif kind == "sgu_norm":
                    v = m.proj[:, :, COL["sv"]:COL["sv"] + 512]
                    dve.wait_ge(*unit_is_done(m, plan, "u_sv"))
                    for t in range(TILES):
                        st.did(dve.bn_stats(m.stats[:, t, 0, :], v[:, t, :]))
                    st.settle()
                    for t in range(TILES):
                        st.did(dve.bn_aggr(m.stats[:, t, 2, 0:2], m.stats[:, t, 0:1, :]))
                    st.settle()
                    st.did(dve.tensor_copy(m.ms[:, 2:4], m.stats[:, :, 2, 1]))
                    rsqrt(dve, st, m.rs[:, 2:4], m.ms[:, 2:4], m.nt[:, 2:4], 1.0, 1e-5)
                    st.settle()
                    for t in range(TILES):
                        st.did(dve.tensor_scalar(v[:, t, :], v[:, t, :], m.stats[:, t, 2, 0:1], m.rs[:, 2 + t:3 + t],
                                                 ALU.subtract, ALU.mult))
                    st.settle()
                    dve.wait_ge(m.small_in3, 48)
                    st.did(dve.tensor_tensor(v, v, m.sgu_g[:, :].unsqueeze(1).to_broadcast([P, TILES, 512]), ALU.mult))
                    st.settle()
                    dve.tensor_tensor(v, v, m.sgu_be[:, :].unsqueeze(1).to_broadcast([P, TILES, 512]), ALU.add)\
                       .then_inc(m.sgu_normed, 1)
                elif kind == "sgu_z":
                    k = plan.bank[s.name]
                    z = m.proj[:, s.t, COL["sv"]:COL["sv"] + 512]
                    u = m.proj[:, s.t, COL["su"]:COL["su"] + 512]
                    dve.wait_ge(m.aux_ready, k.n + 1)
                    dve.tensor_tensor(z.rearrange("p (g d) -> p g d", d=64), m.aux[:, k.bank, :].rearrange("p (g d) -> p g d", d=64),
                                      m.sgu_bias[:, :].unsqueeze(2).to_broadcast([P, 8, 64]), ALU.add).then_inc(m.aux_done[k.bank], 1)
                    dve.wait_ge(*aux_is_done(m, plan, s.name))
                    dve.wait_ge(*unit_is_done(m, plan, "u_su"))
                    dve.tensor_tensor(u, u, z, ALU.mult).then_inc(m.sgu_out, 1)
                elif kind == "dots":
                    weigh(s)
                elif kind == "topk":
                    choose(s.t, s.i)
                elif kind == "low_rank":
                    for x in ("u_p1", "u_p2", "u_p3"):
                        dve.wait_ge(*unit_is_done(m, plan, x))
                    for i, (c, n) in enumerate((("cq", 384), ("ckv", 256))):
                        mean_square(dve, st, m.stats, m.ms[:, 4 + 2 * i:6 + 2 * i], lambda t, c=c, n=n: m.proj[:, t, COL[c]:COL[c] + n], n)
                    rsqrt(dve, st, m.rs[:, 4:8], m.ms[:, 4:8], m.nt[:, 4:8], 1.0, 1e-6)
                    st.settle()
                    for i, (c, n) in enumerate((("cq", 384), ("ckv", 256))):
                        for t in range(TILES):
                            v = m.proj[:, t, COL[c]:COL[c] + n]
                            last = dve.tensor_scalar(v, v, m.rs[:, 4 + 2 * i + t:5 + 2 * i + t], None, ALU.mult)
                            if i + t < 2:
                                st.did(last)
                    last.then_inc(m.low_rank, 1)
                elif kind == "score":
                    maxima(m, dve, plan, att, s)
                elif kind == "value":
                    k, d, n = plan.bank[s.name], DIM[s.b], len(s.heads)
                    inv = inverse_sums(m, dve, st, plan, att, s)
                    dve.wait_ge(m.aux_ready, k.n + 1)
                    bank = m.aux[:, k.bank, :].rearrange("p (h d) -> p h d", d=d)
                    if s.b != "c":
                        dst = m.proj[:, s.t, COL[OUT[s.b]]:COL[OUT[s.b]] + 512].rearrange("p (h d) -> p h d", d=d)
                        dve.tensor_tensor(dst, bank, inv.unsqueeze(2).to_broadcast([P, n, d]), ALU.mult)\
                           .then_inc(m.aux_done[k.bank], 1)
                    else:
                        dst = m.diff_o[:, s.t, :, :, :][:, s.g, :, :]
                        dve.tensor_tensor(dst, bank, inv.unsqueeze(2).to_broadcast([P, n, d]), ALU.mult)\
                           .then_inc(m.aux_done[k.bank], 1)
                        dve.wait_ge(*aux_is_done(m, plan, s.name))
                        if s.g == 0 and s.t == 0:
                            dve.wait_ge(m.small_in4, 32)
                            pr = m.lam_in[:, :].rearrange("p (a b d) -> p a b d", a=2, b=2)
                            st.did(dve.tensor_tensor(pr[:, :, 0, :], pr[:, :, 0, :], pr[:, :, 1, :], ALU.mult))
                            dve.tensor_scalar(m.diff_g[:, :], m.diff_g[:, :], m.one_less_lam[:, bass.ds(l, 1)], None, ALU.mult)\
                               .then_inc(m.lam_ready, 1)
                            st.settle()
                            dve.tensor_reduce(m.lam[:, 0:2], pr[:, :, 0, :], AX_X, ALU.add).then_inc(m.lam_ready, 1)
                elif kind == "diff_mix":
                    dve.wait_ge(m.lam_ready, 3)
                    st.did(dve.scalar_tensor_tensor(m.lam[:, 4:5], m.lam[:, 3:4], -1.0, m.lam[:, 2:3], ALU.mult, ALU.add))
                    st.settle()
                    st.did(dve.tensor_scalar(m.lam[:, 5:6], m.lam[:, 4:5], m.lam_init[:, bass.ds(l, 1)], -1.0, ALU.add, ALU.mult))
                    st.settle()
                    o = m.proj[:, :, COL["dq"]:COL["dq"] + 512].rearrange("p t (j d) -> p t j d", d=128)
                    sq = m.proj[:, :, COL["dk"]:COL["dk"] + 512].rearrange("p t (j d) -> p t j d", d=128)
                    for t in range(TILES):
                        pair = m.diff_o[:, t, :, :, :].rearrange("p g (j two) d -> p (g j) two d", two=2)
                        st.did(dve.scalar_tensor_tensor(o[:, t, :, :], pair[:, :, 1, :], m.lam[:, 5:6], pair[:, :, 0, :],
                                                        ALU.mult, ALU.add))
                    st.settle()
                    st.did(dve.tensor_tensor(sq, o, o, ALU.mult))
                    st.settle()
                    st.did(dve.tensor_reduce(m.ms[:, 8:16].rearrange("p (t j) -> p t j", t=TILES), sq, AX_X, ALU.add))
                    rsqrt(dve, st, m.rs[:, 8:16], m.ms[:, 8:16], m.nt[:, 8:16], 1.0 / 128, 1e-6)
                    st.settle()
                    r = m.rs[:, 8:16].rearrange("p (t j) -> p t j", t=TILES)
                    st.did(dve.tensor_tensor(o, o, r.unsqueeze(3).to_broadcast([P, TILES, 4, 128]), ALU.mult))
                    st.settle()
                    for t in range(TILES):
                        dve.tensor_tensor(o[:, t, :, :], o[:, t, :, :], m.diff_g[:, :].unsqueeze(1).to_broadcast([P, 4, 128]),
                                          ALU.mult).then_inc(m.diffed, 1)
                elif kind == "gate":
                    u = plan.unit["gate_" + s.b].pair
                    g = m.pairs[u]
                    n = gates[s.b] + 1
                    dve.wait_ge(m.gate_tanh, n)
                    dve.scalar_tensor_tensor(m.th[:, :, :], m.th[:, :, :], 1.0, g, ALU.add, ALU.mult).then_inc(m.dense_done[u], 1)
                    dve.wait_ge(*unit_is_done(m, plan, "gate_" + s.b))
                    if s.b == "c":
                        dve.wait_ge(m.diffed, TILES)
                    if s.b == "d":
                        dve.wait_ge(m.sgu_out, TILES)
                    for t in range(TILES):
                        if s.b in "abe":
                            dve.wait_ge(*aux_is_done(m, plan, f"v_{s.b}{t}0"))
                    st.settle()
                    c = COL[OUT[s.b]]
                    dve.scalar_tensor_tensor(m.th[:, :, :], m.th[:, :, :], 0.5, m.proj[:, :, c:c + 512], ALU.mult, ALU.mult)\
                       .then_inc(m.gated, 1)
                elif kind == "evac" and s.name[:4] == "out_":
                    i, u = outs.index(s.name), s.pair
                    src = m.pairs[u]
                    mx = m.mixed[:, :, 512 * (i % 2):512 * (i % 2) + 512]
                    dve.wait_ge(*unit_is_done(m, plan, merges[i]))
                    dve.wait_ge(m.slab_used, plan.last_slab[s.name] + 1)
                    dve.scalar_tensor_tensor(m.sg[:, :, :], m.sg[:, :, :], 1.0, src, ALU.add, ALU.mult).then_inc(m.dense_done[u], 1)
                    dve.wait_ge(*unit_is_done(m, plan, s.name))
                    if i < 2:
                        dve.tensor_scalar(mx, m.sg[:, :, :], 0.5, None, ALU.mult).then_inc(m.mixed_up, 1)
                    else:
                        dve.wait_ge(m.mixed_up, i - 1)
                        dve.scalar_tensor_tensor(mx, m.sg[:, :, :], 0.5, mx, ALU.mult, ALU.add).then_inc(m.mixed_up, 1)
                elif kind == "evac" and s.name[:3] == "res":
                    c = 512 * int(s.name[3])
                    dve.wait_ge(m.slab_used, plan.last_slab[s.name] + 1)
                    dve.tensor_tensor(m.h[:, :, c:c + 512], m.h[:, :, c:c + 512], m.pairs[s.pair],
                                      ALU.add).then_inc(m.dense_done[s.pair], 1)


NAMES_2 = ("gq", "gk", "gv", "gr", "gg", "mq", "mk", "mv")
WIDTHS_2 = (256, 256, 512, 512, 16, 512, 512, 512)
COL_2 = dict(zip(NAMES_2, np.concatenate([[0], np.cumsum(WIDTHS_2)[:-1]]).tolist()))
PROJ_2 = sum(WIDTHS_2)
FF_PARTS = 8
CHUNKS = TOK // 64
GATE_RANK, GLA_TAU, MOBA_HEADS = 16, 16.0, 8
CHUNK = 64
REL = 384
REL_BUCKETS, REL_MAX_DIST = 32, 128


def bucket_rows():
    rel = (TOK - 1 - np.arange(REL)).astype(np.int32)
    n = np.maximum(rel, 0)
    exact = REL_BUCKETS // 2
    ratio = np.maximum(n, 1).astype(np.float32) / np.float32(exact)
    large = exact + (np.log(ratio) / np.float32(np.log(REL_MAX_DIST / exact)) * np.float32(REL_BUCKETS - exact)).astype(np.int32)
    bucket = np.where(n < exact, n, np.minimum(large, REL_BUCKETS - 1))
    rows = np.zeros((REL_BUCKETS + 1, REL), np.float32)
    rows[bucket, np.arange(REL)] = 1.0
    rows[:, rel < 0] = 0.0
    rows[REL_BUCKETS, rel < 0] = MASKED
    return rows


def second_units(w_in, w_out, w_ff1, w_ff2):
    def part(w, col, n, row=0):
        return lambda k0, kn: w[row + k0 * P:row + (k0 + kn) * P, col:col + n].rearrange("(k p) n -> p k n", p=P)

    us = [unit("w_" + c, "x", 8, part(w_in[0], COL_2[c], n), n)
          for c, n in (("gg", 16), ("gq", 512), ("mq", 512), ("mk", 512), ("mv", 512), ("gv", 512), ("gr", 512))]
    us += [unit(f"y{j}", "mx", 8, part(w_out[0], 512 * j, 512), 512) for j in range(2)]
    first = (len(us)) % 2

    def up(j):
        return unit(f"up{j}", "m", 8, part(w_ff1[0], 512 * j, 512), 512, pair=2)

    def down(j):
        return [unit(f"down{j}_{n}", f"hid{j % 2}", 4, part(w_ff2[0], 512 * n, 512, row=512 * j), 512, pair=(first + n) % 2,
                     opens=j == 0, closes=j == FF_PARTS - 1) for n in range(2)]

    us += [up(0), up(1)]
    for j in range(FF_PARTS):
        us += down(j)
        if j + 2 < FF_PARTS:
            us.append(up(j + 2))
    return us


def second_steps(m):
    def split(name, kc, src, dst, after, before, scale=None, shift=None, narrow=False):
        return [step(f"{name}{j}", "shifted" if scale is not None else "split", after=after, before=before, j=j, kc=kc, src=src,
                     dst=dst, gain=scale, shift=shift, gain_ready=None, narrow=narrow) for j in range(-(-kc // 2))]

    def turn(name, n, src, dst, after, scale=1.0):
        return [step(f"{name}{j}", "turn", after=after, j=j, src=src, dst=dst, scale=scale) for j in range(n // 2)]

    def region(c):
        return lambda t: m.proj_2[:, t, COL_2[c]:COL_2[c] + 512]

    s = [step("norm_in", "norm_in")]
    s += split("x", 8, lambda t: m.mixed[:, t, :], "x", [], "w_gg", m.scale_a, m.shift_a)
    s += [step("ada_rows", "ada_rows", after=[("w_gg", 0)])]
    s += [step("gg", "turn_gg", after=[("w_gg", 1)]), step("gla_z", "gla_z", after=[("gg", 1)])]
    s += [step(f"gla_sum{i}", "gla_sum", after=[("gla_z", 2)], i=i) for i in range(3)]
    s += [step("gla_decay", "gla_decay", after=[("gla_z", 2)])]
    s += [step("gla_mul", "gla_mul", after=[("gla_sum2", 0), ("gla_decay", 0), ("w_gq", 0)])]
    for n, src, dst in (("qa", m.qa, m.qa_t), ("ka", m.ka, m.ka_t), ("qb", m.qb, m.qb_t)):
        s += turn(n, 2, lambda t, src=src: src[:, t, :], dst, [("gla_mul", 1)], scale=CHUNK ** -0.5 if n[0] == "q" else 1.0)
    s += [step(f"inner{r}", "inner", after=[("qb0", 1)], r=r) for r in range(2)]
    s += turn("mq", 4, region("mq"), m.q["m"], [("w_mq", 1)], scale=0.125)
    s += turn("mk", 4, region("mk"), m.k["m"], [("w_mk", 1)])
    s += [step(f"state{n}", "state", after=[("w_gv", 1), ("gla_mul", 1)], n=n) for n in range(CHUNKS - 1)]
    s += [step(f"gla_o{t}{r}", "gla_o", after=[("state2", 1), ("inner1", 2)], t=t, r=r) for t in range(TILES) for r in range(2)]
    s += [step("gla_norm", "gla_norm", after=[("gla_o11", 0), ("w_gr", 0)])]
    s += attention_steps("m", lambda t: [("mk1", 1)], 1, [("w_mv", 1)])
    s += split("mx", 8, lambda t: m.mixed[:, t, :], "mx", [("gla_norm", 0), ("v_m10", 0)], "y0")
    s += [step("norm_m", "norm_m", after=[("y1", 0)])]
    s += split("m", 8, lambda t: m.mixed[:, t, :], "m", [("norm_m", 0)], "up0", m.scale_m, m.shift_m)
    for j in range(FF_PARTS):
        s += split(f"hid{j}_", 4, lambda t: m.th[:, t, :], f"hid{j % 2}", [(f"up{j}", 1 if j < FF_PARTS - 1 else 1)],
                   f"down{j}_0", narrow=True)
    return s


def second_block(nc, m, weights, small, out):
    (final_norm_g, b_ada, g_mix, w_gla_gate, b_gla_gate, g_gla_out, g_mlp, g_final) = small
    plan = Plan(second_units(*weights), second_steps(m), rate=2)
    att = Attention(plan)
    ups = [x.name for k, x in plan.order if k == "evac" and x.name.startswith("up")]

    def wait_uses(eng, banks):
        for b in banks:
            eng.wait_ge(m.aux_done[b], max(k.turn for k in plan.bank.values() if k.bank == b) + 1)

    def lhs_ready(x):
        n = {"x": 4, "mx": 4, "m": 4}.get(x.lhs, 2)
        name = x.lhs if n == 4 else f"hid{x.name[4]}_"
        return [aux_is_done(m, plan, f"{name}{j}") for j in range(n)]

    def rows(r):
        return slice(64 * r, 64 * r + 64)

    with nc.Block() as block:
        @block.sync
        def _(sp):
            ada = [m.ada_row[i * 1024:(i + 1) * 1024] for i in range(6)]
            sp.dma_start(m.row_pt, final_norm_g.partition_broadcast(P)).then_inc(m.small_in2, 16)
            for s in plan.slabs:
                load_slab(m, sp, plan, s)
                if s.last and s.unit.name == "w_mk":
                    sp.wait_ge(*aux_is_done(m, plan, "ada_rows"))
                    sp.dma_start(m.ada_row.rearrange("(k p) -> k p", p=P), m.ada_t).then_inc(m.gates_out, 16)
                if s.last and s.unit.name == "w_mv":
                    sp.wait_ge(m.gates_out, 16)
                    sp.dma_start(m.gate_a, ada[2].partition_broadcast(P)).then_inc(m.gates_in, 16)
                    sp.dma_start(m.gate_m, ada[5].partition_broadcast(P)).then_inc(m.gates_in, 16)
                if s.last and s.unit.name == "y1":
                    sp.wait_ge(m.aux_ready, plan.bank["v_m10"].n + 1)
                    sp.dma_start(m.row_pt, g_final.partition_broadcast(P)).then_inc(m.sgu_in, 16)
            sp.wait_ge(m.sgu_in, 16)
            for t in range(TILES):
                sp.wait_ge(m.out_ready, 1 + t)
                sp.dma_start(out[0, t * P:(t + 1) * P, :], m.mixed[:, t, :]).then_inc(m.mem_in, 16)
            sp.wait_ge(m.mem_in, 16 * TILES)

        @block.tensor
        def _(pe):
            pe.wait_ge(m.consts, 1)
            for kind, s in plan.order:
                k = plan.bank.get(s.name) if kind not in ("slab", "evac") else None
                if kind == "slab":
                    if s.first and s.unit.name == "up0":
                        wait_uses(pe, (0, 1))
                    multiply(m, pe, plan, s, lhs_ready(s.unit) if s.first else [])
                elif kind in ("split", "shifted"):
                    if s.name[:3] == "hid":
                        ready = [(m.gated, int(s.name[3]) + 1)]
                    elif s.name[:2] == "mx":
                        ready = [(m.gla_normed, 1), aux_is_done(m, plan, "v_m00"), aux_is_done(m, plan, "v_m10")]
                    else:
                        n = 1 if s.name[0] == "x" else 2
                        ready = [(m.normed, n), (m.normed_act, n)]
                    turn_blocks(m, pe, k, split_blocks(s, m), ready)
                elif kind == "turn":
                    ready = {"mq": [unit_is_done(m, plan, "w_mq")], "mk": [unit_is_done(m, plan, "w_mk")]}\
                        .get(s.name[:2], [(m.gla_scaled, 1)])
                    blocks = [s.src(t)[:, (2 * s.j + i) * P:(2 * s.j + i + 1) * P] for i in range(2) for t in range(TILES)]
                    turn_blocks(m, pe, k, blocks, ready)
                elif kind == "ada_rows":
                    turn_blocks(m, pe, k, [m.ada_cols], [(m.ada_in, 1)])
                elif kind == "turn_gg":
                    c = COL_2["gg"]
                    turn_blocks(m, pe, k, [m.proj_2[:, t, c:c + GATE_RANK] for t in range(TILES)], [unit_is_done(m, plan, "w_gg")])
                elif kind == "gla_z":
                    take_bank(m, pe, k)
                    pe.wait_ge(*aux_is_done(m, plan, "gg"))
                    pe.wait_ge(m.small_in3, 32)
                    for t in range(TILES):
                        last = pe.matmul(m.aux[:, k.bank, t * 256:(t + 1) * 256], m.gg_t[:, t * P:(t + 1) * P], m.w_gate,
                                         start=True, stop=True)
                    last.then_inc(m.aux_ready, 1)
                elif kind == "gla_sum":
                    take_bank(m, pe, k)
                    pe.wait_ge(m.gla_log, 5)
                    pe.wait_ge(m.tables, 4)
                    for t in range(TILES):
                        last = pe.matmul(m.aux[:, k.bank, t * 256:(t + 1) * 256], (m.from_middle, m.to_end, m.from_start)[s.i],
                                         m.log_decay[:, t, :], start=True, stop=True)
                    last.then_inc(m.aux_ready, 1)
                elif kind == "gla_decay":
                    take_bank(m, pe, k)
                    for t in range(TILES):
                        for p in range(2):
                            c = 2 * (2 * t + p)
                            last = pe.matmul(m.aux[:, k.bank, c:c + 2], m.log_decay[:, t, p * P:(p + 1) * P], m.chunk_ones,
                                             start=True, stop=True)
                    last.then_inc(m.aux_ready, 1)
                elif kind == "inner":
                    take_bank(m, pe, k)
                    for need in ("qa0", "ka0"):
                        pe.wait_ge(*aux_is_done(m, plan, need))
                    for p in range(2):
                        for t in range(TILES):
                            tok = slice(t * P, (t + 1) * P)
                            last = pe.matmul(m.aux[:, k.bank, (2 * p + t) * P:(2 * p + t + 1) * P], m.ka_t[rows(s.r), p, tok],
                                             m.qa_t[rows(s.r), p, tok], start=True, stop=True)
                    last.then_inc(m.aux_ready, 1)
                elif kind == "state":
                    take_bank(m, pe, k)
                    pe.wait_ge(*unit_is_done(m, plan, "w_gv"))
                    pe.wait_ge(m.gla_scaled, 1)
                    t, c = s.n // 2, s.n % 2
                    for p in range(2):
                        v = COL_2["gv"] + 256 * p
                        last = pe.matmul(m.aux[:, k.bank, 256 * p:256 * p + 256], m.kb[rows(c), t, p * P:(p + 1) * P],
                                         m.proj_2[rows(c), t, v:v + 256], start=True, stop=True)
                    last.then_inc(m.aux_ready, 1)
                elif kind == "gla_o":
                    take_bank(m, pe, k)
                    pe.wait_ge(m.masked, 1)
                    for n in range(CHUNKS - 1):
                        pe.wait_ge(*aux_is_done(m, plan, f"state{n}"))
                    pe.wait_ge(*unit_is_done(m, plan, "w_gv"))
                    pe.wait_ge(*aux_is_done(m, plan, "qb0"))
                    for p in range(2):
                        v = COL_2["gv"] + 128 * (2 * p + s.r)
                        bank = m.aux[:, k.bank, p * P:(p + 1) * P]
                        pe.matmul(bank, m.inner[:, s.r, 2 * p + s.t, :], m.proj_2[:, s.t, v:v + 128], start=True, stop=False,
                                  skip_group_check=True)
                        for c in range(2):
                            n = 2 * s.t + c
                            if n:
                                tok = slice(64 * n, 64 * n + 64)
                                last = pe.matmul(bank[rows(c), :], m.qb_t[rows(s.r), p, tok], m.state[rows(s.r), n - 1, p, :],
                                                 start=False, stop=c == 1, skip_group_check=True)
                    last.then_inc(m.aux_ready, 1)
                elif kind == "score":
                    take_bank(m, pe, k)
                    if s is att.score_of["m", 0, 0]:
                        for need in ("mq0", "mq1", "mk0", "mk1"):
                            pe.wait_ge(*aux_is_done(m, plan, need))
                        pe.wait_ge(m.bias_in, 16)
                    w = att.width(s)
                    for i, h in enumerate(s.heads):
                        bank = m.aux[:, k.bank, i * w:(i + 1) * w]
                        pe.matmul(bank, m.q["m"][rows(h % 2), h // 2, s.t * P:(s.t + 1) * P], m.k["m"][rows(h % 2), h // 2, 0:w],
                                  start=True, stop=False)
                        last = pe.matmul(bank, m.backward, m.bias[:, h, P - s.t * P:P - s.t * P + w], start=False, stop=True)
                    last.then_inc(m.aux_ready, 1)
                elif kind == "probs":
                    turn_probs(m, pe, plan, att, s)
                elif kind == "value":
                    take_bank(m, pe, k)
                    for hs in groups(s.b, s.t):
                        pe.wait_ge(*aux_is_done(m, plan, att.probs_of[s.b, s.t, hs[0]].name))
                    pe.wait_ge(*unit_is_done(m, plan, "w_mv"))
                    for i, h in enumerate(s.heads):
                        v = COL_2["mv"] + 64 * h
                        for c in range(s.t + 1):
                            last = pe.matmul(m.aux[:, k.bank, i * 64:(i + 1) * 64], m.pt[:, h, c, :], m.proj_2[:, c, v:v + 64],
                                             start=c == 0, stop=c == s.t)
                    last.then_inc(m.aux_ready, 1)

        @block.scalar
        def _(act):
            for dst, src in ((m.ada_bias, b_ada[0]), (m.g_mix, g_mix[0]), (m.g_mlp, g_mlp[0])):
                act.dma_start(dst, src.rearrange("(k p) -> p k", p=P)).then_inc(m.small_in, 16)
            act.dma_start(m.w_gate, w_gla_gate[0]).then_inc(m.small_in3, 16)
            act.dma_start(m.b_gate, b_gla_gate[0].partition_broadcast(P)).then_inc(m.small_in3, 16)
            act.dma_start(m.bias, bass.AP(tensor=m.bias_rows.tensor, offset=0, ap=[[1, P], [REL, MOBA_HEADS], [1, TOK]]))\
               .then_inc(m.bias_in, 16)
            act.dma_start(m.g_out, g_gla_out[0].partition_broadcast(P)).then_inc(m.small_in4, 16)

            def norm(n, ready):
                act.wait_ge(*ready)
                square_tile(m, act, 2 * n)
                act.wait_ge(m.normed, n)
                act.activation(m.mixed[:, 1, :], m.h[:, 1, :], ACT.Copy, scale=m.rs[:, 2 * n + 1:2 * n + 2]).then_inc(m.normed_act, 1)

            square_tile(m, act, 0)
            for i in range(LEAD):
                split_high(m, act, plan.slabs[i])
            for kind, s in plan.order:
                k = plan.bank.get(s.name) if kind not in ("slab", "evac") else None
                if kind == "slab":
                    if s.i + LEAD < len(plan.slabs):
                        split_high(m, act, plan.slabs[s.i + LEAD])
                elif kind == "norm_in":
                    norm(1, (m.scales, 1))
                elif kind == "norm_m":
                    norm(2, (m.h_ready, 2))
                elif kind == "evac" and s.name == "w_gr":
                    act.wait_ge(m.slab_used, plan.last_slab[s.name] + 1)
                    act.activation(m.th[:, :, :], m.pairs[s.pair], ACT.Tanh, scale=0.5).then_inc(m.gate_tanh, 1)
                elif kind == "evac" and s.name[:2] == "w_":
                    act.wait_ge(m.slab_used, plan.last_slab[s.name] + 1)
                    c = COL_2[s.name[2:]]
                    act.activation(m.proj_2[:, :, c:c + s.n], m.pairs[s.pair][:, :, 0:s.n], ACT.Copy).then_inc(m.dense_done[s.pair], 1)
                elif kind == "evac" and s.name[:2] == "up":
                    act.wait_ge(m.slab_used, plan.last_slab[s.name] + 1)
                    act.activation(m.th[:, :, :], m.pairs[2], ACT.Relu).then_inc(m.dense_done[2], 1)
                elif kind == "split":
                    split_hi(m, act, plan, s)
                elif kind == "shifted":
                    k0, kn = split_cols(s, m)
                    act.wait_ge(m.shifted, plan.seq[s.name] + 1)
                    act.activation(m.lhs[s.dst][0][:, k0:k0 + kn, :], m.shift_tmp[:, s.j % 2, :, :], ACT.Copy).then_inc(m.shifted_hi, 1)
                elif kind == "turn":
                    act.wait_ge(m.aux_ready, k.n + 1)
                    act.activation(s.dst[:, 2 * s.j:2 * s.j + 2, :], m.aux[:, k.bank, :].rearrange("p (k n) -> p k n", n=TOK), ACT.Copy,
                                   scale=s.scale).then_inc(m.aux_done[k.bank], 1)
                elif kind == "ada_rows":
                    act.wait_ge(m.aux_ready, k.n + 1)
                    act.activation(m.ada_t, m.aux[0:48, k.bank, 0:P], ACT.Copy).then_inc(m.aux_done[k.bank], 1)
                elif kind == "turn_gg":
                    act.wait_ge(m.aux_ready, k.n + 1)
                    act.activation(m.gg_t, m.aux[0:GATE_RANK, k.bank, 0:TOK], ACT.Copy).then_inc(m.aux_done[k.bank], 1)
                elif kind == "gla_z":
                    act.wait_ge(m.gla_log, 1)
                    act.activation(m.th[:, 0, :], m.th[:, 0, :], ACT.Exp).then_inc(m.gla_log, 1)
                    act.wait_ge(m.gla_log, 3)
                    act.activation(m.th[:, 0, :], m.th[:, 0, :], ACT.Ln).then_inc(m.gla_log, 1)
                elif kind == "gla_sum":
                    act.wait_ge(m.aux_ready, k.n + 1)
                    bank = m.aux[:, k.bank, :].rearrange("p (t n) -> p t n", t=TILES)
                    if s.i == 0:
                        act.activation(m.ka, bank, ACT.Exp, scale=-1.0)
                    act.activation((m.qa, m.kb, m.qb)[s.i], bank, ACT.Exp).then_inc(m.aux_done[k.bank], 1)
                elif kind == "gla_decay":
                    act.wait_ge(m.aux_ready, k.n + 1)
                    act.activation(m.decay, m.aux[:, k.bank, 0:8], ACT.Exp).then_inc(m.aux_done[k.bank], 1)
                elif kind == "inner":
                    act.wait_ge(m.aux_ready, k.n + 1)
                    act.activation(m.inner[:, s.r, :, :], m.aux[:, k.bank, :].rearrange("p (b n) -> p b n", n=P), ACT.Copy)\
                       .then_inc(m.aux_done[k.bank], 1)
                elif kind == "score":
                    exponentials(m, act, plan, att, s)
                elif kind == "probs":
                    keep_probs(m, act, plan, s)
            act.wait_ge(m.h_ready, 4)
            square_tile(m, act, 6)
            for sem_, n in ((m.small_in, 48), (m.small_in3, 32), (m.small_in4, 16), (m.bias_in, 16)):
                act.wait_ge(sem_, n)

        @block.gpsimd
        def _(pool):
            st = Steps(pool, m.pool_step)
            st.did(pool.memset(m.from_start, 1.0))
            st.did(pool.memset(m.to_end, 1.0))
            st.did(pool.memset(m.backward, 0.0))
            st.did(pool.memset(m.chunk_ones, 0.0))
            st.settle()
            st.did(pool.affine_select(out=m.from_start, in_=m.from_start, compare_op=ALU.is_ge, fill=0.0, base=0, pattern=[[1, P]],
                                      channel_multiplier=-1))
            st.did(pool.affine_select(out=m.to_end, in_=m.to_end, compare_op=ALU.is_ge, fill=0.0, base=-1, pattern=[[-1, P]],
                                      channel_multiplier=1))
            st.did(pool.affine_select(out=m.backward, in_=m.backward, compare_op=ALU.not_equal, fill=1.0, base=1 - P,
                                      pattern=[[1, P]], channel_multiplier=1))
            st.settle()
            st.did(pool.memset(m.chunk_ones[0:64, 0:1], 1.0))
            st.did(pool.memset(m.chunk_ones[64:P, 1:2], 1.0))
            st.settle()
            st.did(pool.memset(m.from_start[0:64, 64:P], 0.0))
            st.did(pool.memset(m.to_end[64:P, 0:64], 0.0))
            st.settle()
            for q in range(4):
                r = slice(32 * q, 32 * q + 32)
                pool.tensor_scalar(m.from_middle[r, :], (m.from_start if q % 2 else m.to_end)[r, :], 1.0 if q % 2 else -1.0,
                                   None, ALU.mult).then_inc(m.tables, 1)
            for r in range(2):
                pool.wait_ge(*aux_is_done(m, plan, f"inner{r}"))
                st.did(pool.affine_select(out=m.inner[:, r, :, :], in_=m.inner[:, r, :, :], compare_op=ALU.is_ge, fill=0.0, base=0,
                                          pattern=[[0, 4], [1, P]], channel_multiplier=-1))
            st.settle()
            pool.memset(m.inner[0:64, :, :, 64:P], 0.0).then_inc(m.masked, 1)

        @block.vector
        def _(dve):
            st = Steps(dve, m.dve_step)

            def norm(n):
                norm_stats(m, dve, st, 2 * n, (m.squared, n + 1))
                dve.tensor_scalar(m.mixed[:, 0, :], m.h[:, 0, :], m.rs[:, 2 * n:2 * n + 1], None, ALU.mult).then_inc(m.normed, 1)

            for kind, s in plan.order:
                k = plan.bank.get(s.name) if kind not in ("slab", "evac") else None
                if kind == "slab":
                    if s.i + LEAD < len(plan.slabs):
                        split_low(m, dve, plan.slabs[s.i + LEAD])
                elif kind == "norm_in":
                    norm_stats(m, dve, st, 0, (m.squared, 1))
                    dve.wait_ge(m.small_in2, 16)
                    for t in (1, 0):
                        dve.scalar_tensor_tensor(m.h[:, t, :], m.h[:, t, :], m.rs[:, t:t + 1], m.row_pt, ALU.mult, ALU.mult)\
                           .then_inc(m.scales, 1)
                    dve.wait_ge(m.scales, 2)
                    dve.wait_ge(m.small_in, 48)
                    dve.tensor_tensor(m.ada_cols, m.ada_cols, m.ada_bias, ALU.add).then_inc(m.ada_in, 1)
                    dve.wait_ge(m.ada_in, 1)
                    for scale, g in ((m.scale_a, m.g_mix), (m.scale_m, m.g_mlp)):
                        st.did(dve.scalar_tensor_tensor(scale, scale, 1.0, g, ALU.add, ALU.mult))
                    st.settle()
                    norm(1)
                    for i in range(LEAD):
                        split_low(m, dve, plan.slabs[i])
                elif kind == "norm_m":
                    norm(2)
                elif kind == "split":
                    split_lo(m, dve, plan, s)
                elif kind == "shifted":
                    k0, kn = split_cols(s, m)
                    tmp, (hi, lo) = m.shift_tmp[:, s.j % 2, :, :], m.lhs[s.dst]
                    dve.wait_ge(m.aux_ready, k.n + 1)
                    st.settle()
                    for i in range(kn):
                        last = dve.tensor_scalar(tmp[:, i, :], m.aux[:, k.bank, i * TOK:(i + 1) * TOK], s.gain[:, k0 + i:k0 + i + 1],
                                                 s.shift[:, k0 + i:k0 + i + 1], ALU.mult, ALU.add)
                    last.then_inc(m.shifted, 1)
                    dve.wait_ge(m.shifted_hi, plan.seq[s.name] + 1)
                    dve.tensor_tensor(lo[:, k0:k0 + kn, :], tmp, hi[:, k0:k0 + kn, :].bitcast(F32), ALU.subtract)\
                       .then_inc(m.aux_done[k.bank], 1)
                elif kind == "gla_z":
                    dve.wait_ge(m.aux_ready, k.n + 1)
                    z, e = m.log_decay, m.th[:, 0, :].rearrange("p (t n) -> p t n", t=TILES)
                    dve.tensor_tensor(z, m.aux[:, k.bank, :].rearrange("p (t n) -> p t n", t=TILES),
                                      m.b_gate.unsqueeze(1).to_broadcast([P, TILES, 256]), ALU.add).then_inc(m.aux_done[k.bank], 1)
                    dve.wait_ge(*aux_is_done(m, plan, s.name))
                    dve.scalar_tensor_tensor(e, z, -1.0, z, ALU.mult, ALU.min).then_inc(m.gla_log, 1)
                    dve.wait_ge(m.gla_log, 2)
                    dve.tensor_scalar(e, e, 1.0, None, ALU.add).then_inc(m.gla_log, 1)
                    st.did(dve.tensor_scalar(z, z, 0.0, 1.0 / GLA_TAU, ALU.min, ALU.mult))
                    dve.wait_ge(m.gla_log, 4)
                    st.settle()
                    dve.scalar_tensor_tensor(z, e, -1.0 / GLA_TAU, z, ALU.mult, ALU.add).then_inc(m.gla_log, 1)
                elif kind == "gla_mul":
                    for i in range(3):
                        dve.wait_ge(*aux_is_done(m, plan, f"gla_sum{i}"))
                    dve.wait_ge(*unit_is_done(m, plan, "w_gq"))
                    for x, c in ((m.qa, "gq"), (m.ka, "gk"), (m.qb, "gq"), (m.kb, "gk")):
                        last = dve.tensor_tensor(x, x, m.proj_2[:, :, COL_2[c]:COL_2[c] + 256], ALU.mult)
                    last.then_inc(m.gla_scaled, 1)
                elif kind == "state":
                    dve.wait_ge(m.aux_ready, k.n + 1)
                    if s.n == 0:
                        dve.wait_ge(*aux_is_done(m, plan, "gla_decay"))
                    else:
                        dve.wait_ge(*aux_is_done(m, plan, f"state{s.n - 1}"))
                    st.settle()
                    for r in range(2):
                        new = m.aux[rows(r), k.bank, :].rearrange("p (b n) -> p b n", b=2)[:, :, r * P:(r + 1) * P]
                        if s.n == 0:
                            last = dve.tensor_copy(m.state[rows(r), 0, :, :], new)
                        else:
                            for p in range(2):
                                d = 2 * (2 * (s.n // 2) + p) + s.n % 2
                                last = dve.scalar_tensor_tensor(m.state[rows(r), s.n, p, :], m.state[rows(r), s.n - 1, p, :],
                                                                m.decay[rows(r), d:d + 1], new[:, p, :], ALU.mult, ALU.add)
                    last.then_inc(m.aux_done[k.bank], 1)
                elif kind == "gla_o":
                    dve.wait_ge(m.aux_ready, k.n + 1)
                    o = m.mixed[:, s.t, 0:512].rearrange("p (b r d) -> p b r d", b=2, r=2)[:, :, s.r, :]
                    dve.tensor_copy(o, m.aux[:, k.bank, 0:256].rearrange("p (b d) -> p b d", b=2)).then_inc(m.aux_done[k.bank], 1)
                elif kind == "gla_norm":
                    u = plan.unit["w_gr"].pair
                    dve.wait_ge(m.gate_tanh, 1)
                    dve.scalar_tensor_tensor(m.th[:, :, :], m.th[:, :, :], 1.0, m.pairs[u], ALU.add, ALU.mult).then_inc(m.dense_done[u], 1)
                    for t in range(TILES):
                        for r in range(2):
                            dve.wait_ge(*aux_is_done(m, plan, f"gla_o{t}{r}"))
                    o = m.mixed[:, :, 0:512].rearrange("p t (h d) -> p t h d", d=128)
                    sq = m.proj_2[:, :, 0:512].rearrange("p t (h d) -> p t h d", d=128)
                    st.did(dve.tensor_tensor(sq, o, o, ALU.mult))
                    st.settle()
                    st.did(dve.tensor_reduce(m.ms[:, 8:16].rearrange("p (t h) -> p t h", t=TILES), sq, AX_X, ALU.add))
                    rsqrt(dve, st, m.rs[:, 8:16], m.ms[:, 8:16], m.nt[:, 8:16], 1.0 / 128, 1e-6)
                    st.settle()
                    r = m.rs[:, 8:16].rearrange("p (t h) -> p t h", t=TILES)
                    st.did(dve.tensor_tensor(o, o, r.unsqueeze(3).to_broadcast([P, TILES, 4, 128]), ALU.mult))
                    st.settle()
                    dve.wait_ge(m.small_in4, 16)
                    o = m.mixed[:, :, 0:512]
                    st.did(dve.tensor_tensor(o, o, m.g_out.unsqueeze(1).to_broadcast([P, TILES, 512]), ALU.mult))
                    dve.wait_ge(*unit_is_done(m, plan, "w_gr"))
                    st.settle()
                    dve.scalar_tensor_tensor(o, m.th[:, :, :], 0.5, o, ALU.mult, ALU.mult).then_inc(m.gla_normed, 1)
                elif kind == "score":
                    maxima(m, dve, plan, att, s)
                elif kind == "value":
                    inv = inverse_sums(m, dve, st, plan, att, s)
                    dve.wait_ge(m.aux_ready, k.n + 1)
                    dve.tensor_tensor(m.mixed[:, s.t, 512:1024].rearrange("p (h d) -> p h d", d=64),
                                      m.aux[:, k.bank, :].rearrange("p (h d) -> p h d", d=64),
                                      inv.unsqueeze(2).to_broadcast([P, 8, 64]), ALU.mult).then_inc(m.aux_done[k.bank], 1)
                elif kind == "evac" and (s.name[0] == "y" or (s.name[:4] == "down" and s.closes)):
                    c = 512 * int(s.name[-1])
                    gate = (m.gate_a if s.name[0] == "y" else m.gate_m)[:, c:c + 512]
                    dve.wait_ge(m.slab_used, plan.last_slab[s.name] + 1)
                    dve.wait_ge(m.gates_in, 32)
                    st.settle()
                    dve.tensor_tensor(m.th[:, :, :], m.pairs[s.pair], gate.unsqueeze(1).to_broadcast([P, TILES, 512]), ALU.mult)\
                       .then_inc(m.dense_done[s.pair], 1)
                    dve.wait_ge(*unit_is_done(m, plan, s.name))
                    st.settle()
                    dve.tensor_tensor(m.h[:, :, c:c + 512], m.h[:, :, c:c + 512], m.th[:, :, :], ALU.add).then_inc(m.h_ready, 1)
                    dve.wait_ge(m.h_ready, (2 if s.name[0] == "d" else 0) + int(s.name[-1]) + 1)
                elif kind == "evac" and s.name[:2] == "up":
                    dve.wait_ge(m.dense_done[2], s.turn + 1)
                    dve.tensor_tensor(m.th[:, :, :], m.th[:, :, :], m.th[:, :, :], ALU.mult).then_inc(m.gated, 1)
            norm_stats(m, dve, st, 6, (m.squared, 4))
            dve.wait_ge(m.sgu_in, 16)
            for t in range(TILES):
                dve.scalar_tensor_tensor(m.mixed[:, t, :], m.h[:, t, :], m.rs[:, 6 + t:7 + t], m.row_pt, ALU.mult, ALU.mult)\
                   .then_inc(m.out_ready, 1)


def allocate(nc, ctx, depth):
    def sb(name, shape, dt=F32):
        return ctx.enter_context(nc.sbuf_tensor("b_" + name, shape, dt))

    def sem(name):
        return ctx.enter_context(nc.semaphore(name))

    m = Record()
    m.depth = depth
    m.raw = sb("raw", [P, RAW_SLOTS, SLAB])
    m.wh = sb("wh", [P, SPLIT_SLOTS, SLAB], F32R)
    m.wl = sb("wl", [P, SPLIT_SLOTS, SLAB], F32R)
    xh, xl = sb("xh", [P, 8, TOK], F32R), sb("xl", [P, 8, TOK], F32R)
    mh, ml = sb("mh", [P, 8, TOK], F32R), sb("ml", [P, 8, TOK], F32R)
    gh, gl = sb("gh", [P, 4, TOK], F32R), sb("gl", [P, 4, TOK], F32R)
    m.lhs = {"x": (xh, xl), "mx": (xh, xl), "m": (xh, xl), "mem": (mh, ml), "hid0": (mh[:, 0:4, :], ml[:, 0:4, :]),
             "hid1": (mh[:, 4:8, :], ml[:, 4:8, :]), "og": (gh, gl), "qn": (gh[:, 0:3, :], gl[:, 0:3, :]),
             "kvn": (gh[:, 0:2, :], gl[:, 0:2, :])}
    m.ada_w, m.ada_acc = sb("ada_w", [P, 512]), sb("ada_acc", [P, 512])
    m.h = sb("h", [P, TILES, 1024])
    m.proj = sb("proj", [P, TILES, PROJ])
    kv = sb("kv", [P, 2560])
    m.memk = kv[:, 0:1024].rearrange("p (t n) -> p t n", t=TILES)
    m.memv = kv[:, 1024:2048].rearrange("p (t n) -> p t n", t=TILES)
    m.kfull = kv[:, 0:1536].rearrange("p (t n) -> p t n", t=TILES)
    m.vb = kv[:, 1536:2560].rearrange("p (t n) -> p t n", t=TILES)
    m.qk_a = sb("qk_a", [P, 8, TOK])
    m.qk_b = sb("qk_b", [P, 16, TOK])
    pt = sb("pt", [P, 8 * 2 * P])
    m.pt = pt[:, :].rearrange("p (h c n) -> p h c n", h=8, c=2)
    m.sgu_raw = pt[:, 0:1024].rearrange("p (g j) -> p g j", g=8)
    m.pexp = sb("pexp", [P, PEXP, BANK])
    m.th = sb("th", [P, TILES, 512])
    m.sgu_g, m.sgu_be = m.th[:, 0, :], m.th[:, 1, :]
    m.sg = sb("sg", [P, TILES, 512])
    m.sgu_t = m.sg[:, :, :].rearrange("p t n -> p (t n)").rearrange("p (g i) -> p g i", i=P)
    m.mixed = sb("mixed", [P, TILES, 1024])
    m.diff_o = m.qk_b[:, 8:16, :].rearrange("p k n -> p (k n)").rearrange("p (t g h d) -> p t g h d", t=TILES, g=2, h=4)
    m.index_score = m.proj[:, :, COL["dk"]:COL["dk"] + 256]
    m.index_work = m.proj[:, :, COL["dk"] + 256:COL["dk"] + 512]
    m.unchosen = sb("unchosen", [P, TILES, TOK], BF16)
    m.ident = sb("ident", [P, P])
    m.neg_ident = sb("neg_ident", [P, P], BF16)
    m.later = sb("later", [P, TOK], BF16)
    m.later_neg = sb("later_neg", [P, P])
    m.upto = sb("upto", [P, P])
    m.kk = sb("kk", [P, TILES, 2 * P])
    m.rot = m.proj[:, :, COL["sv"] + 256:COL["sv"] + 512]
    m.diff_g = sb("diff_g", [P, P])
    m.lam_in = sb("lam_in", [P, 256])
    small = sb("small", [P, 441])
    at = [0]

    def cut(n, *dims):
        c = small[:, at[0]:at[0] + n]
        at[0] += n
        if dims:
            names = "abc"[:len(dims)]
            kw = dict(zip(names, dims))
            return c.rearrange(f"p ({' '.join(names)}) -> p {' '.join(names)}", **kw)
        return c
    m.gain, m.qgain, m.kvgain = cut(8), cut(3), cut(2)
    m.stats = cut(36, TILES, 3, 6)
    m.ms, m.rs, m.nt = cut(16), cut(16), cut(16)
    m.sgu_bias, m.wi, m.best = cut(8), cut(8, TILES, 4), cut(8)
    m.sums = {b: cut(16, TILES, 8) for b in "abce"}
    m.sums["m"] = m.sums["a"]
    m.inv = cut(16, TILES, 8)
    m.neg_max = cut(4 * 22)
    m.lam, m.lam_init, m.one_less_lam = cut(8), cut(depth), cut(depth)
    m.pos = cut(2)
    m.cos_p, m.sin_p, m.cos_m, m.sin_m = cut(32, TILES, 16), cut(32, TILES, 16), cut(64, TILES, 32)[:, :, :], None
    small2 = sb("small2", [P, 66])
    m.ada_parts = ADA_PARTS // depth
    m.ada = sb("ada", [P, depth, 4 * m.ada_parts])
    m.c_silu, m.ones_col = cut(8), cut(1)
    m.ada_bias = m.pexp[:, 0, 0:48]
    cols = m.ada[:, :, :].rearrange("p l n -> p (l n)")
    m.shift_a, m.scale_a, m.shift_m, m.scale_m = (cols[:, 8 * i:8 * i + 8] for i in (0, 1, 3, 4))
    m.ada_cols = cols
    m.sin_m = small2[:, 0:64].rearrange("p (t n) -> p t n", t=TILES)
    n = 24
    flat = m.th[:, :, :].rearrange("p t n -> p (t n)")
    m.freq = flat[:, 0:n]
    m.angle, m.turns, m.sin_in, m.cos_in = (flat[:, n + i * 2 * n:n + (i + 1) * 2 * n].rearrange("p (t n) -> p t n", t=TILES)
                                            for i in range(4))
    m.pos_i = small2[:, 64:66].bitcast(I32)
    m.dense = ctx.enter_context(nc.psum_tensor("dense", [P, 4, BANK], F32))
    m.aux = ctx.enter_context(nc.psum_tensor("aux", [P, AUX, BANK], F32))
    m.pairs = [m.dense[:, 0:2, :], m.dense[:, 2:4, :], m.aux[:, 0:2, :]]
    flat = m.proj[:, :, :].rearrange("p t n -> p (t n)")
    m.buckets, m.rel_bias = flat[0:REL_BUCKETS + 1, 6144:6144 + REL], flat[0:REL_BUCKETS + 1, 6528:6536]
    m.bias_out, m.c_col, m.c_tanh = flat[0:MOBA_HEADS, 6536:6536 + REL], flat[:, 6920:6928], flat[:, 6928:6936]
    m.proj_2 = flat[:, 0:TILES * PROJ_2].rearrange("p (t n) -> p t n", t=TILES)
    m.bias = flat[:, 6176:8224].rearrange("p (h n) -> p h n", h=MOBA_HEADS)
    m.gate_m = flat[:, 8224:9248]
    m.g_mix, m.g_mlp, m.decay = (flat[:, 9248 + 8 * i:9256 + 8 * i] for i in range(3))
    m.chunk_ones, m.ada_t = flat[:, 9272:9274], flat[0:48, 9280:9408]
    m.log_decay, m.qa, m.ka, m.kb, m.qb = (kv[:, 512 * i:512 * i + 512].rearrange("p (t n) -> p t n", t=TILES) for i in range(5))
    m.qa_t, m.ka_t, m.qb_t = m.qk_a[:, 0:2, :], m.qk_a[:, 2:4, :], m.qk_a[:, 4:6, :]
    m.backward, m.gg_t = m.qk_a[:, 6, 0:P], m.qk_a[0:GATE_RANK, 7, :]
    m.inner = m.qk_b[:, 8:12, :].rearrange("p k n -> p (k n)").rearrange("p (r b n) -> p r b n", r=2, b=4)
    m.state = m.qk_b[:, 12:15, :].rearrange("p k (b n) -> p k b n", b=2)
    m.w_gate = m.qk_b[0:GATE_RANK, 15, :]
    m.row_pt = pt[:, 0:1024]
    m.gate_a = m.sg[:, :, :].rearrange("p t n -> p (t n)")
    m.shift_tmp = m.th[:, :, :].rearrange("p j (k n) -> p j k n", k=2)
    m.g_out, m.b_gate = m.kk[:, :, :].rearrange("p t n -> p (t n)"), m.lam_in[:, :]
    m.from_start, m.to_end, m.from_middle = m.upto[:, :], m.later_neg[:, :], m.diff_g[:, :]
    m.ada_row = nc.dram_tensor("ada_row", [6144], F32, kind="Internal").ap()
    m.bias_rows = nc.dram_tensor("bias_rows", [MOBA_HEADS, REL], F32, kind="Internal").ap()
    m.consts = sem("consts")
    m.arrived = [sem(f"arrived{i}") for i in range(RAW_SLOTS)]
    m.dense_done = [sem(f"dense_done{i}") for i in range(3)]
    m.aux_done = [sem(f"aux_done{i}") for i in range(AUX)]
    m.freqs, m.diffed, m.sgu_out, m.hi_ready, m.lo_ready, m.slab_used = (sem(n) for n in ("freqs", "diffed", "sgu_out", "hi_ready", "lo_ready", "slab_used"))
    m.aux_ready, m.turned_hi, m.normed, m.small_in, m.small_in2, m.small_in3 = (sem(n) for n in ("aux_ready", "turned_hi", "normed", "small_in", "small_in2", "small_in3"))
    m.small_in4, m.mem_in, m.sgu_in, m.sgu_normed, m.low_rank, m.roped = (sem(n) for n in ("small_in4", "mem_in", "sgu_in", "sgu_normed", "low_rank", "roped"))
    m.chosen, m.max_ready, m.lam_ready, m.gate_tanh, m.gated, m.mixed_up = (sem(n) for n in ("chosen", "max_ready", "lam_ready", "gate_tanh", "gated", "mixed_up"))
    m.dve_step, m.act_step, m.pool_step, m.gla_log, m.gla_scaled, m.gla_normed = (sem(n) for n in ("dve_step", "act_step", "pool_step", "gla_log", "gla_scaled", "gla_normed"))
    m.tables, m.masked, m.shifted, m.shifted_hi, m.bias_in, m.bias_rows_ready = (sem(n) for n in ("tables", "masked", "shifted", "shifted_hi", "bias_in", "bias_rows_ready"))
    m.ones_ready, m.ada_in, m.angles = (sem(n) for n in ("ones_ready", "ada_in", "angles"))
    m.squared, m.scales, m.out_ready, m.normed_act, m.h_ready, m.gates_out, m.gates_in, m.ada_used = (sem(n) for n in ("squared", "scales", "out_ready", "normed_act", "h_ready", "gates_out", "gates_in", "ada_used"))
    m.cleared = range(m.arrived[0].num, m.ada_used.num + 1)
    return m


def network(nc, depth, ins, out):
    with ExitStack() as ctx:
        ctx.enter_context(nc.allow_non_contiguous_dma(reason="gains and biases by feature, a few KB"))
        m = allocate(nc, ctx, depth)
        m.q, m.k = {}, {}
        m.lam_inits = [0.8 - 0.6 * float(np.exp(-0.3 * l)) for l in range(depth)]
        setup_block(nc, m, *[ins[n] for n in ("x", "mem", "positions", "mem_norm_g", "c_2", "rel_bias_2", "buckets")])
        nc.all_engine_barrier(sems_to_clear=m.cleared)
        with nc.Fori(0, depth) as l:
            layer_block(nc, m, l, [ins[n] for n in ("w_in", "mem_w_kv", "mla_w_uq", "mla_w_ukv", "w_branch", "w_out")],
                        [ins[n] for n in ("norm_g", "mla_q_norm_g", "mla_kv_norm_g", "diff_lambda", "diff_norm_g", "sgu_ln_g",
                                          "sgu_ln_b", "sgu_w", "sgu_b")], ins["w_ada_2"])
            nc.all_engine_barrier(sems_to_clear=m.cleared)
        m.q, m.k = {"m": m.qk_b[:, 0:4, :]}, {"m": m.qk_b[:, 4:8, :]}
        second_block(nc, m, [ins[n] for n in ("w_in_2", "w_out_2", "w_ff1_2", "w_ff2_2")],
                     [ins[n] for n in ("final_norm_g", "b_ada_2", "g_mix_2", "w_gla_gate_2", "b_gla_gate_2", "g_gla_out_2", "g_mlp_2", "g_final_2")],
                     out)


_INS = ["x", "mem", "positions", "norm_g", "w_in", "mla_q_norm_g", "mla_kv_norm_g", "mla_w_uq", "mla_w_ukv", "diff_lambda",
        "diff_norm_g", "sgu_ln_g", "sgu_ln_b", "sgu_w", "sgu_b", "mem_norm_g", "mem_w_kv", "w_branch", "w_out", "final_norm_g", "c_2",
        "w_ada_2", "b_ada_2", "g_mix_2", "w_in_2", "w_gla_gate_2", "b_gla_gate_2", "g_gla_out_2", "rel_bias_2", "w_out_2", "g_mlp_2",
        "w_ff1_2", "w_ff2_2", "g_final_2"]


def kernel(**inputs):
    import concourse.bacc as bacc
    from concourse.bass_utils import run_bass_kernel_spmd

    nc = bacc.Bacc("TRN2", target_bir_lowering=False, num_devices=1)
    arrays = {n: np.ascontiguousarray(inputs[n]) for n in _INS}
    arrays["buckets"] = bucket_rows()
    ins = {n: nc.dram_tensor(f"in_{n}_dram", a.shape, mybir.dt.from_np(a.dtype), kind="ExternalInput").ap() for n, a in arrays.items()}
    out = nc.dram_tensor("out_dram", inputs["x"].shape, F32, kind="ExternalOutput").ap()
    network(nc, inputs["norm_g"].shape[0], ins, out)
    r = run_bass_kernel_spmd(nc, [{f"in_{n}_dram": a for n, a in arrays.items()}], core_ids=[0])
    return r.results[0]["out_dram"]
```

```python
from contextlib import ExitStack

import numpy as np

import concourse.bass as bass
from concourse import mybir

F32 = mybir.dt.float32
F32R = mybir.dt.float32r
BF16 = mybir.dt.bfloat16
I32 = mybir.dt.int32
ALU = mybir.AluOpType
ACT = mybir.ActivationFunctionType
AX_X = mybir.AxisListType.X

P = 128
TILES = 2
TOK = P * TILES
BANK = 512
RAW_SLOTS = 4
SPLIT_SLOTS = 4
LEAD = 3
SLAB = 1024
AUX = 4
PEXP = 2

NAMES = ("aq", "ak", "av", "iq", "ik", "iw", "cq", "ckv", "kr", "dq", "dk", "dv", "su", "sv", "eq", "gates", "merge")
WIDTHS = (512, 64, 64, 256, 64, 4, 384, 256, 32, 512, 512, 512, 512, 512, 512, 2560, 5120)
COL = dict(zip(NAMES, np.concatenate([[0], np.cumsum(WIDTHS)[:-1]]).tolist()))
PROJ = COL["gates"]
BRANCHES = {"a": 0, "b": 1, "c": 2, "d": 3, "e": 4}
DSA_HEADS, IDX_HEADS, IDX_DIM, MLA_HEADS, NOPE, ROT = 8, 4, 64, 8, 64, 32
TOPK = TOK // 4
MAGIC = float(0x5F3759DF)
MASKED = -1.0e30
PI_BELOW = 3.1415925
TWO_PI_PARTS = (6.28125, float(np.float16(2 * np.pi - 6.28125)),
                float(2 * np.pi - 6.28125 - float(np.float16(2 * np.pi - 6.28125))))
FREQ = [float(f) for n in (16, 32) for f in np.power(np.float32(500000.0), -np.arange(0, n, 2, dtype=np.float32) / np.float32(n))]
TAKEN = -3.0e38
ADA_PARTS = 12


class Record:
    pass


class Steps:

    def __init__(self, eng, sem):
        self.eng, self.sem, self.n = eng, sem, 0

    def did(self, ins):
        self.n += 1
        return ins.then_inc(self.sem, 1)

    def settle(self):
        if self.n:
            self.eng.wait_ge(self.sem, self.n)


def rsqrt(v, st, y, x, t, scale, eps):
    st.settle()
    st.did(v.tensor_scalar(x, x, scale, eps, ALU.mult, ALU.add))
    st.settle()
    st.did(v.tensor_scalar(y.bitcast(I32), x.bitcast(I32), -0.5, MAGIC, ALU.mult, ALU.add))
    for _ in range(3):
        st.settle()
        st.did(v.scalar_tensor_tensor(t, y, -0.5, y, ALU.mult, ALU.mult))
        st.settle()
        st.did(v.tensor_tensor(t, t, x, ALU.mult))
        st.settle()
        st.did(v.scalar_tensor_tensor(y, t, 1.5, y, ALU.add, ALU.mult))


def unit(name, lhs, kc, src, n, pair=None, opens=True, closes=True):
    x = Record()
    x.name, x.lhs, x.kc, x.src, x.n, x.pair, x.opens, x.closes = name, lhs, kc, src, n, pair, opens, closes
    return x


def step(name, kind, after=(), before=None, narrow=False, j=0, kc=0, src=None, dst=None, gain=None, gain_ready=None, shift=None,
         scale=1.0, w=P, rows=P, b="", t=0, g=0, r=0, i=0, n=0, heads=()):
    s = Record()
    s.name, s.kind, s.after, s.before, s.narrow, s.j, s.kc, s.src, s.dst = name, kind, after, before, narrow, j, kc, src, dst
    s.gain, s.gain_ready, s.shift, s.scale, s.w, s.rows, s.b, s.t, s.g = gain, gain_ready, shift, scale, w, rows, b, t, g
    s.r, s.i, s.n, s.heads = r, i, n, heads
    return s


HAS_BANK = {"split", "turn", "score", "probs", "value", "sgu_w", "sgu_z", "dots",
            "shifted", "turn_gg", "gla_z", "gla_sum", "gla_decay", "inner", "state", "gla_o",
            "ada_sum", "ada_rows"}


class Plan:

    def __init__(self, units, steps, rate=1, ahead=0):
        self.units, self.slabs, self.order, self.ahead = units, [], [], ahead
        begin, placed, at, load, closed = {}, {"start": 0}, {}, {}, {}
        pairs = 0
        for x in units:
            if x.pair is None:
                x.pair, pairs = pairs % 2, pairs + 1
            x.turn = closed.get(x.pair, 0)
            closed[x.pair] = x.turn + x.closes
            begin[x.name] = len(self.slabs)
            per = max(1, SLAB // x.n)
            for k0 in range(0, x.kc, per):
                kn = min(per, x.kc - k0)
                slab = Record()
                slab.i, slab.unit, slab.k0, slab.kn = len(self.slabs), x, k0, kn
                slab.first, slab.last = k0 == 0, k0 + kn == x.kc
                self.slabs.append(slab)
            placed[x.name] = len(self.slabs)
        for s in steps:
            lo = max([placed[a] + gap for a, gap in s.after], default=0)
            end = begin[s.before] if s.before else len(self.slabs)
            n = lo
            if s.kind in HAS_BANK and s.kind != "ada_sum" and s.before is None:
                while load.get(n, 0) >= rate and n < len(self.slabs):
                    n += 1
                load[n] = load.get(n, 0) + 1
            assert n <= end, (s.name, lo, end)
            placed[s.name] = n
            at.setdefault(n, []).append(s)
        for n in range(len(self.slabs) + 1):
            if n:
                self.order.append(("slab", self.slabs[n - 1]))
                if self.slabs[n - 1].last:
                    self.order.append(("evac", self.slabs[n - 1].unit))
            self.order += [(s.kind, s) for s in at.get(n, [])]
        self.bank, self.seq, count, uses = {}, {}, {}, [0] * AUX
        narrow = 0
        for kind, s in self.order:
            if kind in ("slab", "evac"):
                continue
            if kind in HAS_BANK:
                if s.narrow:
                    b, narrow = 2 + narrow % 2, narrow + 1
                else:
                    b = len(self.bank) % AUX
                use = Record()
                use.n, use.bank, use.turn = len(self.bank), b, uses[b]
                self.bank[s.name] = use
                uses[b] += 1
            self.seq[s.name] = count.get(kind, 0)
            count[kind] = count.get(kind, 0) + 1
        self.unit = {x.name: x for x in units}
        self.last_slab = {s.unit.name: s.i for s in self.slabs if s.last}


def load_slab(m, sp, plan, s):
    if s.i < plan.ahead:
        return
    if s.i >= RAW_SLOTS:
        sp.wait_ge(m.lo_ready, s.i - RAW_SLOTS + 1)
    n = s.unit.n
    sp.dma_start(m.raw[:, s.i % RAW_SLOTS, 0:s.kn * n].rearrange("p (k n) -> p k n", n=n), s.unit.src(s.k0, s.kn))\
      .then_inc(m.arrived[s.i % RAW_SLOTS], 16)


def load_ahead(m, sp, w, free):
    for i in range(RAW_SLOTS):
        free(i)
        sp.dma_start(m.raw[:, i, :].rearrange("p (k n) -> p k n", n=512),
                     w[2 * i * P:2 * (i + 1) * P, 0:512].rearrange("(k p) n -> p k n", p=P)).then_inc(m.ahead_in, 16)
    sp.wait_ge(m.ahead_in, 16 * RAW_SLOTS)


def split_high(m, act, plan, s):
    w = s.kn * s.unit.n
    if s.i >= plan.ahead:
        act.wait_ge(m.arrived[s.i % RAW_SLOTS], 16 * ((s.i - plan.ahead) // RAW_SLOTS + 1))
    if s.i >= SPLIT_SLOTS:
        act.wait_ge(m.slab_used, s.i - SPLIT_SLOTS + 1)
    act.activation(m.wh[:, s.i % SPLIT_SLOTS, 0:w], m.raw[:, s.i % RAW_SLOTS, 0:w], ACT.Copy).then_inc(m.hi_ready, 1)


def split_low(m, dve, s):
    w = s.kn * s.unit.n
    dve.wait_ge(m.hi_ready, s.i + 1)
    dve.tensor_tensor(m.wl[:, s.i % SPLIT_SLOTS, 0:w], m.raw[:, s.i % RAW_SLOTS, 0:w],
                      m.wh[:, s.i % SPLIT_SLOTS, 0:w].bitcast(F32), ALU.subtract).then_inc(m.lo_ready, 1)


def multiply(m, pe, plan, s, ready):
    x = s.unit
    if s.first:
        if x.opens and x.turn:
            pe.wait_ge(m.dense_done[x.pair], x.turn)
    for r in ready:
        pe.wait_ge(*r)
    pe.wait_ge(m.lo_ready, s.i + 1)
    hi, lo = m.lhs[x.lhs]
    for t in range(TILES):
        out = m.pairs[x.pair][:, t, 0:x.n]
        for k in range(s.kn):
            tok = slice(t * P, t * P + P)
            wh = m.wh[:, s.i % SPLIT_SLOTS, k * x.n:(k + 1) * x.n]
            wl = m.wl[:, s.i % SPLIT_SLOTS, k * x.n:(k + 1) * x.n]
            pe.matmul(out, hi[:, s.k0 + k, tok], wh, start=x.opens and s.first and k == 0, stop=False)
            pe.matmul(out, hi[:, s.k0 + k, tok], wl, start=False, stop=False)
            last = pe.matmul(out, lo[:, s.k0 + k, tok], wh, start=False, stop=x.closes and s.last and k == s.kn - 1)
    last.then_inc(m.slab_used, 1)


def multiply_turned(m, pe, plan, s, ready):
    x = s.unit
    if s.first and x.turn:
        pe.wait_ge(m.dense_done[x.pair], x.turn)
    for r in ready:
        pe.wait_ge(*r)
    pe.wait_ge(m.lo_ready, s.i + 1)
    hi, lo = m.lhs[x.lhs]
    for b in range(4):
        out = m.pairs[x.pair][:, b // 2, b % 2 * TOK:(b % 2 + 1) * TOK]
        for k in range(s.kn):
            cols = slice(k * x.n + b * P, k * x.n + (b + 1) * P)
            wh, wl = m.wh[:, s.i % SPLIT_SLOTS, cols], m.wl[:, s.i % SPLIT_SLOTS, cols]
            end = s.last and k == s.kn - 1
            pe.matmul(out, wh, hi[:, s.k0 + k, :], start=s.first and k == 0 and b % 2 == 0, stop=False, skip_group_check=True)
            pe.matmul(out, wh, lo[:, s.k0 + k, :], start=False, stop=False, skip_group_check=True)
            last = pe.matmul(out, wl, hi[:, s.k0 + k, :], start=False, stop=end, skip_group_check=True)
    last.then_inc(m.slab_used, 1)


def take_bank(m, pe, k):
    if k.turn:
        pe.wait_ge(m.aux_done[k.bank], k.turn)


def aux_is_done(m, plan, name):
    k = plan.bank[name]
    return m.aux_done[k.bank], k.turn + 1


def unit_is_done(m, plan, name):
    x = plan.unit[name]
    return m.dense_done[x.pair], x.turn + 1


def turn_blocks(m, pe, k, blocks, ready):
    take_bank(m, pe, k)
    for r in ready:
        pe.wait_ge(*r)
    for i, src in enumerate(blocks):
        last = pe.transpose(m.aux[0:src.shape[-1], k.bank, i * P:(i + 1) * P], src, m.ident[:, :])
    last.then_inc(m.aux_ready, 1)


def split_cols(s, m):
    return 2 * s.j, min(2, s.kc - 2 * s.j)


def split_blocks(s, m):
    k0, kn = split_cols(s, m)
    return [s.src(t)[:, (k0 + i) * P:(k0 + i + 1) * P] for i in range(kn) for t in range(TILES)]


def split_hi(m, act, plan, s):
    k, (k0, kn) = plan.bank[s.name], split_cols(s, m)
    hi = m.lhs[s.dst][0]
    act.wait_ge(m.aux_ready, k.n + 1)
    if s.gain is None:
        last = act.activation(hi[:, k0:k0 + kn, :], m.aux[:, k.bank, 0:kn * TOK].rearrange("p (k n) -> p k n", n=TOK), ACT.Copy)
    else:
        if s.gain_ready:
            act.wait_ge(*s.gain_ready)
        for i in range(kn):
            last = act.activation(hi[:, k0 + i, :], m.aux[:, k.bank, i * TOK:(i + 1) * TOK], ACT.Copy,
                                  scale=s.gain[:, k0 + i:k0 + i + 1])
    last.then_inc(m.turned_hi, 1)


def split_lo(m, dve, plan, s):
    k, (k0, kn) = plan.bank[s.name], split_cols(s, m)
    hi, lo = m.lhs[s.dst]
    dve.wait_ge(m.turned_hi, plan.seq[s.name] + 1)
    if s.gain is None:
        last = dve.tensor_tensor(lo[:, k0:k0 + kn, :], m.aux[:, k.bank, 0:kn * TOK].rearrange("p (k n) -> p k n", n=TOK),
                                 hi[:, k0:k0 + kn, :].bitcast(F32), ALU.subtract)
    else:
        for i in range(kn):
            last = dve.scalar_tensor_tensor(lo[:, k0 + i, :], m.aux[:, k.bank, i * TOK:(i + 1) * TOK],
                                            s.gain[:, k0 + i:k0 + i + 1], hi[:, k0 + i, :].bitcast(F32),
                                            ALU.mult, ALU.subtract)
    last.then_inc(m.aux_done[k.bank], 1)


def mean_square(dve, st, stats, out, src, width):
    n = -(-width // BANK)
    w = width // n
    for t in range(TILES):
        for c in range(n):
            st.did(dve.bn_stats(stats[:, t, c, :], src(t)[:, c * w:(c + 1) * w]))
    st.settle()
    for t in range(TILES):
        st.did(dve.bn_aggr(stats[:, t, 2, 0:2], stats[:, t, 0:n, :]))
    st.settle()
    mean = stats[:, :, 2, 0]
    st.did(dve.tensor_tensor(out, mean, mean, ALU.mult))
    st.settle()
    st.did(dve.tensor_tensor(out, out, stats[:, :, 2, 1], ALU.add))


def norm_stats(m, dve, st, col, after=None):
    st.settle()
    for c in range(2):
        st.did(dve.bn_stats(m.stats[:, 0, c, :], m.h[:, 0, c * BANK:(c + 1) * BANK]))
    st.settle()
    st.did(dve.bn_aggr(m.stats[:, 0, 2, 0:2], m.stats[:, 0, 0:2, :]))
    st.settle()
    mean = m.stats[:, 0, 2, 0:1]
    st.did(dve.scalar_tensor_tensor(m.ms[:, col:col + 1], mean, mean, m.stats[:, 0, 2, 1:2], ALU.mult, ALU.add))
    dve.wait_ge(*after)
    rsqrt(dve, st, m.rs[:, col:col + 2], m.ms[:, col:col + 2], m.nt[:, col:col + 2], 1.0, 1e-6)
    st.settle()


def square_tile(m, act, col):
    act.activation(m.mixed[:, 1, :], m.h[:, 1, :], ACT.Square, scale=1.0 / 32, accum_out=m.ms[:, col + 1:col + 2])\
       .then_inc(m.squared, 1)


def setup_block(nc, m, x, mem, positions, mem_norm_g, c, rel_bias, buckets, mem_w_kv):
    def mem_src(t):
        return m.mixed[:, t, :]

    steps = [step(f"mem{j}", "split", j=j, kc=8, src=mem_src, dst="mem", gain=m.gain, gain_ready=(m.small_in, 32)) for j in range(4)]
    plan = Plan([], steps)
    with nc.Block() as block:
        @block.sync
        def _(sp):
            sp.dma_start(m.pos_i[:, :], positions.rearrange("o (t p) -> p (o t)", p=P)).then_inc(m.pos_in, 16)
            sp.dma_start(m.mixed[:, :, :], mem[0].rearrange("(t p) d -> p t d", p=P)).then_inc(m.mem_in, 16)
            sp.dma_start(m.h[:, :, :], x[0].rearrange("(t p) d -> p t d", p=P)).then_inc(m.small_in, 16)
            sp.dma_start(m.gain[:, :], mem_norm_g.rearrange("(k p) -> p k", p=P)).then_inc(m.small_in, 16)
            sp.dma_start(m.c_col, c[0].rearrange("(k p) -> p k", p=P)).then_inc(m.small_in2, 16)
            sp.dma_start(m.buckets, buckets).then_inc(m.small_in4, 16)
            sp.dma_start(m.rel_bias[0:REL_BUCKETS, :], rel_bias).then_inc(m.small_in4, 16)
            load_ahead(m, sp, mem_w_kv[0], lambda i: None)
            sp.wait_ge(m.bias_rows_ready, 1)
            sp.dma_start(m.bias_rows, m.bias_out).then_inc(m.bias_in, 16)
            sp.wait_ge(m.small_in, 32)
            sp.wait_ge(m.pos_in, 16)
            sp.wait_ge(m.bias_in, 16)

        @block.gpsimd
        def _(pool):
            st = Steps(pool, m.pool_step)
            for i, f in enumerate(FREQ):
                pool.memset(m.freq[:, i:i + 1], f).then_inc(m.freqs, 1)
            st.did(pool.memset(m.ident[:, :], 0.0))
            st.did(pool.memset(m.neg_ident[:, :], 0.0))
            st.did(pool.memset(m.later[:, :], 0.0))
            st.did(pool.memset(m.later_neg[:, :], 0.0))
            st.did(pool.memset(m.upto[:, :], 1.0))
            st.settle()
            pool.affine_select(out=m.ident[:, :], in_=m.ident[:, :], compare_op=ALU.not_equal, fill=1.0, base=0,
                               pattern=[[-1, P]], channel_multiplier=1).then_inc(m.consts, 1)
            st.did(pool.affine_select(out=m.neg_ident[:, :], in_=m.neg_ident[:, :], compare_op=ALU.not_equal, fill=MASKED, base=0,
                               pattern=[[-1, P]], channel_multiplier=1))
            st.did(pool.affine_select(out=m.later[:, P:TOK], in_=m.later[:, P:TOK], compare_op=ALU.is_ge, fill=1.0, base=0,
                               pattern=[[-1, P]], channel_multiplier=1))
            st.did(pool.affine_select(out=m.later_neg[:, :], in_=m.later_neg[:, :], compare_op=ALU.is_ge, fill=MASKED, base=0,
                               pattern=[[-1, P]], channel_multiplier=1))
            st.did(pool.affine_select(out=m.upto[:, :], in_=m.upto[:, :], compare_op=ALU.is_ge, fill=0.0, base=0,
                               pattern=[[1, P]], channel_multiplier=-1))
            pool.wait_ge(m.pos_in, 16)
            pool.wait_ge(m.freqs, len(FREQ))
            st.did(pool.tensor_copy(m.pos[:, :], m.pos_i[:, :]))
            st.settle()
            for t in range(TILES):
                st.did(pool.tensor_scalar(m.angle[:, t, :], m.freq[:, :], m.pos[:, t:t + 1], None, ALU.mult))
            st.settle()
            a, k = m.angle[:, :, :], m.turns[:, :, :]
            big = 1.5 * 2.0 ** 23
            for out, quarter in ((m.sin_in, 0.0), (m.cos_in, 0.25)):
                st.did(pool.tensor_scalar(k, a, float(1.0 / (2 * np.pi)), quarter, ALU.mult, ALU.add))
                st.settle()
                st.did(pool.tensor_scalar(k, k, big, None, ALU.add))
                st.settle()
                st.did(pool.tensor_scalar(k, k, big, None, ALU.subtract))
                st.settle()
                src = a
                for part in TWO_PI_PARTS:
                    st.did(pool.tensor_scalar(m.product[:, :, :], k, -part, None, ALU.mult))
                    st.settle()
                    st.did(pool.tensor_tensor(out[:, :, :], m.product[:, :, :], src, ALU.add))
                    st.settle()
                    src = out[:, :, :]
                if quarter:
                    st.did(pool.tensor_scalar(out[:, :, :], out[:, :, :], float(np.pi / 2), None, ALU.add))
                    st.settle()
                for op, turn in ((ALU.is_gt, -1.0), (ALU.is_lt, 1.0)):
                    st.did(pool.tensor_scalar(k, out[:, :, :], -turn * PI_BELOW, turn * float(np.float32(2 * np.pi)), op, ALU.mult))
                    st.settle()
                    st.did(pool.tensor_tensor(out[:, :, :], out[:, :, :], k, ALU.add))
                    st.settle()
                pool.tensor_scalar(out[:, :, :], out[:, :, :], PI_BELOW, -PI_BELOW, ALU.min, ALU.max).then_inc(m.angles, 1)

        @block.vector
        def _(dve):
            st = Steps(dve, m.dve_step)
            for l, v in enumerate(m.lam_inits):
                st.did(dve.memset(m.lam_init[:, l:l + 1], v))
                st.did(dve.memset(m.one_less_lam[:, l:l + 1], 1.0 - v))
            dve.memset(m.rel_bias[REL_BUCKETS:REL_BUCKETS + 1, :], 1.0).then_inc(m.ones_ready, 1)
            dve.wait_ge(m.gate_tanh, 1)
            st.did(dve.scalar_tensor_tensor(m.c_tanh, m.c_tanh, 1.0, m.c_col, ALU.add, ALU.mult))
            st.settle()
            st.did(dve.tensor_scalar(m.c_silu[:, :], m.c_tanh, 0.5, None, ALU.mult))
            st.did(dve.memset(m.ones_col[:, :], 1.0))
            for _, s in plan.order:
                split_lo(m, dve, plan, s)
            dve.wait_ge(m.squared, TILES)
            rsqrt(dve, st, m.mem_rs[:, :], m.ms[:, 0:2], m.nt[:, 0:2], 1.0, 1e-6)

        @block.scalar
        def _(act):
            act.wait_ge(m.small_in2, 16)
            act.activation(m.c_tanh, m.c_col, ACT.Tanh, scale=0.5).then_inc(m.gate_tanh, 1)
            for _, s in plan.order:
                split_hi(m, act, plan, s)
            act.wait_ge(m.aux_ready, 5)
            act.activation(m.bias_out, m.aux[0:MOBA_HEADS, 0, 0:REL], ACT.Copy).then_inc(m.bias_rows_ready, 1)
            for t in range(TILES):
                act.activation(m.square_scratch[:, t, :], mem_src(t), ACT.Square, scale=1.0 / 32, accum_out=m.ms[:, t:t + 1])\
                   .then_inc(m.squared, 1)
            act.wait_ge(m.angles, 2)
            n0, n1 = 8, 16
            for (c, s_, lo, n) in ((m.cos_p, m.sin_p, 0, n0), (m.cos_m, m.sin_m, n0, n1)):
                for half in range(2):
                    act.activation(c[:, :, half * n:half * n + n], m.cos_in[:, :, lo:lo + n], ACT.Sin)
                    act.activation(s_[:, :, half * n:half * n + n], m.sin_in[:, :, lo:lo + n], ACT.Sin,
                                   scale=-1.0 if half == 0 else 1.0)

        @block.tensor
        def _(pe):
            pe.wait_ge(m.consts, 1)
            for _, s in plan.order:
                turn_blocks(m, pe, plan.bank[s.name], split_blocks(s, m), [(m.mem_in, 16)])
            pe.wait_ge(*aux_is_done(m, plan, "mem0"))
            pe.wait_ge(m.small_in4, 32)
            pe.wait_ge(m.ones_ready, 1)
            pe.matmul(m.aux[0:MOBA_HEADS, 0, 0:REL], m.rel_bias, m.buckets, start=True, stop=True).then_inc(m.aux_ready, 1)


def layer_units(m, l, w_in, mem_w_kv, mla_w_uq, mla_w_ukv, w_branch, w_out):
    def part(w, col, n):
        return lambda k0, kn: w[k0 * P:(k0 + kn) * P, col:col + n].rearrange("(k p) n -> p k n", p=P)

    def inw(name, col, n):
        return unit(name, "x", 8, part(w_in[l], col, n), n)

    us = [unit("memk", "mem", 8, part(mem_w_kv[l], 0, 512), 512), unit("memv", "mem", 8, part(mem_w_kv[l], 512, 512), 512)]
    us += [inw("u_" + n, COL[n], 512) for n in ("sv", "su", "eq", "dq", "dk", "dv")]
    us += [inw("u_p0", 0, 512), inw("u_p1", 512, 512), inw("u_p2", 1024, 512), inw("u_p3", 1536, 100)]

    def branch(b):
        n = BRANCHES[b]
        out = [inw("gate_" + b, COL["gates"] + 512 * n, 512)]
        for j in range(2):
            out += [inw(f"merge_{b}{j}", COL["merge"] + 1024 * n + 512 * j, 512),
                    unit(f"out_{b}{j}", "og", 4, part(w_branch[l, n], 512 * j, 512), 512)]
        return out

    gate_c, *rest_c = branch("c")
    us += branch("e") + branch("d")
    us += [unit("uq0", "qn", 3, part(mla_w_uq[l], 0, 512), 512), unit("uq1", "qn", 3, part(mla_w_uq[l], 512, 256), 256)]
    us += [gate_c]
    us += [unit(f"ukv{j}", "kvn", 2, part(mla_w_ukv[l], 512 * j, 512), 512) for j in range(2)]
    us += rest_c + branch("a") + branch("b")
    us += [unit(f"res{j}", "mx", 8, part(w_out[l], 512 * j, 512), 512) for j in range(2)]
    return us


def groups(b, t):
    order = [0, 2, 4, 6, 1, 3, 5, 7] if b in "acm" else list(range(4 if b == "e" else 8))
    per = 4 if (t == 0 and b != "e") else 2
    return [order[i:i + per] for i in range(0, len(order), per)]


def attention_steps(b, first, gap, values=()):
    out, prev = [], None
    for t in range(TILES):
        gs = groups(b, t)
        for i, hs in enumerate(gs):
            out.append(step(f"s_{b}{t}{i}", "score", after=first(t), b=b, t=t, heads=hs))
            if i >= 1:
                out.append(step(f"p_{b}{t}{i - 1}", "probs", after=[(f"s_{b}{t}{i - 1}", gap)], b=b, t=t, heads=gs[i - 1]))
        n = len(gs) - 1
        out.append(step(f"p_{b}{t}{n}", "probs", after=[(f"s_{b}{t}{n}", gap)], b=b, t=t, heads=gs[n]))
        for g in range(2 if b == "c" else 1):
            heads = list(range(4 * g, 4 * g + 4)) if b == "c" else sorted(h for hs in gs for h in hs)
            out.append(step(f"v_{b}{t}{g}", "value", after=[(f"p_{b}{t}{n}", 1), *values], b=b, t=t, heads=heads, g=g))
    return out


def layer_steps(m):
    def region(name, n=512):
        return lambda t: m.proj[:, t, COL[name]:COL[name] + n]

    def split(name, kc, src, dst, after, before, gain=None, gain_ready=None):
        return [step(f"{name}{j}", "split", after=after, before=before, j=j, kc=kc, src=src, dst=dst, gain=gain,
                     gain_ready=gain_ready) for j in range(-(-kc // 2))]

    def turn(name, n, src, w, dst, rows, after, scale=1.0):
        return [step(f"{name}{j}", "turn", after=after, j=j, src=src, w=w, dst=dst, rows=rows, scale=scale)
                for j in range(n // 2)]

    A, B = m.qk_a, m.qk_b
    m.q = {"e": A[:, 0:4, :], "a": A[:, 0:4, :], "c": B[:, 0:4, :], "b": B[0:96, 0:8, :]}
    m.k = {"e": A[:, 4:8, :], "a": A[:, 4:6, :], "c": B[:, 4:8, :], "b": B[0:96, 8:16, :]}
    m.iq = A[:, 6:8, :]
    s = [step("norm_x", "norm_x", after=[("start", 1)])]
    s += [step(f"sgu_w{j}", "sgu_w", after=[("norm_x", 6 + j)], j=j) for j in range(2)]
    s += split("x", 8, lambda t: m.mixed[:, t, :], "x", [("norm_x", 3)], "u_sv", m.gain, (m.small_in, 16))
    s += turn("memk", 4, lambda t: m.memk[:, t, :], P, m.k["e"], P, [("memk", 1), ("x3", 0)])
    s += [step(f"sgu_norm{i}", "sgu_norm", after=[("u_sv", i)], i=i) for i in range(3)]
    s += [step(f"sgu_z{t}", "sgu_z", after=[("u_su", 1)], t=t) for t in range(TILES)]
    s += turn("eq", 4, region("eq"), P, m.q["e"], P, [("u_eq", 1)], scale=float(P) ** -0.5)
    s += attention_steps("e", lambda t: [("eq1", 1)], 2)
    s += [step("rope_d", "rope", after=[("u_dk", 0)])]
    s += turn("dq", 4, region("dq"), P, m.q["c"], P, [("u_dk", 3)], scale=0.125)
    s += turn("dk", 4, region("dk"), P, m.k["c"], P, [("u_dk", 3)])
    s += attention_steps("c", lambda t: [("dk1", 1), ("u_dv", 1), ("v_e10", 0)], 2)
    s += [step(f"diff_mix{i}", "diff_mix", after=[("v_c11", i)], i=i) for i in range(3)]
    s += [step("rope_a", "rope", after=[("u_p1", 0)])]
    s += turn("aq", 4, region("aq"), P, m.q["a"], P, [("u_p1", 3), ("v_e10", 0)], scale=0.125)
    s += turn("kk", 2, lambda t: m.kk[:, t, :], P, m.k["a"], P, [("u_p1", 3), ("v_e10", 0)])
    s += turn("iq", 2, region("iq", 256), P, m.iq, P, [("u_p1", 3), ("v_e10", 0)])
    s += [step(f"dots{2 * t + i}", "dots", after=[("iq0", 1)], t=t, heads=[i, i + 2]) for t in range(TILES) for i in range(2)]
    s += [step(f"top{t}{i}", "topk", after=[(f"dots{2 * t + 1}", 1)] + ([(f"top0{TOPK // 16 - 1}", 1)] if t else []) +
               ([(f"top{t}{i - 1}", 2)] if i else []), t=t, i=i) for t in range(TILES) for i in range(TOPK // 16)]
    s += [step("low_rank", "low_rank", after=[("u_p3", 0)])]
    s += split("qn", 3, region("cq", 384), "qn", [("low_rank", 2), ("out_d1", 0)], "uq0", m.qgain, (m.small_in2, 32))
    s += split("kvn", 2, region("ckv", 256), "kvn", [("low_rank", 2), ("uq1", 0)], "ukv0", m.kvgain, (m.small_in2, 32))
    s += attention_steps("a", lambda t: [(f"top1{TOPK // 16 - 1}", 1), ("v_c11", 0)], 2)
    s += [step("rope_b", "rope", after=[("ukv1", 0)])]
    s += turn("bq", 8, lambda t: m.proj[:, t, COL["su"]:COL["su"] + 768], 96, m.q["b"], 96,
              [("ukv1", 3), ("diff_mix2", 0)], scale=96.0 ** -0.5)
    s += turn("bk", 8, lambda t: m.kfull[:, t, :], 96, m.k["b"], 96, [("ukv1", 3), ("diff_mix2", 0)])
    s += attention_steps("b", lambda t: [("bk3", 1)], 2)
    for b in "edcab":
        s += [step("mix_" + b, "gate", after=[("gate_" + b, 0)], b=b)]
        s += split("og_" + b, 4, lambda t: m.th[:, t, :], "og", [("mix_" + b, 2)] + ([("ukv1", 0)] if b == "c" else []), f"out_{b}0")
    s += split("mx", 8, lambda t: m.mixed[:, t, :], "mx", [("out_b1", 0)], "res0")
    for i in range(8 * m.ada_parts):
        s.append(step(f"ada{i}", "ada", after=[("start", 2 * i + 2)], i=i))
        if i % 8 == 7:
            s.append(step(f"ada_sum{i // 8}", "ada_sum", after=[("start", 2 * i + 6)], i=i // 8))
    return s


class Attention:

    def __init__(self, plan):
        steps = [s for k, s in plan.order if k == "score"]
        self.number = {s.name: i for i, s in enumerate(steps)}
        self.steps = steps
        self.score_of = {(s.b, s.t, s.heads[0]): s for s in steps}
        self.probs_of = {(s.b, s.t, s.heads[0]): s for k, s in plan.order if k == "probs"}

    def width(self, s):
        return TOK if s.b == "e" or s.t == 1 else P


def turn_probs(m, pe, plan, att, s):
    score = att.score_of[s.b, s.t, s.heads[0]]
    e = m.pexp[:, att.number[score.name] % PEXP, :]
    turn_blocks(m, pe, plan.bank[s.name], [e[:, i * P:(i + 1) * P] for i in range(4)], [aux_is_done(m, plan, score.name)])


def maxima(m, dve, plan, att, s):
    k, w, n = plan.bank[s.name], att.width(s), att.number[s.name]
    dve.wait_ge(m.aux_ready, k.n + 1)
    dve.tensor_reduce(m.neg_max[:, 4 * n:4 * n + len(s.heads)], m.aux[:, k.bank, :].rearrange("p (h n) -> p h n", n=w), AX_X,
                      ALU.max, negate=True).then_inc(m.max_ready, 1)


def exponentials(m, act, plan, att, s):
    k, w, n = plan.bank[s.name], att.width(s), att.number[s.name]
    if n >= PEXP:
        old = att.steps[n - PEXP]
        act.wait_ge(m.aux_ready, plan.bank[att.probs_of[old.b, old.t, old.heads[0]].name].n + 1)
    act.wait_ge(m.max_ready, n + 1)
    for i, h in enumerate(s.heads):
        last = act.activation(m.pexp[:, n % PEXP, i * w:(i + 1) * w], m.aux[:, k.bank, i * w:(i + 1) * w], ACT.Exp,
                              bias=m.neg_max[:, 4 * n + i:4 * n + i + 1], accum_out=m.sums[s.b][:, s.t, h:h + 1])
    last.then_inc(m.aux_done[k.bank], 1)


def keep_probs(m, act, plan, s):
    k = plan.bank[s.name]
    act.wait_ge(m.aux_ready, k.n + 1)
    c = 4 // len(s.heads)
    hs = slice(s.heads[0], s.heads[-1] + 1, s.heads[1] - s.heads[0])
    act.activation(m.pt[:, hs, 0:c, :], m.aux[:, k.bank, :].rearrange("p (h c n) -> p h c n", c=c, n=P),
                   ACT.Copy).then_inc(m.aux_done[k.bank], 1)


def inverse_sums(m, dve, st, plan, att, s):
    n = len(s.heads)
    inv = m.inv[:, s.t, 0:n]
    for hs in groups(s.b, s.t):
        dve.wait_ge(*aux_is_done(m, plan, att.score_of[s.b, s.t, hs[0]].name))
    st.settle()
    st.did(dve.reciprocal(inv, m.sums[s.b][:, s.t, s.heads[0]:s.heads[0] + n]))
    st.settle()
    return inv


def layer_block(nc, m, l, weights, small, w_ada, mem_w_next, final_norm_g):
    (norm_g, mla_q_norm_g, mla_kv_norm_g, diff_lambda, diff_norm_g, sgu_ln_g, sgu_ln_b, sgu_w, sgu_b) = small
    plan = Plan(layer_units(m, l, *weights), layer_steps(m), rate=1, ahead=RAW_SLOTS)
    ROPES = {"rope_d": 1, "rope_a": 2, "rope_b": 3}
    ropes_done = {r: plan.seq[r] + 1 for r in ROPES}
    att = Attention(plan)
    gates = {s.b: plan.seq[s.name] for k, s in plan.order if k == "gate"}
    merges = [x.name for k, x in plan.order if k == "evac" and x.name.startswith("merge")]
    outs = [x.name for k, x in plan.order if k == "evac" and x.name.startswith("out")]
    DIM = {"a": 64, "b": 64, "c": 128, "e": 128}
    OUT = {"a": "aq", "b": "cq", "c": "dq", "d": "su", "e": "eq"}

    seen = []

    def lhs_ready(s):
        x = s.unit
        if x.lhs == "mem":
            return []
        name = f"og_{x.name[4]}" if x.lhs == "og" else x.lhs
        names = [f"{name}{j}" for j in range(s.k0 // 2, (s.k0 + s.kn - 1) // 2 + 1)]
        out = [aux_is_done(m, plan, n) for n in names if n not in seen]
        seen.extend(names)
        return out

    def keys(b, h, w):
        if b == "a":
            return m.k["a"][64 * (h % 2):64 * (h % 2) + 64, 0, 0:w]
        if b == "c":
            return m.k["c"][64 * (h % 2):64 * (h % 2) + 64, h // 2, 0:w]
        return m.k[b][:, h, 0:w]

    def queries(b, h, t):
        if b in "ac":
            return m.q[b][64 * (h % 2):64 * (h % 2) + 64, h // 2, t * P:(t + 1) * P]
        return m.q[b][:, h, t * P:(t + 1) * P]

    def values(b, h, c):
        if b == "a":
            return m.proj[:, c, COL["av"]:COL["av"] + 64]
        if b == "c":
            return m.proj[:, c, COL["dv"] + 128 * (h // 2):COL["dv"] + 128 * (h // 2) + 128]
        if b == "b":
            return m.vb[:, c, 64 * h:64 * h + 64]
        return m.memv[:, c, 128 * h:128 * h + 128]

    with nc.Block() as block:
        @block.sync
        def _(sp):
            sp.dma_start(m.gain[:, :], norm_g[l].rearrange("(k p) -> p k", p=P)).then_inc(m.small_in, 16)
            parts = w_ada[0].rearrange("k (l n) -> l k n", l=m.depth)[l]
            for s in plan.slabs:
                load_slab(m, sp, plan, s)
                i = (s.i - 8) // 2
                if s.i % 2 == 0 and 0 <= i < 8 * m.ada_parts:
                    if i:
                        sp.wait_ge(m.ada_used, i)
                    sp.dma_start(m.ada_w[:, :], parts[P * (i % 8):P * (i % 8) + P, 512 * (i // 8):512 * (i // 8) + 512])\
                      .then_inc(m.ada_in, 16)
            sp.wait_ge(m.aux_ready, plan.bank["v_b10"].n + 1)
            sp.dma_start(m.row_pt, final_norm_g.partition_broadcast(P)).then_inc(m.row_in, 16)
            sp.wait_ge(m.row_in, 16)
            n = len(plan.slabs)
            load_ahead(m, sp, mem_w_next[l], lambda i: sp.wait_ge(m.lo_ready, n - (n - 1 - i) % RAW_SLOTS))

        @block.tensor
        def _(pe):
            pe.wait_ge(m.consts, 1)
            for kind, s in plan.order:
                if kind == "slab":
                    multiply(m, pe, plan, s, lhs_ready(s))
                elif kind == "ada_sum":
                    k = plan.bank[s.name]
                    take_bank(m, pe, k)
                    pe.wait_ge(m.ada_used, 8 * s.i + 8)
                    for i in range(4):
                        last = pe.matmul(m.aux[:, k.bank, i:i + 1], m.ada_acc[:, i * P:(i + 1) * P], m.ones_col[:, :],
                                         start=True, stop=True)
                    last.then_inc(m.aux_ready, 1)
                elif kind == "split":
                    src_ready = {"x": [(m.normed, 1)], "q": [(m.low_rank, 1)], "k": [(m.low_rank, 1)],
                                 "m": [(m.mixed_up, len(outs) - (s.j < 2))],
                                 "o": [(m.gated, gates[s.name[3]] + 1 if s.name[0] == "o" else 0)]}[s.name[0]]
                    turn_blocks(m, pe, plan.bank[s.name], split_blocks(s, m), src_ready)
                elif kind == "turn":
                    ready = {"memk": [unit_is_done(m, plan, "memk")], "eq": [unit_is_done(m, plan, "u_eq")],
                             "dq": [(m.roped, ropes_done["rope_d"])], "dk": [(m.roped, ropes_done["rope_d"])],
                             "aq": [(m.roped, ropes_done["rope_a"])], "kk": [(m.roped, ropes_done["rope_a"])],
                             "iq": [(m.roped, ropes_done["rope_a"])],
                             "bq": [(m.roped, ropes_done["rope_b"])], "bk": [(m.roped, ropes_done["rope_b"])]}[s.name[:-1]]
                    blocks = [s.src(t)[:, (2 * s.j + i) * s.w:(2 * s.j + i + 1) * s.w] for i in range(2) for t in range(TILES)]
                    turn_blocks(m, pe, plan.bank[s.name], blocks, ready)
                elif kind == "sgu_w":
                    turn_blocks(m, pe, plan.bank[s.name], [m.sgu_raw[:, 4 * s.j + i, :] for i in range(4)], [(m.sgu_in, 16)])
                elif kind == "sgu_z":
                    k = plan.bank[s.name]
                    take_bank(m, pe, k)
                    pe.wait_ge(*aux_is_done(m, plan, "sgu_w0"))
                    pe.wait_ge(*aux_is_done(m, plan, "sgu_w1"))
                    pe.wait_ge(m.sgu_normed, 1)
                    for g in range(8):
                        c = COL["sv"] + 64 * g
                        last = pe.matmul(m.aux[:, k.bank, 64 * g:64 * g + 64], m.sgu_t[:, g, :], m.proj[:, s.t, c:c + 64],
                                         start=True, stop=True)
                    last.then_inc(m.aux_ready, 1)
                elif kind == "dots":
                    k, w = plan.bank[s.name], P if s.t == 0 else TOK
                    take_bank(m, pe, k)
                    for need in ("iq0", "kk0"):
                        pe.wait_ge(*aux_is_done(m, plan, need))
                    for i, h in enumerate(s.heads):
                        rows = slice(64 * (h % 2), 64 * (h % 2) + 64)
                        last = pe.matmul(m.aux[:, k.bank, i * w:(i + 1) * w], m.iq[rows, h // 2, s.t * P:(s.t + 1) * P],
                                         m.k["a"][rows, 1, 0:w], start=True, stop=True)
                    last.then_inc(m.aux_ready, 1)
                elif kind == "score":
                    k, w = plan.bank[s.name], att.width(s)
                    take_bank(m, pe, k)
                    for need in {"e": ("memk0", "memk1", "eq0", "eq1"), "c": ("dq0", "dq1", "dk0", "dk1"), "a": ("aq0", "aq1", "kk0"),
                                 "b": tuple(f"b{x}{j}" for x in "qk" for j in range(4))}[s.b]:
                        if s is att.score_of[s.b, 0, 0]:
                            pe.wait_ge(*aux_is_done(m, plan, need))
                    if s.b == "a":
                        pe.wait_ge(m.chosen, s.t + 1)
                    mask = None if s.b == "e" else m.unchosen[:, s.t, 0:w] if s.b == "a" else m.later[:, TOK - w:TOK]
                    for i, h in enumerate(s.heads):
                        out = m.aux[:, k.bank, i * w:(i + 1) * w]
                        last = pe.matmul(out, queries(s.b, h, s.t), keys(s.b, h, w), start=True, stop=mask is None)
                        if mask is not None:
                            last = pe.matmul(out, m.neg_ident[:, :], mask, start=False, stop=True)
                    last.then_inc(m.aux_ready, 1)
                elif kind == "probs":
                    turn_probs(m, pe, plan, att, s)
                elif kind == "value":
                    k = plan.bank[s.name]
                    take_bank(m, pe, k)
                    for hs in groups(s.b, s.t):
                        pe.wait_ge(*aux_is_done(m, plan, att.probs_of[s.b, s.t, hs[0]].name))
                    if s.b == "c":
                        pe.wait_ge(*unit_is_done(m, plan, "u_dv"))
                    if s.b == "e":
                        pe.wait_ge(*unit_is_done(m, plan, "memv"))
                    chunks, d = 2 if s.b == "e" or s.t == 1 else 1, DIM[s.b]
                    for i, h in enumerate(s.heads):
                        for c in range(chunks):
                            last = pe.matmul(m.aux[:, k.bank, i * d:(i + 1) * d], m.pt[:, h, c, :], values(s.b, h, c),
                                             start=c == 0, stop=c == chunks - 1)
                    last.then_inc(m.aux_ready, 1)

        @block.scalar
        def _(act):
            for i in range(LEAD):
                split_high(m, act, plan, plan.slabs[i])
            loads = [
                (m.sgu_raw[:, :, :], sgu_w[l].rearrange("g i j -> i g j"), m.sgu_in),
                (m.sgu_g[:, :], sgu_ln_g[l].partition_broadcast(P), m.small_in3),
                (m.sgu_be[:, :], sgu_ln_b[l].partition_broadcast(P), m.small_in3),
                (m.sgu_bias[:, :], sgu_b[l].rearrange("g i -> i g"), m.small_in3),
                (m.qgain[:, :], mla_q_norm_g[l].rearrange("(k p) -> p k", p=P), m.small_in2),
                (m.kvgain[:, :], mla_kv_norm_g[l].rearrange("(k p) -> p k", p=P), m.small_in2),
                (m.lam_in[:, :], diff_lambda[l].rearrange("a d -> (a d)").partition_broadcast(P), m.small_in4),
                (m.diff_g[:, :], diff_norm_g[l].partition_broadcast(P), m.small_in4),
            ]
            for kind, s in plan.order:
                if kind == "slab":
                    if s.i + LEAD < len(plan.slabs):
                        split_high(m, act, plan, plan.slabs[s.i + LEAD])
                    if s.i < len(loads):
                        dst, src, sem_ = loads[s.i]
                        act.dma_start(dst, src).then_inc(sem_, 16)
                elif kind == "norm_x":
                    square_tile(m, act, 0)
                elif kind == "evac":
                    src = m.pairs[s.pair][:, :, 0:s.n]
                    done = m.dense_done[s.pair]
                    if s.name[:3] in ("mem", "u_s", "u_e", "u_d", "u_p", "uq0", "uq1"):
                        act.wait_ge(m.slab_used, plan.last_slab[s.name] + 1)
                        if s.name in ("memk", "memv"):
                            for t in range(TILES):
                                last = act.activation({"memk": m.memk, "memv": m.memv}[s.name][:, t, :], src[:, t, :], ACT.Copy,
                                                      scale=m.mem_rs[:, t:t + 1])
                            last.then_inc(done, 1)
                            continue
                        if s.name[:2] == "uq":
                            c = COL["su"] + 512 * int(s.name[2])
                            dst = m.proj[:, :, c:c + s.n]
                        else:
                            c = 512 * int(s.name[3]) if s.name[:3] == "u_p" else COL[s.name[2:]]
                            dst = m.proj[:, :, c:c + s.n]
                        act.activation(dst, src, ACT.Copy).then_inc(done, 1)
                    elif s.name[:3] == "ukv":
                        act.wait_ge(m.slab_used, plan.last_slab[s.name] + 1)
                        h0 = 4 * int(s.name[3])
                        for t in range(TILES):
                            heads = m.pairs[s.pair][:, t, :].rearrange("p (h d) -> p h d", d=128)
                            kf = m.kfull[:, t, :].rearrange("p (h d) -> p h d", d=96)
                            act.activation(kf[:, h0:h0 + 4, 0:64], heads[:, :, 0:64], ACT.Copy)
                            vv = m.vb[:, t, :].rearrange("p (h d) -> p h d", d=64)
                            last = act.activation(vv[:, h0:h0 + 4, :], heads[:, :, 64:128], ACT.Copy)
                        last.then_inc(done, 1)
                    elif s.name[:5] == "gate_":
                        act.wait_ge(m.slab_used, plan.last_slab[s.name] + 1)
                        act.activation(m.th[:, :, :], src, ACT.Tanh, scale=0.5).then_inc(m.gate_tanh, 1)
                    elif s.name[:5] == "merge":
                        act.wait_ge(m.slab_used, plan.last_slab[s.name] + 1)
                        i = merges.index(s.name)
                        if i:
                            act.wait_ge(m.mixed_up, i)
                        act.activation(m.sg[:, :, :], src, ACT.Tanh, scale=0.5).then_inc(done, 1)
                elif kind == "split":
                    split_hi(m, act, plan, s)
                elif kind == "turn":
                    k = plan.bank[s.name]
                    act.wait_ge(m.aux_ready, k.n + 1)
                    if s.name[:2] == "bk":
                        act.wait_ge(m.diffed, TILES)
                    act.activation(s.dst[:, 2 * s.j:2 * s.j + 2, :],
                                   m.aux[0:s.rows, k.bank, :].rearrange("p (k n) -> p k n", n=TOK), ACT.Copy,
                                   scale=s.scale).then_inc(m.aux_done[k.bank], 1)
                elif kind == "score":
                    exponentials(m, act, plan, att, s)
                elif kind == "probs":
                    keep_probs(m, act, plan, s)
                elif kind == "ada_sum":
                    k = plan.bank[s.name]
                    act.wait_ge(m.aux_ready, k.n + 1)
                    act.activation(m.ada[:, bass.ds(l, 1), 4 * s.i:4 * s.i + 4], m.aux[:, k.bank, 0:4].unsqueeze(1), ACT.Copy)\
                       .then_inc(m.aux_done[k.bank], 1)
                elif kind == "diff_mix" and s.i == 0:
                    act.wait_ge(m.lam_ready, 2)
                    act.activation(m.lam[:, 2:4], m.lam[:, 0:2], ACT.Exp).then_inc(m.lam_ready, 1)
            for sem_, n in ((m.small_in, 16), (m.sgu_in, 16), (m.small_in2, 32), (m.small_in3, 48), (m.small_in4, 32)):
                act.wait_ge(sem_, n)

        @block.gpsimd
        def _(pool):
            st = Steps(pool, m.pool_step)

            def rotate(x, heads, half, cos, sin, last_inc):
                r = m.rot[:, :, 0:heads * 2 * half].rearrange("p t (h d) -> p t h d", h=heads)
                c = cos.unsqueeze(2).to_broadcast([P, TILES, heads, 2 * half])
                s0 = sin[:, :, 0:half].unsqueeze(2).to_broadcast([P, TILES, heads, half])
                s1 = sin[:, :, half:2 * half].unsqueeze(2).to_broadcast([P, TILES, heads, half])
                st.settle()
                st.did(pool.tensor_tensor(r[:, :, :, 0:half], x[:, :, :, half:2 * half], s0, ALU.mult))
                st.did(pool.tensor_tensor(r[:, :, :, half:2 * half], x[:, :, :, 0:half], s1, ALU.mult))
                st.settle()
                st.did(pool.tensor_tensor(x, x, c, ALU.mult))
                st.settle()
                ins = pool.tensor_tensor(x, x, r, ALU.add)
                if last_inc is None:
                    st.did(ins)
                else:
                    ins.then_inc(last_inc, 1)

            def heads_of(c, n, w, lo, hi):
                return m.proj[:, :, c:c + n * w].rearrange("p t (h d) -> p t h d", d=w)[:, :, :, lo:hi]

            for kind, s in plan.order:
                if kind == "ada":
                    chunk = s.i % 8
                    pool.wait_ge(m.ada_in, 16 * s.i + 16)
                    if chunk == 0:
                        if s.i:
                            pool.wait_ge(m.aux_ready, plan.bank[f"ada_sum{s.i // 8 - 1}"].n + 1)
                        pool.tensor_scalar(m.ada_acc[:, :], m.ada_w[:, :], m.c_silu[:, 0:1], None, ALU.mult).then_inc(m.ada_used, 1)
                    else:
                        st.did(pool.tensor_scalar(m.ada_w[:, :], m.ada_w[:, :], m.c_silu[:, chunk:chunk + 1], None, ALU.mult))
                        st.settle()
                        pool.wait_ge(m.ada_used, s.i)
                        pool.tensor_tensor(m.ada_acc[:, :], m.ada_acc[:, :], m.ada_w[:, :], ALU.add).then_inc(m.ada_used, 1)
                if kind != "rope":
                    continue
                if s.name == "rope_d":
                    pool.wait_ge(m.sgu_out, TILES)
                    pool.wait_ge(*unit_is_done(m, plan, "u_dq"))
                    pool.wait_ge(*unit_is_done(m, plan, "u_dk"))
                    rotate(heads_of(COL["dq"], 16, 64, 0, 16), 16, 8, m.cos_p[:, :, :], m.sin_p[:, :, :], m.roped)
                elif s.name == "rope_a":
                    pool.wait_ge(*unit_is_done(m, plan, "u_p0"))
                    pool.wait_ge(*unit_is_done(m, plan, "u_p1"))
                    rotate(heads_of(COL["aq"], 9, 64, 0, 16), 9, 8, m.cos_p[:, :, :], m.sin_p[:, :, :], None)
                    rotate(heads_of(COL["iq"], 5, 64, 0, 16), 5, 8, m.cos_p[:, :, :], m.sin_p[:, :, :], None)
                    st.did(pool.tensor_scalar(m.wi[:, :, :], m.proj[:, :, COL["iw"]:COL["iw"] + 4],
                                              float(IDX_HEADS * IDX_DIM) ** -0.5, None, ALU.mult))
                    st.settle()
                    for i, c in enumerate((COL["ak"], COL["ik"])):
                        for j in range(2):
                            last = pool.tensor_copy(m.kk[:, :, P * i + 64 * j:P * i + 64 * j + 64], m.proj[:, :, c:c + 64])
                            if i + j < 2:
                                st.did(last)
                    last.then_inc(m.roped, 1)
                elif s.name == "rope_b":
                    for x in ("u_p3", "uq0", "uq1", "ukv1"):
                        pool.wait_ge(*unit_is_done(m, plan, x))
                    rotate(heads_of(COL["su"], 8, 96, 64, 96), 8, 16, m.cos_m[:, :, :], m.sin_m[:, :, :], None)
                    rotate(heads_of(COL["kr"], 1, 32, 0, 32), 1, 16, m.cos_m[:, :, :], m.sin_m[:, :, :], None)
                    st.settle()
                    kf = m.kfull[:, :, :].rearrange("p t (h d) -> p t h d", d=96)[:, :, :, 64:96]
                    kr = m.proj[:, :, COL["kr"]:COL["kr"] + 32].unsqueeze(2).to_broadcast([P, TILES, MLA_HEADS, ROT])
                    pool.tensor_copy(kf, kr).then_inc(m.roped, 1)

        @block.vector
        def _(dve):
            st = Steps(dve, m.dve_step)
            def weigh(s):
                k, w = plan.bank[s.name], P if s.t == 0 else TOK
                sc = m.index_score[:, s.t, 0:w]
                dve.wait_ge(m.aux_ready, k.n + 1)
                dve.wait_ge(m.roped, ropes_done["rope_a"])
                for i, h in enumerate(s.heads):
                    out = sc if h == 0 else m.index_work[:, s.t, 0:w]
                    st.settle()
                    ins = dve.tensor_scalar(out, m.aux[:, k.bank, i * w:(i + 1) * w], 0.0, m.wi[:, s.t, h:h + 1], ALU.max, ALU.mult)
                    if i == len(s.heads) - 1:
                        ins.then_inc(m.aux_done[k.bank], 1)
                        dve.wait_ge(*aux_is_done(m, plan, s.name))
                    else:
                        st.did(ins)
                        st.settle()
                    if h:
                        st.did(dve.tensor_tensor(sc, sc, out, ALU.add))

            def choose(t, part):
                w = P if t == 0 else TOK
                sc, work, best = m.index_score[:, t, 0:w], m.index_work[:, t, 0:w], m.best[:, :]
                st.settle()
                if part == 0:
                    st.did(dve.tensor_tensor(sc[:, w - P:w], sc[:, w - P:w], m.later_neg[:, :], ALU.add))
                src = work if part else sc
                for _ in range(2):
                    st.settle()
                    st.did(dve.max(best, src))
                    st.settle()
                    st.did(dve.match_replace(work, best, src, TAKEN))
                    src = work
                if part < TOPK // 16 - 1:
                    return
                st.settle()
                if t:
                    st.did(dve.tensor_scalar(m.unchosen[:, t, 0:P], work[:, 0:P], 0.5 * TAKEN, None, ALU.is_gt))
                dve.scalar_tensor_tensor(m.unchosen[:, t, w - P:w], work[:, w - P:w], 0.5 * TAKEN, m.later[:, P:TOK],
                                         ALU.is_gt, ALU.max).then_inc(m.chosen, 1)

            for i in range(LEAD):
                split_low(m, dve, plan.slabs[i])
            for kind, s in plan.order:
                if kind == "slab":
                    if s.i + LEAD < len(plan.slabs):
                        split_low(m, dve, plan.slabs[s.i + LEAD])
                elif kind == "norm_x":
                    norm_stats(m, dve, st, 0, (m.squared, 1))
                    for t in range(TILES):
                        last = dve.tensor_scalar(m.mixed[:, t, :], m.h[:, t, :], m.rs[:, t:t + 1], None, ALU.mult)
                    last.then_inc(m.normed, 1)
                elif kind == "split":
                    split_lo(m, dve, plan, s)
                elif kind == "sgu_w":
                    k = plan.bank[s.name]
                    dve.wait_ge(m.aux_ready, k.n + 1)
                    dve.tensor_tensor(m.sgu_t[:, 4 * s.j:4 * s.j + 4, :], m.aux[:, k.bank, :].rearrange("p (g i) -> p g i", i=P),
                                      m.upto[:, :].unsqueeze(1).to_broadcast([P, 4, P]), ALU.mult).then_inc(m.aux_done[k.bank], 1)
                elif kind == "sgu_norm":
                    v = m.proj[:, :, COL["sv"]:COL["sv"] + 512]
                    st.settle()
                if kind == "sgu_norm" and s.i == 0:
                    dve.wait_ge(*unit_is_done(m, plan, "u_sv"))
                    for t in range(TILES):
                        st.did(dve.bn_stats(m.stats[:, t, 0, :], v[:, t, :]))
                    st.settle()
                    for t in range(TILES):
                        st.did(dve.bn_aggr(m.stats[:, t, 2, 0:2], m.stats[:, t, 0:1, :]))
                    st.settle()
                    st.did(dve.tensor_copy(m.ms[:, 2:4], m.stats[:, :, 2, 1]))
                if kind == "sgu_norm" and s.i == 1:
                    rsqrt(dve, st, m.rs[:, 2:4], m.ms[:, 2:4], m.nt[:, 2:4], 1.0, 1e-5)
                    st.settle()
                    for t in range(TILES):
                        st.did(dve.tensor_scalar(v[:, t, :], v[:, t, :], m.stats[:, t, 2, 0:1], m.rs[:, 2 + t:3 + t],
                                                 ALU.subtract, ALU.mult))
                if kind == "sgu_norm" and s.i == 2:
                    dve.wait_ge(m.small_in3, 48)
                    st.did(dve.tensor_tensor(v, v, m.sgu_g[:, :].unsqueeze(1).to_broadcast([P, TILES, 512]), ALU.mult))
                    st.settle()
                    dve.tensor_tensor(v, v, m.sgu_be[:, :].unsqueeze(1).to_broadcast([P, TILES, 512]), ALU.add)\
                       .then_inc(m.sgu_normed, 1)
                if kind == "sgu_z":
                    k = plan.bank[s.name]
                    z = m.proj[:, s.t, COL["sv"]:COL["sv"] + 512]
                    u = m.proj[:, s.t, COL["su"]:COL["su"] + 512]
                    dve.wait_ge(m.aux_ready, k.n + 1)
                    dve.tensor_tensor(z.rearrange("p (g d) -> p g d", d=64), m.aux[:, k.bank, :].rearrange("p (g d) -> p g d", d=64),
                                      m.sgu_bias[:, :].unsqueeze(2).to_broadcast([P, 8, 64]), ALU.add).then_inc(m.aux_done[k.bank], 1)
                    dve.wait_ge(*aux_is_done(m, plan, s.name))
                    dve.wait_ge(*unit_is_done(m, plan, "u_su"))
                    dve.tensor_tensor(u, u, z, ALU.mult).then_inc(m.sgu_out, 1)
                elif kind == "dots":
                    weigh(s)
                elif kind == "topk":
                    choose(s.t, s.i)
                elif kind == "low_rank":
                    for x in ("u_p1", "u_p2", "u_p3"):
                        dve.wait_ge(*unit_is_done(m, plan, x))
                    for i, (c, n) in enumerate((("cq", 384), ("ckv", 256))):
                        mean_square(dve, st, m.stats, m.ms[:, 4 + 2 * i:6 + 2 * i], lambda t, c=c, n=n: m.proj[:, t, COL[c]:COL[c] + n], n)
                    rsqrt(dve, st, m.rs[:, 4:8], m.ms[:, 4:8], m.nt[:, 4:8], 1.0, 1e-6)
                    st.settle()
                    for i, (c, n) in enumerate((("cq", 384), ("ckv", 256))):
                        for t in range(TILES):
                            v = m.proj[:, t, COL[c]:COL[c] + n]
                            last = dve.tensor_scalar(v, v, m.rs[:, 4 + 2 * i + t:5 + 2 * i + t], None, ALU.mult)
                            if i + t < 2:
                                st.did(last)
                    last.then_inc(m.low_rank, 1)
                elif kind == "score":
                    maxima(m, dve, plan, att, s)
                elif kind == "value":
                    k, d, n = plan.bank[s.name], DIM[s.b], len(s.heads)
                    inv = inverse_sums(m, dve, st, plan, att, s)
                    dve.wait_ge(m.aux_ready, k.n + 1)
                    bank = m.aux[:, k.bank, :].rearrange("p (h d) -> p h d", d=d)
                    if s.b != "c":
                        dst = m.proj[:, s.t, COL[OUT[s.b]]:COL[OUT[s.b]] + 512].rearrange("p (h d) -> p h d", d=d)
                        dve.tensor_tensor(dst, bank, inv.unsqueeze(2).to_broadcast([P, n, d]), ALU.mult)\
                           .then_inc(m.aux_done[k.bank], 1)
                    else:
                        dst = m.diff_o[:, s.t, :, :, :][:, s.g, :, :]
                        dve.tensor_tensor(dst, bank, inv.unsqueeze(2).to_broadcast([P, n, d]), ALU.mult)\
                           .then_inc(m.aux_done[k.bank], 1)
                        dve.wait_ge(*aux_is_done(m, plan, s.name))
                        if s.g == 0 and s.t == 0:
                            dve.wait_ge(m.small_in4, 32)
                            pr = m.lam_in[:, :].rearrange("p (a b d) -> p a b d", a=2, b=2)
                            st.did(dve.tensor_tensor(pr[:, :, 0, :], pr[:, :, 0, :], pr[:, :, 1, :], ALU.mult))
                            dve.tensor_scalar(m.diff_g[:, :], m.diff_g[:, :], m.one_less_lam[:, bass.ds(l, 1)], None, ALU.mult)\
                               .then_inc(m.lam_ready, 1)
                            st.settle()
                            dve.tensor_reduce(m.lam[:, 0:2], pr[:, :, 0, :], AX_X, ALU.add).then_inc(m.lam_ready, 1)
                elif kind == "diff_mix":
                    o = m.proj[:, :, COL["dq"]:COL["dq"] + 512].rearrange("p t (j d) -> p t j d", d=128)
                    sq = m.proj[:, :, COL["dk"]:COL["dk"] + 512].rearrange("p t (j d) -> p t j d", d=128)
                    st.settle()
                if kind == "diff_mix" and s.i == 0:
                    dve.wait_ge(m.lam_ready, 3)
                    st.did(dve.scalar_tensor_tensor(m.lam[:, 4:5], m.lam[:, 3:4], -1.0, m.lam[:, 2:3], ALU.mult, ALU.add))
                    st.settle()
                    st.did(dve.tensor_scalar(m.lam[:, 5:6], m.lam[:, 4:5], m.lam_init[:, bass.ds(l, 1)], -1.0, ALU.add, ALU.mult))
                    st.settle()
                    for t in range(TILES):
                        pair = m.diff_o[:, t, :, :, :].rearrange("p g (j two) d -> p (g j) two d", two=2)
                        st.did(dve.scalar_tensor_tensor(o[:, t, :, :], pair[:, :, 1, :], m.lam[:, 5:6], pair[:, :, 0, :],
                                                        ALU.mult, ALU.add))
                if kind == "diff_mix" and s.i == 1:
                    st.did(dve.tensor_tensor(sq, o, o, ALU.mult))
                    st.settle()
                    st.did(dve.tensor_reduce(m.ms[:, 8:16].rearrange("p (t j) -> p t j", t=TILES), sq, AX_X, ALU.add))
                if kind == "diff_mix" and s.i == 2:
                    rsqrt(dve, st, m.rs[:, 8:16], m.ms[:, 8:16], m.nt[:, 8:16], 1.0 / 128, 1e-6)
                    st.settle()
                    r = m.rs[:, 8:16].rearrange("p (t j) -> p t j", t=TILES)
                    st.did(dve.tensor_tensor(o, o, r.unsqueeze(3).to_broadcast([P, TILES, 4, 128]), ALU.mult))
                    st.settle()
                    for t in range(TILES):
                        dve.tensor_tensor(o[:, t, :, :], o[:, t, :, :], m.diff_g[:, :].unsqueeze(1).to_broadcast([P, 4, 128]),
                                          ALU.mult).then_inc(m.diffed, 1)
                if kind == "gate":
                    u = plan.unit["gate_" + s.b].pair
                    g = m.pairs[u]
                    n = gates[s.b] + 1
                    dve.wait_ge(m.gate_tanh, n)
                    dve.scalar_tensor_tensor(m.th[:, :, :], m.th[:, :, :], 1.0, g, ALU.add, ALU.mult).then_inc(m.dense_done[u], 1)
                    dve.wait_ge(*unit_is_done(m, plan, "gate_" + s.b))
                    if s.b == "c":
                        dve.wait_ge(m.diffed, TILES)
                    if s.b == "d":
                        dve.wait_ge(m.sgu_out, TILES)
                    for t in range(TILES):
                        if s.b in "abe":
                            dve.wait_ge(*aux_is_done(m, plan, f"v_{s.b}{t}0"))
                    st.settle()
                    c = COL[OUT[s.b]]
                    dve.scalar_tensor_tensor(m.th[:, :, :], m.th[:, :, :], 0.5, m.proj[:, :, c:c + 512], ALU.mult, ALU.mult)\
                       .then_inc(m.gated, 1)
                elif kind == "evac" and s.name[:4] == "out_":
                    i, u = outs.index(s.name), s.pair
                    src = m.pairs[u]
                    mx = m.mixed[:, :, 512 * (i % 2):512 * (i % 2) + 512]
                    dve.wait_ge(*unit_is_done(m, plan, merges[i]))
                    dve.wait_ge(m.slab_used, plan.last_slab[s.name] + 1)
                    dve.scalar_tensor_tensor(m.sg[:, :, :], m.sg[:, :, :], 1.0, src, ALU.add, ALU.mult).then_inc(m.dense_done[u], 1)
                    dve.wait_ge(*unit_is_done(m, plan, s.name))
                    if i < 2:
                        dve.tensor_scalar(mx, m.sg[:, :, :], 0.5, None, ALU.mult).then_inc(m.mixed_up, 1)
                    else:
                        dve.wait_ge(m.mixed_up, i - 1)
                        dve.scalar_tensor_tensor(mx, m.sg[:, :, :], 0.5, mx, ALU.mult, ALU.add).then_inc(m.mixed_up, 1)
                elif kind == "evac" and s.name[:3] == "res":
                    c = 512 * int(s.name[3])
                    dve.wait_ge(m.slab_used, plan.last_slab[s.name] + 1)
                    dve.tensor_tensor(m.h[:, :, c:c + 512], m.h[:, :, c:c + 512], m.pairs[s.pair],
                                      ALU.add).then_inc(m.dense_done[s.pair], 1)


NAMES_2 = ("gq", "gk", "gv", "gr", "gg", "mq", "mk", "mv")
WIDTHS_2 = (256, 256, 512, 512, 16, 512, 512, 512)
COL_2 = dict(zip(NAMES_2, np.concatenate([[0], np.cumsum(WIDTHS_2)[:-1]]).tolist()))
PROJ_2 = sum(WIDTHS_2)
FF_PARTS = 8
GATE_RANK, GLA_TAU, MOBA_HEADS = 16, 16.0, 8
CHUNK = 64
CHUNKS = TOK // CHUNK
REL = 384
REL_BUCKETS, REL_MAX_DIST = 32, 128


def bucket_rows():
    rel = (TOK - 1 - np.arange(REL)).astype(np.int32)
    n = np.maximum(rel, 0)
    exact = REL_BUCKETS // 2
    ratio = np.maximum(n, 1).astype(np.float32) / np.float32(exact)
    large = exact + (np.log(ratio) / np.float32(np.log(REL_MAX_DIST / exact)) * np.float32(REL_BUCKETS - exact)).astype(np.int32)
    bucket = np.where(n < exact, n, np.minimum(large, REL_BUCKETS - 1))
    rows = np.zeros((REL_BUCKETS + 1, REL), np.float32)
    rows[bucket, np.arange(REL)] = 1.0
    rows[:, rel < 0] = 0.0
    rows[REL_BUCKETS, rel < 0] = MASKED
    return rows


def second_units(w_in, w_out, w_ff1, w_ff2):
    def part(w, col, n, row=0):
        return lambda k0, kn: w[row + k0 * P:row + (k0 + kn) * P, col:col + n].rearrange("(k p) n -> p k n", p=P)

    us = [unit("w_" + c, "x", 8, part(w_in[0], COL_2[c], n), n)
          for c, n in (("gg", 16), ("gq", 512), ("mq", 512), ("mk", 512), ("mv", 512), ("gv", 512), ("gr", 512))]
    first = len(us) % 2
    us += [unit(f"y{half}{j}", ("my", "mx")[half], 4, part(w_out[0], 512 * j, 512, row=512 - 512 * half), 512, pair=(first + j) % 2,
                opens=half == 0, closes=half == 1) for half in range(2) for j in range(2)]

    def up(j):
        return unit(f"up{j}", "m", 8, part(w_ff1[0], 512 * j, 512), 512, pair=2)

    def down(j):
        return [unit(f"down{j}_{n}", f"hid{j % 2}", 4, part(w_ff2[0], 512 * n, 512, row=512 * j), 512, pair=(first + n) % 2,
                     opens=j == 0, closes=j == FF_PARTS - 1) for n in range(2)]

    us += [up(0), up(1)]
    for j in range(FF_PARTS):
        us += down(j)
        if j + 2 < FF_PARTS:
            us.append(up(j + 2))
    return us


def second_steps(m):
    def split(name, kc, src, dst, after, before, scale=None, shift=None, narrow=False):
        return [step(f"{name}{j}", "shifted" if scale is not None else "split", after=after, before=before, j=j, kc=kc, src=src,
                     dst=dst, gain=scale, shift=shift, gain_ready=None, narrow=narrow) for j in range(-(-kc // 2))]

    def turn(name, n, src, dst, after, scale=1.0):
        return [step(f"{name}{j}", "turn", after=after, j=j, src=src, dst=dst, scale=scale) for j in range(n // 2)]

    def region(c):
        return lambda t: m.proj_2[:, t, COL_2[c]:COL_2[c] + 512]

    s = [step("norm_in", "norm_in")]
    s += split("x", 8, lambda t: m.mixed[:, t, :], "x", [], "w_gg", m.scale_a, m.shift_a)
    s += [step("first_lows", "first_lows"), step("ada_rows", "ada_rows", after=[("w_gg", 0)])]
    s += [step("gg", "turn_gg", after=[("w_gg", 1)]), step("gla_z", "gla_z", after=[("gg", 1)])]
    s += [step(f"gla_sum{i}", "gla_sum", after=[("gla_z", 2)], i=i) for i in range(3)]
    s += [step("gla_decay", "gla_decay", after=[("gla_z", 2)])]
    s += [step("gla_mul", "gla_mul", after=[("gla_sum2", 0), ("gla_decay", 0), ("w_gq", 0)])]
    for n, src, dst in (("qa", m.qa, m.qa_t), ("ka", m.ka, m.ka_t), ("qb", m.qb, m.qb_t)):
        s += turn(n, 2, lambda t, src=src: src[:, t, :], dst, [("gla_mul", 1)], scale=CHUNK ** -0.5 if n[0] == "q" else 1.0)
    s += [step(f"inner{r}", "inner", after=[("qb0", 1)], r=r) for r in range(2)]
    s += turn("mq", 4, region("mq"), m.q["m"], [("w_mq", 1)], scale=0.125)
    s += turn("mk", 4, region("mk"), m.k["m"], [("w_mk", 1)])
    s += [step(f"state{n}", "state", after=[("w_gv", 1), ("gla_mul", 1)], n=n) for n in range(CHUNKS - 1)]
    s += [step(f"gla_o{t}{r}", "gla_o", after=[("state2", 1), ("inner1", 2)], t=t, r=r) for t in range(TILES) for r in range(2)]
    s += [step("gla_gate", "gla_gate", after=[("w_gr", 0)])]
    s += [step("gla_norm", "gla_norm", after=[("gla_o11", 1), ("w_gr", 0)])]
    s += attention_steps("m", lambda t: [("mk1", 1)], 1, [("w_mv", 1)])
    s += split("mx", 4, lambda t: m.mixed[:, t, 0:512], "mx", [("gla_norm", 2)], "y10")
    s += split("my", 4, lambda t: m.mixed[:, t, 512:1024], "my", [("w_gr", 0), ("v_m10", 1)], "y00")
    s += [step("norm_m", "norm_m", after=[("y11", 0)])]
    s += split("m", 8, lambda t: m.mixed[:, t, :], "m", [("norm_m", 0)], "up0", m.scale_m, m.shift_m)
    return s


def second_block(nc, m, weights, small, out):
    (b_ada, g_mix, w_gla_gate, b_gla_gate, g_gla_out, g_mlp, g_final) = small
    plan = Plan(second_units(*weights), second_steps(m), rate=2)
    att = Attention(plan)
    ups = [x.name for k, x in plan.order if k == "evac" and x.name.startswith("up")]

    def wait_uses(eng, banks):
        for b in banks:
            eng.wait_ge(m.aux_done[b], max(k.turn for k in plan.bank.values() if k.bank == b) + 1)

    seen = []

    def lhs_ready(s):
        x = s.unit
        if x.lhs[:3] == "hid":
            return [(m.hidden, 2 * int(x.name[4]) + 2)] if s.first and x.name[-1] == "0" else []
        name = x.lhs
        names = [f"{name}{j}" for j in range(s.k0 // 2, (s.k0 + s.kn - 1) // 2 + 1)]
        out = [aux_is_done(m, plan, n) for n in names if n not in seen]
        seen.extend(names)
        return out

    def rows(r):
        return slice(64 * r, 64 * r + 64)

    with nc.Block() as block:
        @block.sync
        def _(sp):
            ada = [m.ada_row[i * 1024:(i + 1) * 1024] for i in range(6)]
            for dst, src in ((m.ada_bias, b_ada[0]), (m.g_mix, g_mix[0]), (m.g_mlp, g_mlp[0])):
                sp.dma_start(dst, src.rearrange("(k p) -> p k", p=P)).then_inc(m.small_in, 16)
            for s in plan.slabs:
                load_slab(m, sp, plan, s)
                if s.i == RAW_SLOTS - 1:
                    sp.dma_start(m.w_gate, w_gla_gate[0]).then_inc(m.small_in3, 16)
                    sp.dma_start(m.b_gate, b_gla_gate[0].partition_broadcast(P)).then_inc(m.small_in3, 16)
                    sp.dma_start(m.bias, bass.AP(tensor=m.bias_rows.tensor, offset=0, ap=[[1, P], [REL, MOBA_HEADS], [1, TOK]]))\
                      .then_inc(m.bias_in, 16)
                    sp.dma_start(m.g_out, g_gla_out[0].partition_broadcast(P)).then_inc(m.small_in4, 16)
                if s.last and s.unit.name == "w_mk":
                    sp.wait_ge(*aux_is_done(m, plan, "ada_rows"))
                    sp.dma_start(m.ada_row.rearrange("(k p) -> k p", p=P), m.ada_t).then_inc(m.gates_out, 16)
                if s.last and s.unit.name == "w_mv":
                    sp.wait_ge(m.gates_out, 16)
                    sp.dma_start(m.gate_a, ada[2].partition_broadcast(P)).then_inc(m.gates_in, 16)
                    sp.dma_start(m.gate_m, ada[5].partition_broadcast(P)).then_inc(m.gates_in, 16)
                if s.last and s.unit.name == "y11":
                    sp.wait_ge(m.aux_ready, plan.bank["v_m10"].n + 1)
                    sp.dma_start(m.row_pt, g_final.partition_broadcast(P)).then_inc(m.sgu_in, 16)
            for sem_, n in ((m.small_in, 48), (m.small_in3, 32), (m.small_in4, 16), (m.bias_in, 16), (m.sgu_in, 16)):
                sp.wait_ge(sem_, n)
            for t in range(TILES):
                sp.wait_ge(m.out_ready, 1 + t)
                sp.dma_start(out[0, t * P:(t + 1) * P, :], m.mixed[:, t, :]).then_inc(m.mem_in, 16)
            sp.wait_ge(m.mem_in, 16 * TILES)

        @block.tensor
        def _(pe):
            pe.wait_ge(m.consts, 1)
            for kind, s in plan.order:
                k = plan.bank.get(s.name) if kind not in ("slab", "evac") else None
                if kind == "slab":
                    if s.first and s.unit.name == "up0":
                        wait_uses(pe, (0, 1))
                    (multiply_turned if s.unit.name[:2] == "up" else multiply)(m, pe, plan, s, lhs_ready(s))
                elif kind in ("split", "shifted"):
                    if s.name[:2] == "mx":
                        ready = [(m.gla_normed, 1)]
                    elif s.name[:2] == "my":
                        ready = [aux_is_done(m, plan, "v_m00"), aux_is_done(m, plan, "v_m10")]
                    else:
                        n = 1 if s.name[0] == "x" else 2
                        ready = [(m.normed, n), (m.normed_act, n)]
                    turn_blocks(m, pe, k, split_blocks(s, m), ready)
                elif kind == "turn":
                    ready = {"mq": [unit_is_done(m, plan, "w_mq")], "mk": [unit_is_done(m, plan, "w_mk")]}\
                        .get(s.name[:2], [(m.gla_scaled, 1)])
                    blocks = [s.src(t)[:, (2 * s.j + i) * P:(2 * s.j + i + 1) * P] for i in range(2) for t in range(TILES)]
                    turn_blocks(m, pe, k, blocks, ready)
                elif kind == "ada_rows":
                    turn_blocks(m, pe, k, [m.ada_cols], [(m.ada_in, 1)])
                elif kind == "turn_gg":
                    c = COL_2["gg"]
                    turn_blocks(m, pe, k, [m.proj_2[:, t, c:c + GATE_RANK] for t in range(TILES)], [unit_is_done(m, plan, "w_gg")])
                elif kind == "gla_z":
                    take_bank(m, pe, k)
                    pe.wait_ge(*aux_is_done(m, plan, "gg"))
                    pe.wait_ge(m.small_in3, 32)
                    for t in range(TILES):
                        last = pe.matmul(m.aux[:, k.bank, t * 256:(t + 1) * 256], m.gg_t[:, t * P:(t + 1) * P], m.w_gate,
                                         start=True, stop=True)
                    last.then_inc(m.aux_ready, 1)
                elif kind == "gla_sum":
                    take_bank(m, pe, k)
                    pe.wait_ge(m.gla_log, 5)
                    pe.wait_ge(m.tables, 4)
                    for t in range(TILES):
                        last = pe.matmul(m.aux[:, k.bank, t * 256:(t + 1) * 256], (m.from_middle, m.to_end, m.from_start)[s.i],
                                         m.log_decay[:, t, :], start=True, stop=True)
                    last.then_inc(m.aux_ready, 1)
                elif kind == "gla_decay":
                    take_bank(m, pe, k)
                    for t in range(TILES):
                        for p in range(2):
                            c = 2 * (2 * t + p)
                            last = pe.matmul(m.aux[:, k.bank, c:c + 2], m.log_decay[:, t, p * P:(p + 1) * P], m.chunk_ones,
                                             start=True, stop=True)
                    last.then_inc(m.aux_ready, 1)
                elif kind == "inner":
                    take_bank(m, pe, k)
                    for need in ("qa0", "ka0"):
                        pe.wait_ge(*aux_is_done(m, plan, need))
                    for p in range(2):
                        for t in range(TILES):
                            tok = slice(t * P, (t + 1) * P)
                            last = pe.matmul(m.aux[:, k.bank, (2 * p + t) * P:(2 * p + t + 1) * P], m.ka_t[rows(s.r), p, tok],
                                             m.qa_t[rows(s.r), p, tok], start=True, stop=True)
                    last.then_inc(m.aux_ready, 1)
                elif kind == "state":
                    take_bank(m, pe, k)
                    pe.wait_ge(*unit_is_done(m, plan, "w_gv"))
                    pe.wait_ge(m.gla_scaled, 1)
                    t, c = s.n // 2, s.n % 2
                    for p in range(2):
                        v = COL_2["gv"] + 256 * p
                        last = pe.matmul(m.aux[:, k.bank, 256 * p:256 * p + 256], m.kb[rows(c), t, p * P:(p + 1) * P],
                                         m.proj_2[rows(c), t, v:v + 256], start=True, stop=True)
                    last.then_inc(m.aux_ready, 1)
                elif kind == "gla_o":
                    take_bank(m, pe, k)
                    pe.wait_ge(m.masked, 1)
                    for n in range(CHUNKS - 1):
                        pe.wait_ge(*aux_is_done(m, plan, f"state{n}"))
                    pe.wait_ge(*unit_is_done(m, plan, "w_gv"))
                    pe.wait_ge(*aux_is_done(m, plan, "qb0"))
                    for p in range(2):
                        v = COL_2["gv"] + 128 * (2 * p + s.r)
                        bank = m.aux[:, k.bank, p * P:(p + 1) * P]
                        pe.matmul(bank, m.inner[:, s.r, 2 * p + s.t, :], m.proj_2[:, s.t, v:v + 128], start=True, stop=False,
                                  skip_group_check=True)
                        for c in range(2):
                            n = 2 * s.t + c
                            if n:
                                tok = slice(64 * n, 64 * n + 64)
                                last = pe.matmul(bank[rows(c), :], m.qb_t[rows(s.r), p, tok], m.state[rows(s.r), n - 1, p, :],
                                                 start=False, stop=c == 1, skip_group_check=True)
                    last.then_inc(m.aux_ready, 1)
                elif kind == "score":
                    take_bank(m, pe, k)
                    if s is att.score_of["m", 0, 0]:
                        for need in ("mq0", "mq1", "mk0", "mk1"):
                            pe.wait_ge(*aux_is_done(m, plan, need))
                        pe.wait_ge(m.bias_in, 16)
                    w = att.width(s)
                    for i, h in enumerate(s.heads):
                        bank = m.aux[:, k.bank, i * w:(i + 1) * w]
                        pe.matmul(bank, m.q["m"][rows(h % 2), h // 2, s.t * P:(s.t + 1) * P], m.k["m"][rows(h % 2), h // 2, 0:w],
                                  start=True, stop=False)
                        last = pe.matmul(bank, m.backward, m.bias[:, h, P - s.t * P:P - s.t * P + w], start=False, stop=True)
                    last.then_inc(m.aux_ready, 1)
                elif kind == "probs":
                    turn_probs(m, pe, plan, att, s)
                elif kind == "value":
                    take_bank(m, pe, k)
                    for hs in groups(s.b, s.t):
                        pe.wait_ge(*aux_is_done(m, plan, att.probs_of[s.b, s.t, hs[0]].name))
                    pe.wait_ge(*unit_is_done(m, plan, "w_mv"))
                    for i, h in enumerate(s.heads):
                        v = COL_2["mv"] + 64 * h
                        for c in range(s.t + 1):
                            last = pe.matmul(m.aux[:, k.bank, i * 64:(i + 1) * 64], m.pt[:, h, c, :], m.proj_2[:, c, v:v + 64],
                                             start=c == 0, stop=c == s.t)
                    last.then_inc(m.aux_ready, 1)

        @block.scalar
        def _(act):
            square_tile(m, act, 0)

            def norm(n, ready):
                act.wait_ge(*ready)
                square_tile(m, act, 2 * n)
                act.wait_ge(m.normed, n)
                act.activation(m.mixed[:, 1, :], m.h[:, 1, :], ACT.Copy, scale=m.rs[:, 2 * n + 1:2 * n + 2]).then_inc(m.normed_act, 1)

            for kind, s in plan.order:
                k = plan.bank.get(s.name) if kind not in ("slab", "evac") else None
                if kind == "slab":
                    if s.i + LEAD < len(plan.slabs):
                        split_high(m, act, plan, plan.slabs[s.i + LEAD])
                elif kind == "norm_in":
                    norm(1, (m.scales, 1))
                    for i in range(LEAD):
                        split_high(m, act, plan, plan.slabs[i])
                elif kind == "norm_m":
                    norm(2, (m.h_ready, 2))
                elif kind == "evac" and s.name == "w_gr":
                    act.wait_ge(m.slab_used, plan.last_slab[s.name] + 1)
                    act.activation(m.th[:, :, :], m.pairs[s.pair], ACT.Tanh, scale=0.5).then_inc(m.gate_tanh, 1)
                elif kind == "evac" and s.name[:2] == "w_":
                    act.wait_ge(m.slab_used, plan.last_slab[s.name] + 1)
                    c = COL_2[s.name[2:]]
                    act.activation(m.proj_2[:, :, c:c + s.n], m.pairs[s.pair][:, :, 0:s.n], ACT.Copy).then_inc(m.dense_done[s.pair], 1)
                elif kind == "evac" and s.name[:2] == "up":
                    j = int(s.name[2])
                    act.wait_ge(m.slab_used, plan.last_slab[s.name] + 1)
                    if j:
                        act.wait_ge(m.hidden, 2 * j)
                    act.activation(m.th[:, :, :], m.pairs[2], ACT.Relu).then_inc(m.dense_done[2], 1)
                    act.wait_ge(m.gated, j + 1)
                    act.activation(m.lhs[f"hid{j % 2}"][0], m.hid, ACT.Copy).then_inc(m.hidden, 1)
                elif kind == "split":
                    split_hi(m, act, plan, s)
                elif kind == "shifted":
                    k0, kn = split_cols(s, m)
                    act.wait_ge(m.aux_ready, k.n + 1)
                    act.wait_ge(m.scaled, 1)
                    for i in range(kn):
                        last = act.activation(m.lhs[s.dst][0][:, k0 + i, :], m.aux[:, k.bank, i * TOK:(i + 1) * TOK], ACT.Identity,
                                              scale=s.gain[:, k0 + i:k0 + i + 1], bias=s.shift[:, k0 + i:k0 + i + 1])
                    last.then_inc(m.shifted_hi, 1)
                elif kind == "turn":
                    act.wait_ge(m.aux_ready, k.n + 1)
                    act.activation(s.dst[:, 2 * s.j:2 * s.j + 2, :], m.aux[:, k.bank, :].rearrange("p (k n) -> p k n", n=TOK), ACT.Copy,
                                   scale=s.scale).then_inc(m.aux_done[k.bank], 1)
                elif kind == "ada_rows":
                    act.wait_ge(m.aux_ready, k.n + 1)
                    act.activation(m.ada_t, m.aux[0:48, k.bank, 0:P], ACT.Copy).then_inc(m.aux_done[k.bank], 1)
                elif kind == "turn_gg":
                    act.wait_ge(m.aux_ready, k.n + 1)
                    act.activation(m.gg_t, m.aux[0:GATE_RANK, k.bank, 0:TOK], ACT.Copy).then_inc(m.aux_done[k.bank], 1)
                elif kind == "gla_z":
                    act.wait_ge(m.gla_log, 1)
                    act.activation(m.th[:, 0, :], m.th[:, 0, :], ACT.Exp).then_inc(m.gla_log, 1)
                    act.wait_ge(m.gla_log, 3)
                    act.activation(m.th[:, 0, :], m.th[:, 0, :], ACT.Ln).then_inc(m.gla_log, 1)
                elif kind == "gla_sum":
                    act.wait_ge(m.aux_ready, k.n + 1)
                    bank = m.aux[:, k.bank, :].rearrange("p (t n) -> p t n", t=TILES)
                    if s.i == 0:
                        act.activation(m.ka, bank, ACT.Exp, scale=-1.0)
                    act.activation((m.qa, m.kb, m.qb)[s.i], bank, ACT.Exp).then_inc(m.aux_done[k.bank], 1)
                elif kind == "gla_decay":
                    act.wait_ge(m.aux_ready, k.n + 1)
                    act.activation(m.decay, m.aux[:, k.bank, 0:8], ACT.Exp).then_inc(m.aux_done[k.bank], 1)
                elif kind == "inner":
                    act.wait_ge(m.aux_ready, k.n + 1)
                    act.activation(m.inner[:, s.r, :, :], m.aux[:, k.bank, :].rearrange("p (b n) -> p b n", n=P), ACT.Copy)\
                       .then_inc(m.aux_done[k.bank], 1)
                elif kind == "score":
                    exponentials(m, act, plan, att, s)
                elif kind == "probs":
                    keep_probs(m, act, plan, s)
            act.wait_ge(m.h_ready, 4)
            square_tile(m, act, 6)

        @block.gpsimd
        def _(pool):
            st = Steps(pool, m.pool_step)
            st.did(pool.memset(m.from_start, 1.0))
            st.did(pool.memset(m.to_end, 1.0))
            st.did(pool.memset(m.backward, 0.0))
            st.did(pool.memset(m.chunk_ones, 0.0))
            st.settle()
            st.did(pool.affine_select(out=m.from_start, in_=m.from_start, compare_op=ALU.is_ge, fill=0.0, base=0, pattern=[[1, P]],
                                      channel_multiplier=-1))
            st.did(pool.affine_select(out=m.to_end, in_=m.to_end, compare_op=ALU.is_ge, fill=0.0, base=-1, pattern=[[-1, P]],
                                      channel_multiplier=1))
            st.did(pool.affine_select(out=m.backward, in_=m.backward, compare_op=ALU.not_equal, fill=1.0, base=1 - P,
                                      pattern=[[1, P]], channel_multiplier=1))
            st.settle()
            st.did(pool.memset(m.chunk_ones[0:64, 0:1], 1.0))
            st.did(pool.memset(m.chunk_ones[64:P, 1:2], 1.0))
            st.settle()
            st.did(pool.memset(m.from_start[0:64, 64:P], 0.0))
            st.did(pool.memset(m.to_end[64:P, 0:64], 0.0))
            st.settle()
            for q in range(4):
                r = slice(32 * q, 32 * q + 32)
                pool.tensor_scalar(m.from_middle[r, :], (m.from_start if q % 2 else m.to_end)[r, :], 1.0 if q % 2 else -1.0,
                                   None, ALU.mult).then_inc(m.tables, 1)
            pool.wait_ge(m.tables, 4)
            pool.wait_ge(m.normed, 1)
            pool.wait_ge(m.normed_act, 1)
            for t in range(TILES):
                pool.tensor_scalar(m.h[:, t, :], m.h[:, t, :], m.rs[:, t:t + 1], None, ALU.mult).then_inc(m.x_ready, 1)
            pool.wait_ge(m.x_ready, TILES)
            for r in range(2):
                pool.wait_ge(*aux_is_done(m, plan, f"inner{r}"))
                st.did(pool.affine_select(out=m.inner[:, r, :, :], in_=m.inner[:, r, :, :], compare_op=ALU.is_ge, fill=0.0, base=0,
                                          pattern=[[0, 4], [1, P]], channel_multiplier=-1))
            st.settle()
            pool.memset(m.inner[0:64, :, :, 64:P], 0.0).then_inc(m.masked, 1)

        @block.vector
        def _(dve):
            st = Steps(dve, m.dve_step)

            def norm(n):
                norm_stats(m, dve, st, 2 * n, (m.squared, n + 1))
                dve.tensor_scalar(m.mixed[:, 0, :], m.h[:, 0, :], m.rs[:, 2 * n:2 * n + 1], None, ALU.mult).then_inc(m.normed, 1)

            for kind, s in plan.order:
                k = plan.bank.get(s.name) if kind not in ("slab", "evac") else None
                if kind == "slab":
                    if s.i + LEAD < len(plan.slabs):
                        split_low(m, dve, plan.slabs[s.i + LEAD])
                elif kind == "norm_in":
                    def squares(col):
                        for c in range(2):
                            st.did(dve.bn_stats(m.stats[:, 0, c, :], m.h[:, 0, c * BANK:(c + 1) * BANK]))
                        st.settle()
                        st.did(dve.bn_aggr(m.stats[:, 0, 2, 0:2], m.stats[:, 0, 0:2, :]))
                        st.settle()
                        mean = m.stats[:, 0, 2, 0:1]
                        st.did(dve.scalar_tensor_tensor(m.ms[:, col:col + 1], mean, mean, m.stats[:, 0, 2, 1:2], ALU.mult, ALU.add))

                    squares(0)
                    dve.wait_ge(m.squared, 1)
                    for t in (1, 0):
                        dve.tensor_tensor(m.h[:, t, :], m.h[:, t, :], m.row_pt, ALU.mult).then_inc(m.scales, 1)
                    st.settle()
                    st.did(dve.tensor_scalar(m.ms[:, 0:2], m.ms[:, 0:2], 1e-6, None, ALU.add))
                    dve.wait_ge(m.scales, 2)
                    squares(2)
                    st.did(dve.reciprocal(m.nt[:, 2:4], m.ms[:, 0:2]))
                    dve.wait_ge(m.squared, 2)
                    st.settle()
                    st.did(dve.tensor_tensor(m.ms[:, 2:4], m.ms[:, 2:4], m.nt[:, 2:4], ALU.mult))
                    st.settle()
                    st.did(dve.tensor_scalar(m.ms[:, 2:4], m.ms[:, 2:4], 1e-6, None, ALU.add))
                    rsqrt(dve, st, m.rs[:, 0:4], m.ms[:, 0:4], m.nt[:, 0:4], 1.0, 0.0)
                    st.settle()
                    st.did(dve.tensor_tensor(m.rs[:, 2:4], m.rs[:, 0:2], m.rs[:, 2:4], ALU.mult))
                    st.settle()
                    dve.tensor_scalar(m.mixed[:, 0, :], m.h[:, 0, :], m.rs[:, 2:3], None, ALU.mult).then_inc(m.normed, 1)
                    dve.wait_ge(m.small_in, 48)
                    dve.tensor_tensor(m.ada_cols, m.ada_cols, m.ada_bias, ALU.add).then_inc(m.ada_in, 1)
                    dve.wait_ge(m.ada_in, 1)
                    for scale, g in ((m.scale_a, m.g_mix), (m.scale_m, m.g_mlp)):
                        last = dve.scalar_tensor_tensor(scale, scale, 1.0, g, ALU.add, ALU.mult)
                    last.then_inc(m.scaled, 1)
                    dve.wait_ge(m.scaled, 1)
                elif kind == "first_lows":
                    for i in range(LEAD):
                        split_low(m, dve, plan.slabs[i])
                elif kind == "norm_m":
                    norm(2)
                elif kind == "split":
                    split_lo(m, dve, plan, s)
                elif kind == "shifted":
                    k0, kn = split_cols(s, m)
                    tmp, (hi, lo) = m.shift_tmp[:, s.j % 2, :, :], m.lhs[s.dst]
                    dve.wait_ge(m.shifted_hi, plan.seq[s.name] + 1)
                    for i in range(kn):
                        last = dve.scalar_tensor_tensor(tmp[:, i, :], m.aux[:, k.bank, i * TOK:(i + 1) * TOK],
                                                        s.gain[:, k0 + i:k0 + i + 1], hi[:, k0 + i, :].bitcast(F32),
                                                        ALU.mult, ALU.subtract)
                        st.did(last)
                    st.settle()
                    for i in range(kn):
                        last = dve.tensor_scalar(lo[:, k0 + i, :], tmp[:, i, :], s.shift[:, k0 + i:k0 + i + 1], None, ALU.add)
                    last.then_inc(m.aux_done[k.bank], 1)
                elif kind == "gla_z":
                    dve.wait_ge(m.aux_ready, k.n + 1)
                    z, e = m.log_decay, m.th[:, 0, :].rearrange("p (t n) -> p t n", t=TILES)
                    dve.tensor_tensor(z, m.aux[:, k.bank, :].rearrange("p (t n) -> p t n", t=TILES),
                                      m.b_gate.unsqueeze(1).to_broadcast([P, TILES, 256]), ALU.add).then_inc(m.aux_done[k.bank], 1)
                    dve.wait_ge(*aux_is_done(m, plan, s.name))
                    dve.scalar_tensor_tensor(e, z, -1.0, z, ALU.mult, ALU.min).then_inc(m.gla_log, 1)
                    dve.wait_ge(m.gla_log, 2)
                    dve.tensor_scalar(e, e, 1.0, None, ALU.add).then_inc(m.gla_log, 1)
                    st.did(dve.tensor_scalar(z, z, 0.0, 1.0 / GLA_TAU, ALU.min, ALU.mult))
                    dve.wait_ge(m.gla_log, 4)
                    st.settle()
                    dve.scalar_tensor_tensor(z, e, -1.0 / GLA_TAU, z, ALU.mult, ALU.add).then_inc(m.gla_log, 1)
                elif kind == "gla_mul":
                    for i in range(3):
                        dve.wait_ge(*aux_is_done(m, plan, f"gla_sum{i}"))
                    dve.wait_ge(*unit_is_done(m, plan, "w_gq"))
                    for x, c in ((m.qa, "gq"), (m.ka, "gk"), (m.qb, "gq"), (m.kb, "gk")):
                        last = dve.tensor_tensor(x, x, m.proj_2[:, :, COL_2[c]:COL_2[c] + 256], ALU.mult)
                    last.then_inc(m.gla_scaled, 1)
                elif kind == "state":
                    dve.wait_ge(m.aux_ready, k.n + 1)
                    if s.n == 0:
                        dve.wait_ge(*aux_is_done(m, plan, "gla_decay"))
                    else:
                        dve.wait_ge(*aux_is_done(m, plan, f"state{s.n - 1}"))
                    st.settle()
                    for r in range(2):
                        new = m.aux[rows(r), k.bank, :].rearrange("p (b n) -> p b n", b=2)[:, :, r * P:(r + 1) * P]
                        if s.n == 0:
                            last = dve.tensor_copy(m.state[rows(r), 0, :, :], new)
                        else:
                            for p in range(2):
                                d = 2 * (2 * (s.n // 2) + p) + s.n % 2
                                last = dve.scalar_tensor_tensor(m.state[rows(r), s.n, p, :], m.state[rows(r), s.n - 1, p, :],
                                                                m.decay[rows(r), d:d + 1], new[:, p, :], ALU.mult, ALU.add)
                    last.then_inc(m.aux_done[k.bank], 1)
                elif kind == "gla_o":
                    dve.wait_ge(m.aux_ready, k.n + 1)
                    o = m.mixed[:, s.t, 0:512].rearrange("p (b r d) -> p b r d", b=2, r=2)[:, :, s.r, :]
                    dve.tensor_copy(o, m.aux[:, k.bank, 0:256].rearrange("p (b d) -> p b d", b=2)).then_inc(m.aux_done[k.bank], 1)
                elif kind == "gla_gate":
                    u = plan.unit["w_gr"].pair
                    dve.wait_ge(m.gate_tanh, 1)
                    dve.scalar_tensor_tensor(m.th[:, :, :], m.th[:, :, :], 1.0, m.pairs[u], ALU.add, ALU.mult).then_inc(m.dense_done[u], 1)
                    dve.wait_ge(*unit_is_done(m, plan, "w_gr"))
                    dve.wait_ge(m.small_in4, 16)
                    st.did(dve.scalar_tensor_tensor(m.th[:, :, :], m.th[:, :, :], 0.5, m.g_out.unsqueeze(1).to_broadcast([P, TILES, 512]),
                                                    ALU.mult, ALU.mult))
                elif kind == "gla_norm":
                    for t in range(TILES):
                        for r in range(2):
                            dve.wait_ge(*aux_is_done(m, plan, f"gla_o{t}{r}"))
                    o = m.mixed[:, :, 0:512].rearrange("p t (h d) -> p t h d", d=128)
                    sq = m.proj_2[:, :, 0:512].rearrange("p t (h d) -> p t h d", d=128)
                    st.did(dve.tensor_tensor(sq, o, o, ALU.mult))
                    st.settle()
                    st.did(dve.tensor_reduce(m.ms[:, 8:16].rearrange("p (t h) -> p t h", t=TILES), sq, AX_X, ALU.add))
                    rsqrt(dve, st, m.rs[:, 8:16], m.ms[:, 8:16], m.nt[:, 8:16], 1.0 / 128, 1e-6)
                    st.settle()
                    r = m.rs[:, 8:16].rearrange("p (t h) -> p t h", t=TILES)
                    st.did(dve.tensor_tensor(o, o, r.unsqueeze(3).to_broadcast([P, TILES, 4, 128]), ALU.mult))
                    st.settle()
                    o = m.mixed[:, :, 0:512]
                    dve.tensor_tensor(o, m.th[:, :, :], o, ALU.mult).then_inc(m.gla_normed, 1)
                elif kind == "score":
                    maxima(m, dve, plan, att, s)
                elif kind == "value":
                    inv = inverse_sums(m, dve, st, plan, att, s)
                    dve.wait_ge(m.aux_ready, k.n + 1)
                    dve.tensor_tensor(m.mixed[:, s.t, 512:1024].rearrange("p (h d) -> p h d", d=64),
                                      m.aux[:, k.bank, :].rearrange("p (h d) -> p h d", d=64),
                                      inv.unsqueeze(2).to_broadcast([P, 8, 64]), ALU.mult).then_inc(m.aux_done[k.bank], 1)
                elif kind == "evac" and s.closes and s.name[:2] in ("y1", "do"):
                    c = 512 * int(s.name[-1])
                    gate = (m.gate_a if s.name[0] == "y" else m.gate_m)[:, c:c + 512]
                    dve.wait_ge(m.slab_used, plan.last_slab[s.name] + 1)
                    dve.wait_ge(m.gates_in, 32)
                    dve.wait_ge(m.x_ready, TILES)
                    st.settle()
                    dve.tensor_tensor(m.th[:, :, :], m.pairs[s.pair], gate.unsqueeze(1).to_broadcast([P, TILES, 512]), ALU.mult)\
                       .then_inc(m.dense_done[s.pair], 1)
                    dve.wait_ge(*unit_is_done(m, plan, s.name))
                    st.settle()
                    dve.tensor_tensor(m.h[:, :, c:c + 512], m.h[:, :, c:c + 512], m.th[:, :, :], ALU.add).then_inc(m.h_ready, 1)
                    dve.wait_ge(m.h_ready, (2 if s.name[0] == "d" else 0) + int(s.name[-1]) + 1)
                elif kind == "evac" and s.name[:2] == "up":
                    j = int(s.name[2])
                    dve.wait_ge(m.dense_done[2], s.turn + 1)
                    dve.tensor_tensor(m.hid, m.hid, m.hid, ALU.mult).then_inc(m.gated, 1)
                    dve.wait_ge(m.hidden, 2 * j + 1)
                    hi, lo = m.lhs[f"hid{j % 2}"]
                    dve.tensor_tensor(lo, m.hid, hi.bitcast(F32), ALU.subtract).then_inc(m.hidden, 1)
            norm_stats(m, dve, st, 6, (m.squared, 4))
            dve.wait_ge(m.sgu_in, 16)
            for t in range(TILES):
                dve.scalar_tensor_tensor(m.mixed[:, t, :], m.h[:, t, :], m.rs[:, 6 + t:7 + t], m.row_pt, ALU.mult, ALU.mult)\
                   .then_inc(m.out_ready, 1)


def allocate(nc, ctx, depth):
    def sb(name, shape, dt=F32):
        return ctx.enter_context(nc.sbuf_tensor("b_" + name, shape, dt))

    def sem(name):
        return ctx.enter_context(nc.semaphore(name))

    m = Record()
    m.depth = depth
    m.raw = sb("raw", [P, RAW_SLOTS, SLAB])
    m.wh = sb("wh", [P, SPLIT_SLOTS, SLAB], F32R)
    m.wl = sb("wl", [P, SPLIT_SLOTS, SLAB], F32R)
    xh, xl = sb("xh", [P, 8, TOK], F32R), sb("xl", [P, 8, TOK], F32R)
    mh, ml = sb("mh", [P, 8, TOK], F32R), sb("ml", [P, 8, TOK], F32R)
    gh, gl = sb("gh", [P, 4, TOK], F32R), sb("gl", [P, 4, TOK], F32R)
    m.lhs = {"x": (xh, xl), "mx": (xh, xl), "m": (xh, xl), "my": (xh[:, 4:8, :], xl[:, 4:8, :]), "mem": (mh, ml),
             "hid0": (mh[:, 0:4, :], ml[:, 0:4, :]),
             "hid1": (mh[:, 4:8, :], ml[:, 4:8, :]), "og": (gh, gl), "qn": (gh[:, 0:3, :], gl[:, 0:3, :]),
             "kvn": (gh[:, 0:2, :], gl[:, 0:2, :])}
    m.ada_w, m.ada_acc = sb("ada_w", [P, 512]), sb("ada_acc", [P, 512])
    m.h = sb("h", [P, TILES, 1024])
    m.proj = sb("proj", [P, TILES, PROJ])
    kv = sb("kv", [P, 2560])
    m.memk = kv[:, 0:1024].rearrange("p (t n) -> p t n", t=TILES)
    m.memv = kv[:, 1024:2048].rearrange("p (t n) -> p t n", t=TILES)
    m.kfull = kv[:, 0:1536].rearrange("p (t n) -> p t n", t=TILES)
    m.vb = kv[:, 1536:2560].rearrange("p (t n) -> p t n", t=TILES)
    m.qk_a = sb("qk_a", [P, 8, TOK])
    m.qk_b = sb("qk_b", [P, 16, TOK])
    pt = sb("pt", [P, 8 * 2 * P])
    m.pt = pt[:, :].rearrange("p (h c n) -> p h c n", h=8, c=2)
    m.sgu_raw = pt[:, 0:1024].rearrange("p (g j) -> p g j", g=8)
    m.pexp = sb("pexp", [P, PEXP, BANK])
    m.th = sb("th", [P, TILES, 512])
    m.sgu_g, m.sgu_be = m.th[:, 0, :], m.th[:, 1, :]
    m.sg = sb("sg", [P, TILES, 512])
    m.sgu_t = m.sg[:, :, :].rearrange("p t n -> p (t n)").rearrange("p (g i) -> p g i", i=P)
    m.mixed = sb("mixed", [P, TILES, 1024])
    m.diff_o = m.qk_b[:, 8:16, :].rearrange("p k n -> p (k n)").rearrange("p (t g h d) -> p t g h d", t=TILES, g=2, h=4)
    m.index_score = m.proj[:, :, COL["dk"]:COL["dk"] + 256]
    m.index_work = m.proj[:, :, COL["dk"] + 256:COL["dk"] + 512]
    m.unchosen = sb("unchosen", [P, TILES, TOK], BF16)
    m.ident = sb("ident", [P, P])
    m.neg_ident = sb("neg_ident", [P, P], BF16)
    m.later = sb("later", [P, TOK], BF16)
    m.later_neg = sb("later_neg", [P, P])
    m.upto = sb("upto", [P, P])
    m.kk = sb("kk", [P, TILES, 2 * P])
    m.rot = m.proj[:, :, COL["sv"] + 256:COL["sv"] + 512]
    m.diff_g = sb("diff_g", [P, P])
    m.lam_in = sb("lam_in", [P, 256])
    small = sb("small", [P, 441])
    at = [0]

    def cut(n, *dims):
        c = small[:, at[0]:at[0] + n]
        at[0] += n
        if dims:
            names = "abc"[:len(dims)]
            kw = dict(zip(names, dims))
            return c.rearrange(f"p ({' '.join(names)}) -> p {' '.join(names)}", **kw)
        return c
    m.gain, m.qgain, m.kvgain = cut(8), cut(3), cut(2)
    m.stats = cut(36, TILES, 3, 6)
    m.ms, m.rs, m.nt = cut(16), cut(16), cut(16)
    m.sgu_bias, m.wi, m.best = cut(8), cut(8, TILES, 4), cut(8)
    m.sums = {b: cut(16, TILES, 8) for b in "abce"}
    m.sums["m"] = m.sums["a"]
    m.inv = cut(16, TILES, 8)
    m.neg_max = cut(4 * 22)
    m.lam, m.lam_init, m.one_less_lam = cut(8), cut(depth), cut(depth)
    m.pos = cut(2)
    m.cos_p, m.sin_p, m.cos_m, m.sin_m = cut(32, TILES, 16), cut(32, TILES, 16), cut(64, TILES, 32)[:, :, :], None
    small2 = sb("small2", [P, 68])
    m.mem_rs = small2[:, 66:68]
    m.ada_parts = ADA_PARTS // depth
    m.ada = sb("ada", [P, depth, 4 * m.ada_parts])
    m.c_silu, m.ones_col = cut(8), cut(1)
    m.ada_bias = m.pexp[:, 0, 0:48]
    cols = m.ada[:, :, :].rearrange("p l n -> p (l n)")
    m.shift_a, m.scale_a, m.shift_m, m.scale_m = (cols[:, 8 * i:8 * i + 8] for i in (0, 1, 3, 4))
    m.ada_cols = cols
    m.sin_m = small2[:, 0:64].rearrange("p (t n) -> p t n", t=TILES)
    n = 24
    flat = m.th[:, :, :].rearrange("p t n -> p (t n)")
    m.freq = flat[:, 0:n]
    m.angle, m.turns, m.sin_in, m.cos_in, m.product = (flat[:, n + i * 2 * n:n + (i + 1) * 2 * n]
                                                       .rearrange("p (t n) -> p t n", t=TILES) for i in range(5))
    m.pos_i = small2[:, 64:66].bitcast(I32)
    m.dense = ctx.enter_context(nc.psum_tensor("dense", [P, 4, BANK], F32))
    m.aux = ctx.enter_context(nc.psum_tensor("aux", [P, AUX, BANK], F32))
    m.pairs = [m.dense[:, 0:2, :], m.dense[:, 2:4, :], m.aux[:, 0:2, :]]
    flat = m.proj[:, :, :].rearrange("p t n -> p (t n)")
    m.buckets, m.rel_bias = flat[0:REL_BUCKETS + 1, 6144:6144 + REL], flat[0:REL_BUCKETS + 1, 6528:6536]
    m.square_scratch = flat[:, 0:2048].rearrange("p (t n) -> p t n", t=TILES)
    m.bias_out, m.c_col, m.c_tanh = flat[0:MOBA_HEADS, 6536:6536 + REL], flat[:, 6920:6928], flat[:, 6928:6936]
    m.proj_2 = flat[:, 0:TILES * PROJ_2].rearrange("p (t n) -> p t n", t=TILES)
    m.bias = flat[:, 6176:8224].rearrange("p (h n) -> p h n", h=MOBA_HEADS)
    m.gate_m = flat[:, 8224:9248]
    m.g_mix, m.g_mlp, m.decay = (flat[:, 9248 + 8 * i:9256 + 8 * i] for i in range(3))
    m.chunk_ones, m.ada_t = flat[:, 9272:9274], flat[0:48, 9280:9408]
    m.log_decay, m.qa, m.ka, m.kb, m.qb = (kv[:, 512 * i:512 * i + 512].rearrange("p (t n) -> p t n", t=TILES) for i in range(5))
    m.qa_t, m.ka_t, m.qb_t = m.qk_a[:, 0:2, :], m.qk_a[:, 2:4, :], m.qk_a[:, 4:6, :]
    m.backward, m.gg_t = m.qk_a[:, 6, 0:P], m.qk_a[0:GATE_RANK, 7, :]
    m.inner = m.qk_b[:, 8:12, :].rearrange("p k n -> p (k n)").rearrange("p (r b n) -> p r b n", r=2, b=4)
    m.state = m.qk_b[:, 12:15, :].rearrange("p k (b n) -> p k b n", b=2)
    m.w_gate = m.qk_b[0:GATE_RANK, 15, :]
    m.row_pt = pt[:, 0:1024]
    m.gate_a = m.sg[:, :, :].rearrange("p t n -> p (t n)")
    m.shift_tmp = m.th[:, :, :].rearrange("p j (k n) -> p j k n", k=2)
    m.hid = m.th[:, :, :].rearrange("p t (k n) -> p (t k) n", n=TOK)
    m.g_out, m.b_gate = m.kk[:, :, :].rearrange("p t n -> p (t n)"), m.lam_in[:, :]
    m.from_start, m.to_end, m.from_middle = m.upto[:, :], m.later_neg[:, :], m.diff_g[:, :]
    m.ada_row = nc.dram_tensor("ada_row", [6144], F32, kind="Internal").ap()
    m.bias_rows = nc.dram_tensor("bias_rows", [MOBA_HEADS, REL], F32, kind="Internal").ap()
    m.consts = sem("consts")
    m.arrived = [sem(f"arrived{i}") for i in range(RAW_SLOTS)]
    m.dense_done = [sem(f"dense_done{i}") for i in range(3)]
    m.aux_done = [sem(f"aux_done{i}") for i in range(AUX)]
    m.freqs, m.diffed, m.sgu_out, m.hi_ready = (sem(n) for n in ("freqs", "diffed", "sgu_out", "hi_ready"))
    m.lo_ready, m.slab_used = (sem(n) for n in ("lo_ready", "slab_used"))
    m.aux_ready, m.turned_hi, m.normed, m.small_in = (sem(n) for n in ("aux_ready", "turned_hi", "normed", "small_in"))
    m.small_in2, m.small_in3 = (sem(n) for n in ("small_in2", "small_in3"))
    m.small_in4, m.mem_in, m.sgu_in, m.sgu_normed = (sem(n) for n in ("small_in4", "mem_in", "sgu_in", "sgu_normed"))
    m.low_rank, m.roped = (sem(n) for n in ("low_rank", "roped"))
    m.chosen, m.max_ready, m.lam_ready, m.gate_tanh = (sem(n) for n in ("chosen", "max_ready", "lam_ready", "gate_tanh"))
    m.gated, m.mixed_up = (sem(n) for n in ("gated", "mixed_up"))
    m.dve_step, m.pool_step, m.gla_log = (sem(n) for n in ("dve_step", "pool_step", "gla_log"))
    m.gla_scaled, m.gla_normed = (sem(n) for n in ("gla_scaled", "gla_normed"))
    m.tables, m.masked, m.scaled, m.shifted_hi = (sem(n) for n in ("tables", "masked", "scaled", "shifted_hi"))
    m.bias_in, m.bias_rows_ready = (sem(n) for n in ("bias_in", "bias_rows_ready"))
    m.ones_ready, m.ada_in, m.angles = (sem(n) for n in ("ones_ready", "ada_in", "angles"))
    m.squared, m.scales, m.out_ready, m.normed_act = (sem(n) for n in ("squared", "scales", "out_ready", "normed_act"))
    m.h_ready, m.pos_in, m.ahead_in, m.hidden = (sem(n) for n in ("h_ready", "pos_in", "ahead_in", "hidden"))
    m.row_in = sem("row_in")
    m.x_ready, m.gates_out, m.gates_in, m.ada_used = (sem(n) for n in ("x_ready", "gates_out", "gates_in", "ada_used"))
    m.cleared = range(m.arrived[0].num, m.ada_used.num + 1)
    return m


def network(nc, depth, ins, out):
    with ExitStack() as ctx:
        ctx.enter_context(nc.allow_non_contiguous_dma(reason="gains and biases by feature, a few KB"))
        m = allocate(nc, ctx, depth)
        m.q, m.k = {}, {}
        m.lam_inits = [0.8 - 0.6 * float(np.exp(-0.3 * l)) for l in range(depth)]
        setup_block(nc, m, *[ins[n] for n in ("x", "mem", "positions", "mem_norm_g", "c_2", "rel_bias_2", "buckets", "mem_w_kv")])
        nc.all_engine_barrier(sems_to_clear=m.cleared)
        with nc.Fori(0, depth) as l:
            layer_block(nc, m, l, [ins[n] for n in ("w_in", "mem_w_kv", "mla_w_uq", "mla_w_ukv", "w_branch", "w_out")],
                        [ins[n] for n in ("norm_g", "mla_q_norm_g", "mla_kv_norm_g", "diff_lambda", "diff_norm_g", "sgu_ln_g",
                                          "sgu_ln_b", "sgu_w", "sgu_b")], ins["w_ada_2"], ins["mem_w_next"],
                        ins["final_norm_g"])
            nc.all_engine_barrier(sems_to_clear=m.cleared)
        m.q, m.k = {"m": m.qk_b[:, 0:4, :]}, {"m": m.qk_b[:, 4:8, :]}
        second_block(nc, m, [ins[n] for n in ("w_in_2", "w_out_2", "w_ff1_2", "w_ff2_2")],
                     [ins[n] for n in ("b_ada_2", "g_mix_2", "w_gla_gate_2", "b_gla_gate_2", "g_gla_out_2", "g_mlp_2", "g_final_2")],
                     out)


_INS = ["x", "mem", "positions", "norm_g", "w_in", "mla_q_norm_g", "mla_kv_norm_g", "mla_w_uq", "mla_w_ukv", "diff_lambda",
        "diff_norm_g", "sgu_ln_g", "sgu_ln_b", "sgu_w", "sgu_b", "mem_norm_g", "mem_w_kv", "w_branch", "w_out", "final_norm_g", "c_2",
        "w_ada_2", "b_ada_2", "g_mix_2", "w_in_2", "w_gla_gate_2", "b_gla_gate_2", "g_gla_out_2", "rel_bias_2", "w_out_2", "g_mlp_2",
        "w_ff1_2", "w_ff2_2", "g_final_2"]


def kernel(**inputs):
    import concourse.bacc as bacc
    from concourse.bass_utils import run_bass_kernel_spmd

    nc = bacc.Bacc("TRN2", target_bir_lowering=False, num_devices=1)
    arrays = {n: np.ascontiguousarray(inputs[n]) for n in _INS}
    arrays["buckets"] = bucket_rows()
    arrays["mem_w_next"] = np.roll(arrays["mem_w_kv"], -1, axis=0)
    ins = {n: nc.dram_tensor(f"in_{n}_dram", a.shape, mybir.dt.from_np(a.dtype), kind="ExternalInput").ap() for n, a in arrays.items()}
    out = nc.dram_tensor("out_dram", inputs["x"].shape, F32, kind="ExternalOutput").ap()
    network(nc, inputs["norm_g"].shape[0], ins, out)
    r = run_bass_kernel_spmd(nc, [{f"in_{n}_dram": a for n, a in arrays.items()}], core_ids=[0])
    return r.results[0]["out_dram"]
```
